# Optimizing a Trainium2 kernel written in Bass

```python
import jax, jax.numpy as jnp
from jax import lax
import numpy as np

D_MODEL = 1024
BATCH = 1
SEQ = 1024
DEPTH = 2

N_EVEN = (DEPTH + 1) // 2
N_ODD = DEPTH // 2
EPS = 1e-6

GLA_HEADS = 4
GLA_DK = 64
GLA_DV = 128
GLA_RANK = 16
GLA_TAU = 16.0
GLA_CHUNK = 64
GLA_QK = GLA_HEADS * GLA_DK
GLA_V = GLA_HEADS * GLA_DV

SWA_HEADS = 8
SWA_KV_HEADS = 2
SWA_HEAD_DIM = 64
SWA_GROUP = SWA_HEADS // SWA_KV_HEADS
WINDOW = 128
SWA_BLOCK = 128
SWA_Q = SWA_HEADS * SWA_HEAD_DIM
SWA_KV = SWA_KV_HEADS * SWA_HEAD_DIM

N_BUCKETS = 32
MAX_DISTANCE = 128

IN_SPLITS = (GLA_QK, GLA_QK, GLA_V, GLA_V, GLA_RANK, SWA_Q, SWA_KV, SWA_KV)
IN_COLS = GLA_QK + GLA_QK + GLA_V + GLA_V + GLA_RANK + SWA_Q + SWA_KV + SWA_KV
MIX_OUT = GLA_V + SWA_Q

POOL_WINDOWS = (2, 4, 8, 16)
POOL_GROUP = D_MODEL // 4

D_FF = 4 * D_MODEL


def rms_norm(x, w):
    xf = x.astype(jnp.float32)
    y = xf * lax.rsqrt(jnp.mean(xf * xf, axis=-1, keepdims=True) + EPS)
    return (y * w.astype(jnp.float32)).astype(x.dtype)

def ada_modulation(c, w, b):
    mod = jax.nn.silu(c) @ w + b
    shift, scale, gate = jnp.split(mod, 3, axis=-1)
    return shift[:, None], scale[:, None], gate[:, None]

def t5_bucket(dist):
    max_exact = N_BUCKETS // 2
    d = np.maximum(dist, 1).astype(np.float64)
    large = max_exact + (np.log(d / max_exact) / np.log(MAX_DISTANCE / max_exact)
                         * (N_BUCKETS - max_exact)).astype(np.int32)
    large = np.minimum(large, N_BUCKETS - 1)
    return np.where(dist < max_exact, dist, large).astype(np.int32)

def gla_chunked(q, k, v, log_a):
    B, S, H, dk = q.shape
    dv = v.shape[-1]
    C = GLA_CHUNK
    nc = S // C
    f32 = jnp.float32
    qf = (q.astype(f32) * dk ** -0.5).reshape(B, nc, C, H, dk)
    kf = k.astype(f32).reshape(B, nc, C, H, dk)
    vf = v.astype(f32).reshape(B, nc, C, H, dv)
    b = jnp.cumsum(log_a.reshape(B, nc, C, H, dk), axis=2)
    b_last = b[:, :, -1]
    q_t = qf * jnp.exp(b)
    k_t = kf * jnp.exp(-b)
    k_end = kf * jnp.exp(b_last[:, :, None] - b)
    causal = jnp.tril(jnp.ones((C, C), dtype=bool))
    a = jnp.einsum('bnihd,bnjhd->bnhij', q_t, k_t)
    a = jnp.where(causal, a, 0.0)
    o_intra = jnp.einsum('bnhij,bnjhe->bnihe', a, vf)
    d_state = jnp.einsum('bnjhd,bnjhe->bnhde', k_end, vf)
    decay = jnp.exp(b_last)

    def step(s_prev, inp):
        ds, dec = inp
        return dec[..., None] * s_prev + ds, s_prev

    _, s_in = lax.scan(step, jnp.zeros((B, H, dk, dv), f32),
                       (jnp.moveaxis(d_state, 1, 0), jnp.moveaxis(decay, 1, 0)))
    s_in = jnp.moveaxis(s_in, 0, 1)
    o_inter = jnp.einsum('bnihd,bnhde->bnihe', q_t, s_in)
    return (o_intra + o_inter).reshape(B, S, H, dv)

def sliding_window_attention(q, k, v, rel_bias, sinks):
    B, S = q.shape[0], q.shape[1]
    nb = S // SWA_BLOCK
    L = SWA_BLOCK
    f32 = jnp.float32
    qb = q.reshape(B, nb, L, SWA_KV_HEADS, SWA_GROUP, SWA_HEAD_DIM)

    def band(t):
        tb = t.reshape(B, nb, L, SWA_KV_HEADS, SWA_HEAD_DIM)
        prev = jnp.pad(tb, ((0, 0), (1, 0), (0, 0), (0, 0), (0, 0)))[:, :-1]
        return jnp.concatenate([prev, tb], axis=2)

    kb, vb = band(k), band(v)
    s = jnp.einsum('bnqhgd,bnkhd->bnhgqk', qb, kb,
                   preferred_element_type=f32) * (SWA_HEAD_DIM ** -0.5)
    qi = np.arange(L)[:, None] + L
    kj = np.arange(2 * L)[None, :]
    dist = qi - kj
    valid = (dist >= 0) & (dist < WINDOW)
    bucket = t5_bucket(np.maximum(dist, 0))
    bias = jnp.transpose(rel_bias[jnp.asarray(bucket)].astype(f32), (2, 0, 1))
    s = s + bias.reshape(SWA_KV_HEADS, SWA_GROUP, L, 2 * L)
    blk_ok = (np.arange(nb)[:, None, None] > 0) | (np.arange(2 * L)[None, None, :] >= L)
    mask = valid[None] & blk_ok
    s = jnp.where(jnp.asarray(mask)[None, :, None, None], s, -1e30)
    sink = sinks.astype(f32).reshape(SWA_KV_HEADS, SWA_GROUP)[None, None, :, :, None, None]
    m = jnp.maximum(jnp.max(s, axis=-1, keepdims=True), sink)
    p = jnp.exp(s - m)
    p = p / (jnp.sum(p, axis=-1, keepdims=True) + jnp.exp(sink - m))
    o = jnp.einsum('bnhgqk,bnkhd->bnqhgd', p, vb.astype(f32))
    return o.reshape(B, S, SWA_Q).astype(q.dtype)

def hybrid_attention_mixer(h, w_in, gla_w_gate, gla_b_gate, gla_norm_w, sinks, rel_bias, w_out):
    B, S, _ = h.shape
    proj = h @ w_in
    offs = np.cumsum(IN_SPLITS)[:-1].tolist()
    gq, gk, gv, gg, glr, sq, sk, sv = jnp.split(proj, offs, axis=-1)
    gate_logits = (glr @ gla_w_gate + gla_b_gate).astype(jnp.float32)
    log_a = (jax.nn.log_sigmoid(gate_logits) / GLA_TAU).reshape(B, S, GLA_HEADS, GLA_DK)
    o_gla = gla_chunked(gq.reshape(B, S, GLA_HEADS, GLA_DK), gk.reshape(B, S, GLA_HEADS, GLA_DK),
                        gv.reshape(B, S, GLA_HEADS, GLA_DV), log_a).astype(h.dtype)
    o_gla = rms_norm(o_gla, gla_norm_w) * jax.nn.silu(gg.reshape(B, S, GLA_HEADS, GLA_DV))
    o_gla = o_gla.reshape(B, S, GLA_V)
    o_swa = sliding_window_attention(sq.reshape(B, S, SWA_HEADS, SWA_HEAD_DIM),
                                     sk.reshape(B, S, SWA_KV_HEADS, SWA_HEAD_DIM),
                                     sv.reshape(B, S, SWA_KV_HEADS, SWA_HEAD_DIM), rel_bias, sinks)
    return jnp.concatenate([o_gla, o_swa], axis=-1) @ w_out

def multiscale_pool_mixer(h, pool_w, pool_scale):
    B, S, _ = h.shape
    hf = h.astype(jnp.float32)
    cs = jnp.cumsum(hf, axis=1)
    t = jnp.arange(S)
    outs = []
    for gi, w in enumerate(POOL_WINDOWS):
        lo, hi = gi * POOL_GROUP, (gi + 1) * POOL_GROUP
        csg = cs[..., lo:hi]
        lag = jnp.pad(csg, ((0, 0), (w, 0), (0, 0)))[:, :S]
        cnt = jnp.minimum(t + 1, w).astype(jnp.float32)[None, :, None]
        pooled = (csg - lag) / cnt - hf[..., lo:hi]
        outs.append(pooled.astype(h.dtype) @ pool_w[gi])
    return jnp.concatenate(outs, axis=-1) * pool_scale

def squared_relu_mlp(h, w1, w2):
    return jnp.square(jax.nn.relu(h @ w1)) @ w2

def first_inputs(seed: int = 0) -> dict:
    key = jax.random.key(seed)
    ks = jax.random.split(key, 17)
    f32 = jnp.float32
    nrm = lambda k, s: jax.random.normal(k, s, f32)
    return {
        "x": nrm(ks[0], (BATCH, SEQ, D_MODEL)),
        "c": nrm(ks[1], (BATCH, D_MODEL)),
        "norm_w": 1.0 + 0.05 * nrm(ks[2], (DEPTH, 2, D_MODEL)),
        "ada_w": nrm(ks[3], (DEPTH, 2, D_MODEL, 3 * D_MODEL)) * (0.5 * D_MODEL ** -0.5),
        "ada_b": 0.01 * nrm(ks[4], (DEPTH, 2, 3 * D_MODEL)),
        "attn_w_in": nrm(ks[5], (N_EVEN, D_MODEL, IN_COLS)) * D_MODEL ** -0.5,
        "gla_w_gate": nrm(ks[6], (N_EVEN, GLA_RANK, GLA_QK)) * GLA_RANK ** -0.5,
        "gla_b_gate": 0.1 * nrm(ks[7], (N_EVEN, GLA_QK)),
        "gla_norm_w": 1.0 + 0.05 * nrm(ks[8], (N_EVEN, GLA_DV)),
        "attn_sinks": 0.5 * nrm(ks[9], (N_EVEN, SWA_HEADS)),
        "attn_w_out": nrm(ks[10], (N_EVEN, MIX_OUT, D_MODEL)) * MIX_OUT ** -0.5,
        "rel_bias": 0.5 * nrm(ks[11], (N_BUCKETS, SWA_HEADS)),
        "pool_w": nrm(ks[12], (N_ODD, 4, POOL_GROUP, POOL_GROUP)) * POOL_GROUP ** -0.5,
        "pool_scale": 1.0 + 0.1 * nrm(ks[13], (N_ODD, D_MODEL)),
        "mlp_w1": nrm(ks[14], (DEPTH, D_MODEL, D_FF)) * D_MODEL ** -0.5,
        "mlp_w2": nrm(ks[15], (DEPTH, D_FF, D_MODEL)) * D_FF ** -0.5,
        "final_norm_w": 1.0 + 0.05 * nrm(ks[16], (D_MODEL,)),
    }

def first_block(x, c, norm_w, ada_w, ada_b, attn_w_in, gla_w_gate, gla_b_gate, gla_norm_w,
              attn_sinks, attn_w_out, rel_bias, pool_w, pool_scale, mlp_w1, mlp_w2, final_norm_w):
    for layer in range(DEPTH):
        i = layer // 2
        shift, scale, gate = ada_modulation(c, ada_w[layer, 0], ada_b[layer, 0])
        h = rms_norm(x, norm_w[layer, 0]) * (1.0 + scale) + shift
        if layer % 2 == 0:
            y = hybrid_attention_mixer(h, attn_w_in[i], gla_w_gate[i], gla_b_gate[i], gla_norm_w[i],
                                       attn_sinks[i], rel_bias, attn_w_out[i])
        else:
            y = multiscale_pool_mixer(h, pool_w[i], pool_scale[i])
        x = x + (gate * y).astype(x.dtype)
        shift, scale, gate = ada_modulation(c, ada_w[layer, 1], ada_b[layer, 1])
        h = rms_norm(x, norm_w[layer, 1]) * (1.0 + scale) + shift
        x = x + (gate * squared_relu_mlp(h, mlp_w1[layer], mlp_w2[layer])).astype(x.dtype)
    return rms_norm(x, final_norm_w)


DEPTH_2 = 1

SB_HEADS = 8
SB_HEAD_DIM = 64
SB_WIDTH = SB_HEADS * SB_HEAD_DIM
SB_BLOCK = 128

GDN_HEADS = 4
GDN_HEAD_DIM = 128
GDN_WIDTH = GDN_HEADS * GDN_HEAD_DIM
GDN_CHUNK = 64
CONV_K = 4


SPLIT_SIZES = (3 * SB_WIDTH, SB_WIDTH, 3 * GDN_WIDTH, GDN_WIDTH, GDN_HEADS, GDN_HEADS, D_MODEL, D_MODEL)
N_IN = 3 * SB_WIDTH + SB_WIDTH + 3 * GDN_WIDTH + GDN_WIDTH + 2 * GDN_HEADS + 2 * D_MODEL


def rms_norm_2(x, w):
    xf = x.astype(jnp.float32)
    y = xf * lax.rsqrt(jnp.mean(xf * xf, axis=-1, keepdims=True) + EPS)
    return (y * w.astype(jnp.float32)).astype(x.dtype)

def l2_normalize(x):
    return x * lax.rsqrt(jnp.sum(x * x, axis=-1, keepdims=True) + EPS)

def split_heads(t, n_heads, head_dim):
    b, s, _ = t.shape
    return t.reshape(b, s, n_heads, head_dim).transpose(0, 2, 1, 3)

def merge_heads(t):
    b, h, s, d = t.shape
    return t.transpose(0, 2, 1, 3).reshape(b, s, h * d)

def stick_breaking_attention(q, k, v):
    seq = q.shape[2]
    scale = SB_HEAD_DIM ** -0.5
    outs = []
    for blk in range(seq // SB_BLOCK):
        t0 = blk * SB_BLOCK
        t1 = t0 + SB_BLOCK
        qb = q[:, :, t0:t1].astype(jnp.float32)
        kb = k[:, :, :t1].astype(jnp.float32)
        vb = v[:, :, :t1].astype(jnp.float32)
        z = jnp.einsum('bhqd,bhkd->bhqk', qb, kb) * scale
        q_pos = t0 + jnp.arange(SB_BLOCK)[:, None]
        k_pos = jnp.arange(t1)[None, :]
        causal = k_pos < q_pos
        log_keep = jnp.where(causal, -jax.nn.softplus(z), 0.0)
        suffix = lax.cumsum(log_keep, axis=3, reverse=True) - log_keep
        log_a = jax.nn.log_sigmoid(z) + suffix
        a = jnp.where(causal, jnp.exp(log_a), 0.0)
        outs.append(jnp.einsum('bhqk,bhkd->bhqd', a, vb))
    return jnp.concatenate(outs, axis=2).astype(q.dtype)

def causal_depthwise_conv(x, w):
    channels = x.shape[-1]
    return lax.conv_general_dilated(
        x, w[:, None, :].astype(x.dtype), window_strides=(1,), padding=[(CONV_K - 1, 0)],
        dimension_numbers=('NWC', 'WIO', 'NWC'), feature_group_count=channels)

def gated_delta_rule_chunked(q, k, v, g, beta):
    b, h, seq, dk = q.shape
    dv = v.shape[-1]
    c = GDN_CHUNK
    n = seq // c
    q = q * dk ** -0.5
    q = q.reshape(b, h, n, c, dk)
    k = k.reshape(b, h, n, c, dk)
    v = v.reshape(b, h, n, c, dv)
    beta = beta.reshape(b, h, n, c)
    g = jnp.cumsum(g.reshape(b, h, n, c), axis=-1)
    idx = jnp.arange(c)
    lower_incl = idx[:, None] >= idx[None, :]
    strict = idx[:, None] > idx[None, :]
    decay = jnp.exp(jnp.where(lower_incl, g[..., :, None] - g[..., None, :], -jnp.inf))
    kk = jnp.einsum('bhnid,bhnjd->bhnij', k, k)
    m = jnp.where(strict, beta[..., :, None] * kk * decay, 0.0)
    rhs = jnp.concatenate([v * beta[..., None], k * (beta * jnp.exp(g))[..., None]], axis=-1)
    sol = lax.linalg.triangular_solve(m, rhs, left_side=True, lower=True, unit_diagonal=True)
    u = sol[..., :dv]
    w = sol[..., dv:]
    intra = jnp.where(lower_incl, jnp.einsum('bhnid,bhnjd->bhnij', q, k) * decay, 0.0)

    def step(state, inp):
        q_c, k_c, u_c, w_c, g_c, intra_c = inp
        v_new = u_c - jnp.einsum('bhcd,bhde->bhce', w_c, state)
        o = (jnp.einsum('bhcd,bhde->bhce', q_c * jnp.exp(g_c)[..., None], state)
             + jnp.einsum('bhij,bhje->bhie', intra_c, v_new))
        g_last = g_c[..., -1:]
        state = (state * jnp.exp(g_last)[..., None]
                 + jnp.einsum('bhcd,bhce->bhde', k_c * jnp.exp(g_last - g_c)[..., None], v_new))
        return state, o

    chunk_first = lambda t: jnp.moveaxis(t, 2, 0)
    xs = tuple(chunk_first(t) for t in (q, k, u, w, g, intra))
    state0 = jnp.zeros((b, h, dk, dv), jnp.float32)
    _, o = lax.scan(step, state0, xs)
    return jnp.moveaxis(o, 0, 2).reshape(b, h, seq, dv)

def hybrid_layer(x, pre_w, post_w, w_in, conv_w, a_log, dt_bias, gdn_norm_w,
                 w_branch_sb, w_branch_gdn, w_out):
    f32 = jnp.float32
    h = rms_norm_2(x, pre_w)
    proj = h @ w_in
    points = [int(p) for p in np.cumsum(SPLIT_SIZES)[:-1]]
    sb_qkv, sb_gate, gdn_qkv, gdn_gate, gdn_a, gdn_b, merge_sb, merge_gdn = jnp.split(proj, points, axis=-1)

    q_sb, k_sb, v_sb = [split_heads(t, SB_HEADS, SB_HEAD_DIM) for t in jnp.split(sb_qkv, 3, axis=-1)]
    o_sb = merge_heads(stick_breaking_attention(q_sb, k_sb, v_sb)) * jax.nn.silu(sb_gate)

    gdn_qkv = jax.nn.silu(causal_depthwise_conv(gdn_qkv, conv_w))
    q_g, k_g, v_g = [split_heads(t, GDN_HEADS, GDN_HEAD_DIM).astype(f32) for t in jnp.split(gdn_qkv, 3, axis=-1)]
    q_g = l2_normalize(q_g)
    k_g = l2_normalize(k_g)
    g = (-jnp.exp(a_log.astype(f32)) * jax.nn.softplus(gdn_a.astype(f32) + dt_bias.astype(f32))).transpose(0, 2, 1)
    beta = jax.nn.sigmoid(gdn_b.astype(f32)).transpose(0, 2, 1)
    o_g = gated_delta_rule_chunked(q_g, k_g, v_g, g, beta)
    o_g = merge_heads(rms_norm_2(o_g, gdn_norm_w)).astype(x.dtype) * jax.nn.silu(gdn_gate)

    merged = (jax.nn.sigmoid(merge_sb) * (o_sb @ w_branch_sb)
              + jax.nn.sigmoid(merge_gdn) * (o_g @ w_branch_gdn))
    y = merged @ w_out
    return x + rms_norm_2(y, post_w)

def second_inputs(seed: int = 0) -> dict:
    key = jax.random.key(seed)
    ks = jax.random.split(key, 12)
    f32 = jnp.float32

    def normal(k, shape, scale):
        return jax.random.normal(k, shape, f32) * scale

    x = normal(ks[0], (BATCH, SEQ, D_MODEL), 1.0)
    pre_norm_w = 1.0 + normal(ks[1], (DEPTH_2, D_MODEL), 0.05)
    post_norm_w = 1.0 + normal(ks[2], (DEPTH_2, D_MODEL), 0.05)
    w_in = normal(ks[3], (DEPTH_2, D_MODEL, N_IN), D_MODEL ** -0.5)
    conv_w = normal(ks[4], (DEPTH_2, CONV_K, 3 * GDN_WIDTH), CONV_K ** -0.5)
    a_log = jnp.log(jax.random.uniform(ks[5], (DEPTH_2, GDN_HEADS), f32, minval=0.5, maxval=16.0))
    dt = jnp.exp(jax.random.uniform(ks[6], (DEPTH_2, GDN_HEADS), f32,
                                    minval=math_log(0.001), maxval=math_log(0.1)))
    dt_bias = dt + jnp.log(-jnp.expm1(-dt))
    gdn_norm_w = 1.0 + normal(ks[7], (DEPTH_2, GDN_HEAD_DIM), 0.05)
    w_branch_sb = normal(ks[8], (DEPTH_2, SB_WIDTH, D_MODEL), SB_WIDTH ** -0.5)
    w_branch_gdn = normal(ks[9], (DEPTH_2, GDN_WIDTH, D_MODEL), GDN_WIDTH ** -0.5)
    w_out = normal(ks[10], (DEPTH_2, D_MODEL, D_MODEL), D_MODEL ** -0.5)
    return {"x": x, "pre_norm_w": pre_norm_w, "post_norm_w": post_norm_w, "w_in": w_in,
            "conv_w": conv_w, "a_log": a_log, "dt_bias": dt_bias, "gdn_norm_w": gdn_norm_w,
            "w_branch_sb": w_branch_sb, "w_branch_gdn": w_branch_gdn, "w_out": w_out}

def math_log(v):
    return float(np.log(v))

def second_block(x, pre_norm_w, post_norm_w, w_in, conv_w, a_log, dt_bias, gdn_norm_w,
              w_branch_sb, w_branch_gdn, w_out):
    for layer in range(DEPTH_2):
        x = hybrid_layer(x, pre_norm_w[layer], post_norm_w[layer], w_in[layer], conv_w[layer],
                         a_log[layer], dt_bias[layer], gdn_norm_w[layer],
                         w_branch_sb[layer], w_branch_gdn[layer], w_out[layer])
    return x


def setup_inputs(seed=0):
    out = dict(first_inputs(seed))
    for name, value in second_inputs(seed + 1).items():
        if name != "x":
            out[name + "_2"] = value
    return out


def reference(
    x, c, norm_w, ada_w, ada_b, attn_w_in, gla_w_gate, gla_b_gate, gla_norm_w, attn_sinks,
    attn_w_out, rel_bias, pool_w, pool_scale, mlp_w1, mlp_w2, final_norm_w, pre_norm_w_2,
    post_norm_w_2, w_in_2, conv_w_2, a_log_2, dt_bias_2, gdn_norm_w_2, w_branch_sb_2,
    w_branch_gdn_2, w_out_2,
):
    x = first_block(
        x, c, norm_w, ada_w, ada_b, attn_w_in, gla_w_gate, gla_b_gate, gla_norm_w, attn_sinks,
        attn_w_out, rel_bias, pool_w, pool_scale, mlp_w1, mlp_w2, final_norm_w,
    )
    return second_block(
        x, pre_norm_w_2, post_norm_w_2, w_in_2, conv_w_2, a_log_2, dt_bias_2, gdn_norm_w_2,
        w_branch_sb_2, w_branch_gdn_2, w_out_2,
    )


_drawn_inputs = setup_inputs


def setup_inputs(seed=0):
    import zlib

    import numpy as np

    out = dict(_drawn_inputs(seed))
    spreads = {}
    factors = {'gla_b_gate': 4.986, 'gla_norm_w': 5.034, 'attn_sinks': 8.0, 'rel_bias': 3.153}
    for name, (base, spread) in spreads.items():
        noise = np.random.default_rng([zlib.crc32(name.encode()), seed]).standard_normal(out[name].shape)
        drawn = base * np.exp(spread * noise) if base else spread * noise
        out[name] = __import__('jax').numpy.asarray(drawn.astype(out[name].dtype))
    for name, factor in factors.items():
        out[name] = (out[name] * factor).astype(out[name].dtype)
    return out
```

```python
from contextlib import ExitStack

import numpy as np

import concourse.bass as bass
from concourse import mybir

F32 = mybir.dt.float32
F32R = mybir.dt.float32r
U32 = mybir.dt.uint32
ALU = mybir.AluOpType
ACT = mybir.ActivationFunctionType
AX_X = mybir.AxisListType.X

P = 128
S = 1024
D = 1024
KT = D // P
NT = S // P
EPS = 1e-6
FF = 4 * D
HID = 512
NBLK = FF // HID
NEG = -1e30
SLOTS = 4
RAWS = 2
AHEAD = 3
CH = 1024
NADA = 3 * KT

CONST_AT = {"ident": 0, "causal": 128, "strict": 256, "rcnt": 384, "levels": 400}
CONST_W = 1168


def t5_bucket(dist):
    d = np.maximum(dist, 1).astype(np.float64)
    large = 16 + (np.log(d / 16) / np.log(128 / 16) * 16).astype(np.int32)
    return np.where(dist < 16, dist, np.minimum(large, 31)).astype(np.int32)


def constants():
    c = np.zeros((P, CONST_W), np.float32)
    j, i = np.arange(P)[:, None], np.arange(P)[None, :]
    same = (i // 64) == (j // 64)
    c[:, 0:128] = i == j
    c[:, 128:256] = same & (i >= j)
    c[:, 256:384] = same & (i > j)
    for n in range(6):
        s = 1 << n
        c[:, 400 + 128 * n:528 + 128 * n] = (i // (2 * s) == j // (2 * s)) & (j % (2 * s) < s) & (i % (2 * s) >= s)
    c[:, 384:400] = 1.0 / (1.0 + np.arange(16))
    onehot = np.zeros((32, 384), np.float32)
    m = np.arange(128, 256)
    onehot[t5_bucket(255 - m), m] = 1.0
    return c, onehot, same.astype(np.float32)


def build_program(nc, A, out):
    ctx = ExitStack()
    with ctx:
        def sem(name):
            return ctx.enter_context(nc.semaphore(name))

        def sb(name, shape, dt=F32):
            return ctx.enter_context(nc.sbuf_tensor(name, shape, dt))

        T = {}

        def region(name, kb, *plans):
            for plan in plans:
                with ExitStack() as turn:
                    size = 0
                    for n, shape, dt in plan:
                        T[n] = turn.enter_context(nc.sbuf_tensor(n, shape, dt))
                        size += 4 * int(np.prod(shape[1:]))
                    assert size <= kb * 1024, (name, size)
            sb(name, [P, kb * 256])

        raw = sb("raw", [P, RAWS, CH])
        wh = sb("wh", [P, SLOTS, CH], F32R)
        wl = sb("wl", [P, SLOTS, CH], F32R)
        region("R0", 32,
               [("xT", [P, KT, S], F32)],
               [("sq", [P, 4, S], F32), ("sk", [P, S], F32), ("sv", [P, NT, P], F32), ("bias", [P, 8, 256], F32)],
               [("ogh", [P, 4, S], F32R), ("ogl", [P, 4, S], F32R)],
               [("ah", [P, 4, S], F32R), ("al", [P, 4, S], F32R)],
               [("hp", [P, KT, S], F32)],
               [("sbq", [P, 4, S], F32), ("sbk", [P, 4, S], F32)],
               [("pad3", [P, 4 * S], F32), ("gkF", [P, 4, S], F32)],
               [("mrg", [P, KT, S], F32)],
               [("x5", [P, KT, S], F32)])
        region("H", 64,
               [("G", [P, 8, 384], F32), ("relrep", [32, 8, P], F32), ("onehot", [32, 384], F32), ("rows", [P, 2, P], F32)],
               [("hh", [P, KT, S], F32R), ("hl", [P, KT, S], F32R)],
               [("osh", [P, 4, S], F32R), ("osl", [P, 4, S], F32R), ("ssb", [P, 2, 2048], F32), ("pT", [P, 2, 1024], F32)],
               [("pad0", [P, 8 * S], F32), ("kt_", [P, 2, S], F32), ("keT", [P, NT, 256], F32), ("Eb", [P, 2, S], F32),
                ("rmask", [P, S], F32), ("asb", [P, 2, 512], F32)],
               [("g_" + n, [P, 512], F32) for n in ("dgG", "dgB", "D", "U", "X", "Y", "W1", "vb", "kb", "vn")] +
               [("g_" + n, [P, 2, 512], F32) for n in ("Us", "I", "kd", "wT", "qe")],
               [("outb", [P, NT, D], F32)],
               [("pad1", [P, 12 * S], F32), ("osq", [P, 512], F32), ("orstd", [P, 512], F32), ("ou", [P, 512], F32),
                ("ofull", [P, 512], F32)])
        region("R3a", 32,
               [("ab0", [P, 4, 1024], F32), ("acc0", [P, 1024], F32)],
               [("gq", [P, 2, S], F32), ("gk", [P, 2, S], F32), ("gv", [P, NT, 512], F32)],
               [("xb", [P, KT, S], F32)],
               [("sbv", [P, NT, 512], F32), ("onesb", [P, S], F32), ("lowm", [P, P], F32)],
               [("pad4", [P, 4 * S], F32), ("sgt", [P, 2, S], F32), ("vtmp", [P, S], F32)],
               [("gvT", [P, NT, 512], F32), ("gkT", [P, NT, 512], F32)],
               [("og2h", [P, 4, S], F32R), ("og2l", [P, 4, S], F32R)],
               [("yF", [P, KT, S], F32)])
        region("R3b", 32,
               [("xin", [P, NT, D], F32)],
               [("sqb", [P, 2, S], F32), ("tb", [P, 2, S], F32), ("rstd", [P, S], F32), ("rbuf", [P, 2, S], F32), ("sq1", [P, S], F32)],
               [("gg", [P, 4, S], F32), ("la", [P, 2, S], F32), ("cum", [P, 2, S], F32)],
               [("pad2", [P, 4 * S], F32), ("st", [P, 16, 2, P], F32)],
               [("ab1", [P, 4, 1024], F32), ("acc1", [P, 1024], F32)],
               [("sb_e", [P, 3, S], F32), ("sb_s", [P, 3, S], F32), ("sb_aT", [P, 2, S], F32)],
               [("gqF", [P, 4, S], F32), ("pad", [P, S + 4], F32), ("cv", [P, 2, S], F32)],
               [("pad5", [P, 4 * S], F32), ("g_S", [P, 4, P], F32), ("g_lvl", [P, 768], F32), ("g_dec", [P, 2, 4, 2], F32)],
               [("pad6", [P, 4 * S], F32), ("rb", [P, 2, S], F32), ("sg2", [P, 2, S], F32)],
               [("os2h", [P, 4, S], F32R), ("os2l", [P, 4, S], F32R)],
               [("mt6", [P, 2, S], F32)])
        zero = sb("zero", [P, 64])
        gsm = sb("gsm", [P, 8, 32])
        dtb = sb("dtb", [P, 8])
        T["same"] = sb("same", [P, P])
        cst = sb("cst", [P, 400])
        ones = sb("ones", [P, P])
        vt = sb("vt", [P, 220])
        mod = sb("mod", [P, 96])
        mul = sb("mul", [P, 32])
        sc = sb("sc", [P, 8])
        wgate = sb("wgate", [16, 256])
        pgate = sb("pgate", [P, 8])
        epsc = sb("epsc", [P, 1])
        sinks = sb("sinks", [P, 8])
        relb = sb("relb", [32, 8])
        stat8 = sb("stat8", [P, 2, 5, 8])
        dec = sb("dec", [P, 2, 16])
        xT, xb, rows = T["xT"], T["xb"], T["rows"]
        ident, causal, rcnt = cst[:, 0:128], cst[:, 128:256], cst[:, 384:400]

        acc = ctx.enter_context(nc.psum_tensor("acc", [P, 2, 1024], F32))
        att = ctx.enter_context(nc.psum_tensor("att", [P, 4, 512], F32))
        xres = nc.dram_tensor("xres", [P, KT * S], F32, kind="Internal")
        hres = nc.dram_tensor("hres", [2, P, KT * S], F32, kind="Internal")
        gscr = nc.dram_tensor("gscr", [8 * P * 384], F32, kind="Internal")

        raw_in = [sem(f"raw_in{n}") for n in range(RAWS)]
        w_hi, w_lo = sem("w_hi"), sem("w_lo")
        acc_done = [sem("acc_done0"), sem("acc_done1")]
        acc_free = [sem("acc_free0"), sem("acc_free1")]
        dstep, astep = sem("dstep"), sem("astep")

        class Chain:
            def __init__(self, s):
                self.s, self.n, self.extra = s, 0, 0

            def __call__(self, ins):
                self.n += 1
                ins.then_inc(self.s, 1)
                self.eng.wait_ge(self.s, self.n + self.extra)

        dlink, alink = Chain(dstep), Chain(astep)

        chunks = []
        G = [0]

        def kview(w, cols):
            return w.rearrange("(k p) c -> p k c", p=P)[:, :, cols]

        win = A["attn_w_in"][0]
        G_XT = G[0]; G[0] += 8
        C_IN = len(chunks)
        G_IN = G[0]
        for p in range(4):
            src = [(slice(0, P), slice(0, KT), slice(64 * g, 64 * g + 64), kview(win, slice(1552 + g * 256 + p * 64, 1616 + g * 256 + p * 64)))
                   for g in range(2)]
            chunks.append((src, KT, 128, G[0])); G[0] += 1
        chunks.append((kview(win, slice(2064, 2192)), KT, 128, G[0])); G[0] += 1
        chunks.append((kview(win, slice(2192, 2320)), KT, 128, G[0])); G[0] += 1
        for n in range(4):
            chunks.append((kview(win, slice(n * 128, n * 128 + 128)), KT, 128, G[0])); G[0] += 1
        for n in range(4):
            chunks.append((kview(win, slice(512 + n * 128, 640 + n * 128)), KT, 128, G[0] + 2 * (n // 2) + 1))
        G[0] += 4
        for n in range(4):
            chunks.append((kview(win, slice(1024 + n * 128, 1152 + n * 128)), KT, 128, G[0])); G[0] += 1
        chunks.append((kview(win, slice(1536, 1552)), KT, 16, G[0])); G[0] += 1
        C_OUT, G_OUT = len(chunks), G[0]
        for n in range(8):
            w = A["attn_w_out"][0][:, n * P:(n + 1) * P]
            src = [(slice(0, P), slice(0, 4), slice(0, P), w[0:512, :].rearrange("(k p) c -> p k c", p=P))]
            src += [(slice(64 * g, 64 * g + 64), slice(4, 8), slice(0, P),
                     w[512 + 256 * g:768 + 256 * g, :].rearrange("(k p) c -> p k c", p=64)) for g in range(2)]
            chunks.append((src, KT, P, G[0])); G[0] += 1

        def mlp_src(l, i, k):
            if k < 4:
                return A["mlp_w1"][l].rearrange("(k p) c -> p k c", p=P)[:, :, bass.ds(i * HID + k * P, P)]
            w2 = A["mlp_w2"][l].rearrange("(i k p) c -> i p k c", p=P, k=4)
            return w2[i, :, :, (k - 4) * 256:(k - 3) * 256] if isinstance(i, int) else \
                w2[bass.ds(i, 1), :, :, (k - 4) * 256:(k - 3) * 256].rearrange("i p k c -> (i p) k c")

        def add_mlp(l):
            cb, gb = len(chunks), G[0]
            for i in range(NBLK):
                for k in range(8):
                    chunks.append(((lambda l=l, k=k: (lambda j: mlp_src(l, j, k)))(), KT if k < 4 else 4, 128 if k < 4 else 256,
                                   gb + 12 * i + (k if k < 4 else 5 + 2 * (k - 4))))
            G[0] += 12 * NBLK
            return cb, gb

        C_M0, G_M0 = add_mlp(0)
        C_PL, G_PL = len(chunks), G[0]
        for q in range(2):
            src = A["pool_w"][0].rearrange("g (k p) c -> p (g k) c", p=P)[:, 4 * q:4 * q + 4, :]
            chunks.append((src, 4, 256, G[0] + 3)); G[0] += 4
        C_M1, G_M1 = add_mlp(1)
        win2c = lambda a, n=P: (kview(A["w_in_2"][0], slice(a, a + n)), KT, n)
        C_SB, G_SB = len(chunks), G[0]
        assert (C_SB + 1) % SLOTS != SLOTS - 1
        chunks.append((*win2c(0), G[0])); G[0] += 1
        for n in range(4):
            chunks.append((*win2c(1024 + n * P), G[0] + 2 * (n // 2) + 1))
        G[0] += 4
        for n in range(1, 8):
            chunks.append((*win2c(n * P), G[0])); G[0] += 1
        C_SG, G_SG = len(chunks), G[0]
        for n in range(4):
            chunks.append((*win2c(1536 + n * P), G[0])); G[0] += 1
        C_GD, G_GD = len(chunks), G[0]
        for n in list(range(8, 12)) + list(range(8)):
            chunks.append((*win2c(2048 + n * P), G[0])); G[0] += 1
        C_AB, G_AB = len(chunks), G[0]
        chunks.append((*win2c(4096, 8), G[0])); G[0] += 1
        C_GG, G_GG = len(chunks), G[0]
        for n in range(4):
            chunks.append((*win2c(3584 + n * P), G[0])); G[0] += 1
        C_MG, G_MG = len(chunks), G[0]
        branch = lambda name, m: (A[name][0].rearrange("(k p) c -> p k c", p=P)[:, :, m * P:(m + 2) * P], 4, 256)
        for m in range(0, 8, 2):
            for name, c0 in (("w_branch_sb_2", 4104), ("w_branch_gdn_2", 5128)):
                chunks.append((*win2c(c0 + m * P), G[0]))
                chunks.append((*branch(name, m), G[0] + 3))
                chunks.append((*win2c(c0 + m * P + P), G[0] + 2))
                G[0] += 4
        C_O2, G_O2 = len(chunks), G[0]
        for n in range(8):
            chunks.append((kview(A["w_out_2"][0], slice(n * P, n * P + P)), KT, P, G[0])); G[0] += 1
        C_END, G_END = len(chunks), G[0]

        def wait_done(eng, g, extra=0):
            eng.wait_ge(acc_done[g % 2], g // 2 + 1 + extra)

        def load_chunk(sp, c, i=None, step=0):
            if c >= C_END:
                return
            src, nk, ncol, _ = chunks[c]
            if callable(src):
                src = src(i if i is not None else (c - (C_M0 if c < C_PL else C_M1)) // 8)
            if c >= RAWS:
                sp.wait_ge(w_lo, c - RAWS + 1 + step)
            if isinstance(src, list):
                view = raw[:, c % RAWS, 0:nk * ncol].rearrange("p (k c) -> p k c", k=nk)
                for ps, ks, cs, s in src:
                    sp.dma_start(view[ps, ks, cs], s).then_inc(raw_in[c % RAWS], 16)
            else:
                sp.dma_start(raw[:, c % RAWS, 0:nk * ncol], src).then_inc(raw_in[c % RAWS], 16)

        def landed(c):
            return sum(16 * (len(chunks[k][0]) if isinstance(chunks[k][0], list) else 1) for k in range(c % RAWS, c + 1, RAWS))

        def split_hi(act, c, step=0, gstep=0):
            if c >= C_END:
                return
            n = chunks[c][1] * chunks[c][2]
            act.wait_ge(raw_in[c % RAWS], landed(c) + step * (16 // RAWS))
            if c >= SLOTS:
                wait_done(act, chunks[c - SLOTS][3], gstep)
            act.activation(wh[:, c % SLOTS, 0:n], raw[:, c % RAWS, 0:n], ACT.Copy).then_inc(w_hi, 1)

        def split_lo(pool, c, step=0):
            if c >= C_END:
                return
            n = chunks[c][1] * chunks[c][2]
            pool.wait_ge(w_hi, c + 1 + step)
            pool.tensor_tensor(wl[:, c % SLOTS, 0:n], raw[:, c % RAWS, 0:n],
                               wh[:, c % SLOTS, 0:n].bitcast(F32), ALU.subtract).then_inc(w_lo, 1)

        def acc_ready(pe, g, extra=0):
            if g >= 2:
                pe.wait_ge(acc_free[g % 2], g // 2 + extra)

        def product_f(pe, g, c, cols, kts, xs, width=P, step=0, gstep=0, on_kt=None):
            pe.wait_ge(w_lo, c + 1 + step)
            acc_ready(pe, g, gstep)
            for n, kt in enumerate(kts):
                if on_kt:
                    on_kt(n)
                xh, xl = xs(n)
                at = kt * chunks[c][2] + cols
                h, l = wh[:, c % SLOTS, at:at + width], wl[:, c % SLOTS, at:at + width]
                for half in range(2):
                    o = acc[0:width, g % 2, half * 512:half * 512 + 512]
                    s = slice(half * 512, half * 512 + 512)
                    first, last = n == 0, n == len(kts) - 1
                    pe.matmul(o, h, xh[:, s], start=first, stop=False)
                    pe.matmul(o, h, xl[:, s], start=False, stop=False)
                    mm = pe.matmul(o, l, xh[:, s], start=False, stop=last)
            mm.then_inc(acc_done[g % 2], 1)

        def product_t(pe, g, c, nch, t0, nt):
            pe.wait_ge(w_lo, c + nch)
            acc_ready(pe, g)
            N = nch * P
            for t in range(nt):
                o = acc[:, g % 2, t * N:(t + 1) * N]
                ts = slice((t0 + t) * P, (t0 + t + 1) * P)
                for kt in range(KT):
                    ks = slice(kt * P, kt * P + P)
                    s0 = c % SLOTS
                    rh, rl = wh[:, s0:s0 + nch, ks], wl[:, s0:s0 + nch, ks]
                    pe.matmul(o, hh[:, kt, ts], rh, start=kt == 0, stop=False)
                    pe.matmul(o, hh[:, kt, ts], rl, start=False, stop=False)
                    mm = pe.matmul(o, hl[:, kt, ts], rh, start=False, stop=kt == KT - 1)
            mm.then_inc(acc_done[g % 2], 1)

        hh, hl = T["hh"], T["hl"]
        sqb, tb, rstd = T["sqb"], T["tb"], T["rstd"]

        norm_sems = {x: sem("norm_" + x) for x in ("sq", "stat", "rs", "t", "hi", "out")}
        norm_at = dict.fromkeys(norm_sems, 0)

        class Norm:
            def __init__(self, mode):
                self.sq, self.stat, self.rs, self.t, self.hi, self.out = norm_sems.values()
                self.sq0, self.stat0, self.rs0, self.t0, self.hi0, self.out0 = norm_at.values()
                for x, n in (("sq", KT), ("stat", KT), ("rs", 1), ("t", 0 if mode == "inplace" else KT),
                             ("hi", 0 if mode == "inplace" else KT), ("out", 0 if mode == "plain" else KT)):
                    norm_at[x] += n

            def wait_out(self, eng, n):
                eng.wait_ge(self.out, self.out0 + n)

        N0, N_mlp0, NP_, N_mlp1, NF, N2, NY = (Norm(m) for m in ("split", "split", "plain", "split", "inplace", "split", "inplace"))

        def norm_pe(pe, N):
            for kt in range(KT):
                pe.wait_ge(N.sq, N.sq0 + kt + 1)
                for half in range(2):
                    mm = pe.matmul(att[:, half, :], ones[:, :], sqb[:, kt % 2, half * 512:half * 512 + 512],
                                   start=kt == 0, stop=kt == KT - 1)
                mm.then_inc(N.stat, 1)

        def x_complete(eng, g):
            for n in (g - 2, g - 1):
                eng.wait_ge(acc_free[n % 2], n // 2 + 1)

        def norm_act(act, N, X, a=None, b=None, dest=None):
            for kt in range(KT):
                if kt >= 2:
                    act.wait_ge(N.stat, N.stat0 + kt - 1)
                act.activation(sqb[:, kt % 2, :], X[:, kt, :], ACT.Square).then_inc(N.sq, 1)
            act.wait_ge(N.stat, N.stat0 + KT)
            alink(act.activation(rstd[:, :], att[:, 0:2, :].rearrange("p a b -> p (a b)"), ACT.Ln, scale=1.0 / D, bias=epsc[:, 0:1]))
            act.activation(rstd[:, :], rstd[:, :], ACT.Exp, scale=-0.5).then_inc(N.rs, 1)
            if a is not None:
                for kt in range(KT):
                    act.wait_ge(N.t, N.t0 + kt + 1)
                    bias = b(kt) if b else 0.0
                    act.activation((dest or hh)[:, kt, :], tb[:, kt % 2, :], ACT.Identity, bias=bias, scale=a(kt)).then_inc(N.hi, 1)

        def norm_dve(dve, N, X, a, b, mode):
            dve.wait_ge(N.rs, N.rs0 + 1)
            for kt in range(KT + 1):
                if kt < KT:
                    if mode == "inplace":
                        dve.scalar_tensor_tensor(out=X[:, kt, :], in0=X[:, kt, :], scalar=a(kt), in1=rstd[:, :],
                                                 op0=ALU.mult, op1=ALU.mult).then_inc(N.out, 1)
                        continue
                    if kt >= 2:
                        dve.wait_ge(N.hi, N.hi0 + kt - 1)
                    dve.tensor_tensor(tb[:, kt % 2, :], X[:, kt, :], rstd[:, :], ALU.mult).then_inc(N.t, 1)
                    if mode == "split":
                        dve.wait_ge(N.t, N.t0 + kt + 1)
                        if b:
                            dlink(dve.tensor_scalar(sqb[:, kt % 2, :], tb[:, kt % 2, :], a(kt), b(kt), ALU.mult, ALU.add))
                        else:
                            dlink(dve.tensor_scalar(sqb[:, kt % 2, :], tb[:, kt % 2, :], a(kt), None, ALU.mult))
                if kt >= 1 and mode == "split":
                    j = kt - 1
                    dve.wait_ge(N.hi, N.hi0 + j + 1)
                    dve.tensor_tensor(hl[:, j, :], sqb[:, j % 2, :], hh[:, j, :].bitcast(F32), ALU.subtract).then_inc(N.out, 1)

        def modcol(sub, third, m):
            c = sub * 24 + third * 8 + m
            return mod[:, c:c + 1]

        s_ada_in = [sem(f"ada_in{n}") for n in range(4)]
        s_ada_use, s_ada_sum, s_ada_mod = sem("ada_use"), sem("ada_sum"), sem("ada_mod")
        ADA_ORDER = [0, 1, 3, 2]
        ada = A["ada_w"].rearrange("a b k c -> (a b) k c")

        def ada_buf(n):
            return (T["ab0"], T["acc0"]) if n < NADA else (T["ab1"], T["acc1"])

        def ada_load(sp, n):
            sub, r = ADA_ORDER[n // NADA], n % NADA
            if n >= 4:
                sp.wait_ge(s_ada_use, n - 3)
            sp.dma_start(ada_buf(n)[0][:, n % 4, :], ada[sub, (r % 8) * P:(r % 8 + 1) * P, (r // 8) * 1024:(r // 8 + 1) * 1024])\
                .then_inc(s_ada_in[n % 4], 16)

        def ada_mult(dve, n):
            ab, ac = ada_buf(n)
            kt = n % 8
            dve.wait_ge(s_ada_in[n % 4], 16 * (n // 4 + 1))
            if kt == 0:
                dve.tensor_scalar(ac[:, :], ab[:, n % 4, :], sc[:, 0:1], None, ALU.mult).then_inc(s_ada_use, 1)
            else:
                dve.wait_ge(s_ada_use, n)
                dve.scalar_tensor_tensor(out=ac[:, :], in0=ab[:, n % 4, :], scalar=sc[:, kt:kt + 1], in1=ac[:, :],
                                         op0=ALU.mult, op1=ALU.add).then_inc(s_ada_use, 1)

        def ada_sum(pe, third):
            pe.wait_ge(s_ada_use, 8 * third + 8)
            if third:
                pe.wait_ge(s_ada_mod, third)
            for m in range(8):
                mm = pe.matmul(att[:, 3, m:m + 1], ada_buf(8 * third)[1][:, m * P:(m + 1) * P], ones[:, 0:1], start=True, stop=True)
            mm.then_inc(s_ada_sum, 1)

        def ada_mod(dve, third):
            c0 = ADA_ORDER[third // 3] * 24 + (third % 3) * 8
            dve.wait_ge(s_ada_sum, third + 1)
            dve.tensor_tensor(mod[:, c0:c0 + 8], att[:, 3, 0:8], vt[:, c0:c0 + 8], ALU.add).then_inc(s_ada_mod, 1)

        def ada_scale(dve, sub):
            dve.scalar_tensor_tensor(out=mul[:, sub * 8:sub * 8 + 8], in0=mod[:, sub * 24 + 8:sub * 24 + 16], scalar=1.0,
                                     in1=vt[:, 96 + sub * 8:104 + sub * 8], op0=ALU.add, op1=ALU.mult).then_inc(s_mul, 1)

        s_mul = sem("mul_ready")
        s_x, s_row, s_cst, s_vt, s_sc, s_set = sem("x_in"), sem("rows_in"), sem("cst_in"), sem("vt_ready"), sem("silu_c"), sem("set")
        s_vps = sem("rows_turned")
        s_rel, s_gps, s_gsb, s_bias = sem("relrep"), sem("g_ps"), sem("g_sb"), sem("bias_moved")
        s_xmv, X_OUT, X_BACK, X_OUT2, X_BACK2 = sem("x_moved"), 16, 32, 48, 64

        def start_sp(sp):
            for t in range(NT):
                sp.dma_start(T["xin"][:, t, :], A["x"][0, t * P:(t + 1) * P, :]).then_inc(s_x, 16)
            for n in range(NADA):
                ada_load(sp, n)
            for c in range(2):
                load_chunk(sp, c)
            for h in range(2):
                sp.wait_ge(acc_free[h], 4)
            sp.dma_start(xres.ap(), xT[:, :, :].rearrange("p a b -> p (a b)")).then_inc(s_xmv, 16)
            sp.wait_ge(s_gsb, 10)
            sp.dma_start(gscr.ap().rearrange("(h p m) -> p h m", h=8, p=P), T["G"][:, :, :]).then_inc(s_bias, 16)

        def rowsrc():
            v = lambda x, r: x.rearrange("(r c) -> r c", c=P) if r is None else x
            yield 0, 0, 96, A["ada_b"].rearrange("a b (r c) -> (a b r) c", c=P)
            yield 0, 96, 32, A["norm_w"].rearrange("a b (r c) -> (a b r) c", c=P)
            at = 0
            for name, n in (("c", 8), ("final_norm_w", 8), ("pool_scale", 8), ("pre_norm_w_2", 8), ("post_norm_w_2", 8),
                            ("gla_norm_w", 1), ("gdn_norm_w_2", 1), ("gla_b_gate", 2), ("conv_w_2", 48)):
                ap = A[name]
                if name == "final_norm_w":
                    src = ap.rearrange("(r c) -> r c", c=P)
                elif name == "conv_w_2":
                    src = ap.rearrange("a t (r c) -> (a t r) c", c=P)
                else:
                    src = ap.rearrange("a (r c) -> (a r) c", c=P)
                yield 1, at, n, src
                at += n
        V = {"c": 128, "final": 136, "pool": 144, "pre": 152, "post": 160, "glan": 168, "gdnn": 169, "glab": 170, "conv": 172}

        def vcol(name, n=0):
            return vt[:, V[name] + n:V[name] + n + 1]

        def start_act(act):
            act.dma_start(cst[:, :], A["const"][:, 0:400]).then_inc(s_cst, 16)
            for which, at, n, src in rowsrc():
                act.dma_start(rows[at:at + n, which, :], src).then_inc(s_row, 16)
            act.dma_start(wgate[:, :], A["gla_w_gate"][0]).then_inc(s_cst, 16)
            act.dma_start(relb[:, :], A["rel_bias"]).then_inc(s_cst, 16)
            act.dma_start(T["onehot"][:, :], A["onehot"]).then_inc(s_cst, 16)
            act.dma_start(sinks[:, :], A["attn_sinks"].broadcast_to([P, 8])).then_inc(s_cst, 16)
            act.wait_ge(s_vt, 2)
            act.activation(sc[:, :], vt[:, 128:136], ACT.Silu).then_inc(s_sc, 1)
            for ft in range(KT):
                wait_done(act, G_XT + ft)
                act.activation(xT[:, ft, :], acc[:, ft % 2, :], ACT.Copy).then_inc(acc_free[ft % 2], 1)
            for h in range(8):
                act.wait_ge(s_gps, h + 1)
                act.activation(T["G"][:, h, :], att[:, h % 2, 0:384], ACT.Copy).then_inc(s_gsb, 1)

        def start_dve(dve):
            dve.memset(ones[:, :], 1.0).then_inc(s_set, 1)
            dve.memset(epsc[:, :], EPS).then_inc(s_set, 1)
            for n, cols in ((0, 128), (1, 92)):
                dve.wait_ge(s_vps, n + 1)
                dve.tensor_copy(vt[:, 128 * n:128 * n + cols], att[:, 2 + n, 0:cols]).then_inc(s_vt, 1)
            dve.wait_ge(s_cst, 80)
            dve.tensor_copy(T["relrep"][:, :, :], relb[:, :].unsqueeze(2).broadcast_to([32, 8, P])).then_inc(s_rel, 1)
            dve.wait_ge(s_sc, 1)
            for third in range(3):
                for k in range(8):
                    ada_mult(dve, 8 * third + k)
                ada_mod(dve, third)
            dve.wait_ge(s_ada_mod, 3)
            ada_scale(dve, 0)
            dve.wait_ge(s_gsb, 8)
            dve.memset(T["G"][:, :, 0:128], NEG).then_inc(s_gsb, 1)
            dve.memset(T["G"][:, :, 256:384], NEG).then_inc(s_gsb, 1)

        def start_pe(pe):
            pe.wait_ge(s_cst, 80)
            pe.wait_ge(s_row, 16 * 11)
            pe.transpose(att[:, 2, 0:128], rows[:, 0, :], ident).then_inc(s_vps, 1)
            pe.transpose(att[:, 3, 0:92], rows[0:92, 1, :], ident[0:92, 0:92]).then_inc(s_vps, 1)
            pe.wait_ge(s_x, 16 * NT)
            for ft in range(KT):
                acc_ready(pe, G_XT + ft)
                for t in range(NT):
                    mm = pe.transpose(acc[:, ft % 2, t * P:(t + 1) * P], T["xin"][:, t, ft * P:(ft + 1) * P], ident)
                mm.then_inc(acc_done[ft % 2], 1)
            pe.wait_ge(s_rel, 1)
            for h in range(8):
                if h >= 2:
                    pe.wait_ge(s_gsb, h - 1)
                pe.matmul(att[:, h % 2, 0:384], T["relrep"][:, h, :], T["onehot"][:, :], start=True, stop=True).then_inc(s_gps, 1)
            pe.wait_ge(s_set, 1)
            pe.wait_ge(s_vt, 2)
            for third in range(3):
                ada_sum(pe, third)

        IN_TILES = 19

        def in_pe(pe):
            norm_pe(pe, N0)
            def seen(n):
                N0.wait_out(pe, n + 1)
            xs = lambda n: (hh[:, n, :], hl[:, n, :])
            g, c = G_IN, C_IN
            for n in range(10):
                if n == 5:
                    product_t(pe, g, c, 1, 0, 8)
                else:
                    product_f(pe, g, c, 0, range(KT), xs, on_kt=seen if n == 0 else None)
                g += 1; c += 1
            for n in range(2):
                for u in range(2):
                    product_t(pe, g, c, 2, 4 * u, 4)
                    g += 1
                c += 2
            for n in range(4):
                product_f(pe, g, c, 0, range(KT), xs)
                g += 1; c += 1
            product_f(pe, g, c, 0, range(KT), xs, width=16)

        def in_act(act):
            for c in range(AHEAD):
                split_hi(act, c)
            norm_act(act, N0, xT, a=lambda kt: mul[:, kt:kt + 1], b=lambda kt: modcol(0, 0, kt))
            for c in range(C_IN, C_OUT):
                split_hi(act, c + AHEAD)
                if 14 <= c < 18:
                    g = G_IN + c
                    wait_done(act, g)
                    act.activation(T["gg"][:, c - 14, :], acc[:, g % 2, :], ACT.Silu).then_inc(acc_free[g % 2], 1)

        def in_pool(pool):
            for c in range(AHEAD):
                split_lo(pool, c)
            for c in range(C_IN, C_OUT):
                split_lo(pool, c + AHEAD)

        def in_dve(dve):
            dve.wait_ge(s_mul, 1)
            norm_dve(dve, N0, xT, lambda kt: mul[:, kt:kt + 1], lambda kt: modcol(0, 0, kt), "split")
            dve.wait_ge(s_xmv, X_OUT)
            for n in range(IN_TILES):
                g = G_IN + n
                if 14 <= n < 18:
                    continue
                wait_done(dve, g)
                src = acc[:, g % 2, :]
                if n < 4:
                    dst = T["sq"][:, n, :]
                elif n == 4:
                    dst = T["sk"][:, :]
                elif n == 5:
                    dst, src = T["sv"][:, :, :], src.rearrange("p (t c) -> p t c", t=8)
                elif n < 8:
                    dst = T["gq"][:, n - 6, :]
                elif n < 10:
                    dst = T["gk"][:, n - 8, :]
                elif n < 14:
                    t0, c0 = 4 * (n % 2), 256 * ((n - 10) // 2)
                    dst, src = T["gv"][:, t0:t0 + 4, c0:c0 + 256], src.rearrange("p (t c) -> p t c", t=4)
                else:
                    dst, src = T["cum"][0:16, 0, :], acc[0:16, g % 2, :]
                dve.tensor_copy(dst, src).then_inc(acc_free[g % 2], 1)

        def in_sp(sp):
            for c in range(C_IN + 2, C_OUT + AHEAD + 2):
                load_chunk(sp, c)
                if c == 4:
                    N0.wait_out(sp, KT)
                    sp.wait_ge(s_xmv, X_OUT)
                    sp.wait_ge(s_bias, 16)
                    src = bass.AP(gscr, 127, [[383, P], [P * 384, 8], [1, 256]])
                    sp.dma_start(T["bias"][:, :, :], src).then_inc(s_bias, 16)

        s_sco, s_scb, s_mx = sem("swa_scores"), sem("swa_scaled"), sem("swa_max")
        s_es, s_pexp, s_pn = sem("swa_exp_sink"), sem("swa_exp"), sem("swa_probs")
        s_ptr, s_pts, s_o, s_oh, s_ol = sem("swa_turned"), sem("swa_turned_sb"), sem("swa_o"), sem("swa_o_hi"), sem("swa_o_lo")
        NB = S // P

        def swa_keys(n):
            return slice(0, 256) if n else slice(128, 256)

        def swa_pe(pe):
            def scores(n):
                for g in (4, 5):
                    pe.wait_ge(acc_free[(G_IN + g) % 2], (G_IN + g) // 2 + 1)
                if n:
                    pe.wait_ge(s_scb, n)
                else:
                    pe.wait_ge(s_gsb, 8)
                    pe.wait_ge(N0.rs, N0.rs0 + 1)
                ks = swa_keys(n)
                k0 = (n - 1) * P + ks.start
                for h in range(8):
                    r = slice(64 * (h // 4), 64 * (h // 4) + 64)
                    o = att[:, h // 2, (h % 2) * 256 + ks.start:(h % 2) * 256 + 256]
                    mm = pe.matmul(o, T["sq"][r, h % 4, n * P:(n + 1) * P], T["sk"][r, k0:(n + 1) * P], start=True, stop=True)
                mm.then_inc(s_sco, 1)

            def values(n):
                pe.wait_ge(s_pn, n + 1)
                halves = (0, 1) if n else (1,)
                for grp in range(2):
                    u = 2 * n + grp
                    if u >= 1:
                        pe.wait_ge(s_pts, u)
                    for hh4 in range(4):
                        for half in halves:
                            h = 4 * grp + hh4
                            mm = pe.transpose(acc[:, 0, (2 * hh4 + half) * P:(2 * hh4 + half + 1) * P],
                                              T["ssb"][:, n % 2, h * 256 + half * P:h * 256 + half * P + P], ident)
                    mm.then_inc(s_ptr, 1)
                if n:
                    pe.wait_ge(s_ol, n)
                for grp in range(2):
                    u = 2 * n + grp
                    pe.wait_ge(s_pts, u + 1)
                    r = slice(64 * grp, 64 * grp + 64)
                    for hh4 in range(4):
                        for half in halves:
                            mm = pe.matmul(acc[r, 1, hh4 * P:(hh4 + 1) * P], T["sv"][:, n - 1 + half, r],
                                           T["pT"][:, grp, (2 * hh4 + half) * P:(2 * hh4 + half + 1) * P],
                                           start=half == halves[0], stop=half == 1)
                mm.then_inc(s_o, 1)

            for n in range(NB + 1):
                if n < NB:
                    scores(n)
                if n:
                    values(n - 1)

        def swa_dve(dve):
            s8 = lambda n, k: stat8[:, n % 2, k, :]

            def scaled(n):
                ks = swa_keys(n)
                dve.wait_ge(s_sco, n + 1)
                if n == 0:
                    dve.wait_ge(s_bias, 32)
                    dve.wait_ge(s_cst, 80)
                src = att[:, :, :].rearrange("p b (h k) -> p (b h) k", h=2)[:, :, ks]
                dst = T["ssb"][:, n % 2, :].rearrange("p (h k) -> p h k", h=8)[:, :, ks]
                dve.scalar_tensor_tensor(out=dst, in0=src, scalar=0.125, in1=T["bias"][:, :, ks],
                                         op0=ALU.mult, op1=ALU.add).then_inc(s_scb, 1)
                dve.wait_ge(s_scb, n + 1)
                dlink(dve.tensor_reduce(s8(n, 0), dst, AX_X, ALU.max))
                dlink(dve.tensor_tensor(s8(n, 0), s8(n, 0), sinks[:, :], ALU.max))
                dlink(dve.tensor_tensor(s8(n, 1), sinks[:, :], s8(n, 0), ALU.subtract))
                dve.tensor_scalar(s8(n, 0), s8(n, 0), -1.0, None, ALU.mult).then_inc(s_mx, 1)

            def normal(n):
                ks = swa_keys(n)
                dve.wait_ge(s_pexp, 8 * (n + 1))
                dlink(dve.tensor_tensor(s8(n, 4), s8(n, 2), s8(n, 3), ALU.add))
                dlink(dve.reciprocal(s8(n, 4), s8(n, 4)))
                w = ks.stop - ks.start
                dst = T["ssb"][:, n % 2, :].rearrange("p (h k) -> p h k", h=8)[:, :, ks]
                dve.tensor_tensor(dst, dst, s8(n, 4).unsqueeze(2).broadcast_to([P, 8, w]), ALU.mult).then_inc(s_pn, 1)

            def out_lo(n):
                dve.wait_ge(s_oh, n + 1)
                t = slice(n * P, n * P + P)
                dve.tensor_tensor(T["osl"][:, :, t], acc[:, 1, 0:512].rearrange("p (h q) -> p h q", h=4),
                                  T["osh"][:, :, t].bitcast(F32), ALU.subtract).then_inc(s_ol, 1)

            for n in range(NB + 1):
                if n < NB:
                    scaled(n)
                if n:
                    normal(n - 1)
                if n >= 2:
                    out_lo(n - 2)
            out_lo(NB - 1)

        def swa_act(act):
            def exps(n):
                ks = swa_keys(n)
                act.wait_ge(s_mx, n + 1)
                act.activation(stat8[:, n % 2, 3, :], stat8[:, n % 2, 1, :], ACT.Exp).then_inc(s_es, 1)
                act.wait_ge(s_es, n + 1)
                for h in range(8):
                    v = T["ssb"][:, n % 2, h * 256 + ks.start:h * 256 + 256]
                    act.activation(v, v, ACT.Exp, bias=stat8[:, n % 2, 0, h:h + 1],
                                   accum_out=stat8[:, n % 2, 2, h:h + 1]).then_inc(s_pexp, 1)

            def turned(n):
                for grp in range(2):
                    u = 2 * n + grp
                    act.wait_ge(s_ptr, u + 1)
                    if n:
                        act.wait_ge(s_o, n)
                    if n:
                        act.activation(T["pT"][:, grp, :], acc[:, 0, :], ACT.Copy).then_inc(s_pts, 1)
                    else:
                        dst = T["pT"][:, grp, :].rearrange("p (h k q) -> p h k q", h=4, k=2)[:, :, 1, :]
                        src = acc[:, 0, :].rearrange("p (h k q) -> p h k q", h=4, k=2)[:, :, 1, :]
                        act.activation(dst, src, ACT.Copy).then_inc(s_pts, 1)

            def out_hi(n):
                act.wait_ge(s_o, n + 1)
                act.activation(T["osh"][:, :, n * P:(n + 1) * P], acc[:, 1, 0:512].rearrange("p (h q) -> p h q", h=4),
                               ACT.Copy).then_inc(s_oh, 1)

            for n in range(NB + 1):
                if n < NB:
                    exps(n)
                if n:
                    turned(n - 1)
                    out_hi(n - 1)

        kt_, keT, Eb, rmask, asb = (T[x] for x in ("kt_", "keT", "Eb", "rmask", "asb"))
        gq, gk, gv, gg, la, cum, st = (T[x] for x in ("gq", "gk", "gv", "gg", "la", "cum", "st"))
        osq, orstd, ou, ofull = (T[x] for x in ("osq", "orstd", "ou", "ofull"))
        s_gl, s_ab, s_mn, s_lg, s_ls, s_cum = (sem("gla_" + x) for x in ("logits", "abs", "min", "ln", "logsig", "cum"))
        s_e1, s_e2, s_d3, s_e3, s_qt, s_kt, s_ke, s_dec = (sem("gla_" + x) for x in
            ("exp_b", "exp_nb", "diff", "exp_end", "q", "k", "k_end", "decay"))
        s_ket, s_kes, s_ds, s_st = (sem("gla_" + x) for x in ("k_turned", "k_turned_sb", "dstate", "state"))
        s_ga, s_gas, s_go, s_gsq, s_gst, s_grs, s_gu, s_gf, s_gh, s_glo = (sem("gla_" + x) for x in
            ("scores", "scores_sb", "o", "sq", "stat", "rstd", "u", "full", "hi", "lo"))
        glr = T["cum"]

        def by_parity(t):
            return t[:, :].rearrange("p (n b i) -> p b n i", b=2, i=P)

        def o_banks(t):
            return att[:, 2 * (t % 2):2 * (t % 2) + 2, 0:256].rearrange("p b (n i) -> p b n i", i=P)

        def gla_pe(pe):
            for tile in range(2):
                pe.wait_ge(s_ol, NB)
                for half in range(2):
                    mm = pe.matmul(acc[:, tile, half * 512:half * 512 + 512], wgate[:, tile * P:(tile + 1) * P],
                                   glr[0:16, 0, half * 512:half * 512 + 512], start=True, stop=True)
                mm.then_inc(s_gl, 1)
            for hp in range(2):
                pe.wait_ge(s_ke, hp + 1)
                pe.wait_ge(s_mn, 2)
                for t in range(NT):
                    mm = pe.transpose(acc[:, hp, t * P:(t + 1) * P], gk[:, hp, t * P:(t + 1) * P], ident)
                mm.then_inc(s_ket, 1)
            for c in range(15):
                if c == 0:
                    pe.wait_ge(s_kes, 2)
                if c >= 4:
                    pe.wait_ge(s_st, 2 * (c - 3))
                r = slice(64 * (c % 2), 64 * (c % 2) + 64)
                for h in range(4):
                    mm = pe.matmul(att[64 * (h % 2):64 * (h % 2) + 64, c % 4, (h // 2) * P:(h // 2 + 1) * P],
                                   keT[r, c // 2, h * 64:h * 64 + 64], gv[r, c // 2, h * P:(h + 1) * P], start=True, stop=True)
                mm.then_inc(s_ds, 1)
            def scores(t):
                if t == 0:
                    pe.wait_ge(s_qt, 2)
                    pe.wait_ge(s_kt, 2)
                if t:
                    pe.wait_ge(s_gas, t)
                for h in range(4):
                    r = slice(64 * (h % 2), 64 * (h % 2) + 64)
                    mm = pe.matmul(acc[:, 0, 512 * (h % 2) + (h // 2) * P:512 * (h % 2) + (h // 2 + 1) * P], kt_[r, h // 2, t * P:(t + 1) * P],
                                   gq[r, h // 2, t * P:(t + 1) * P], start=True, stop=True)
                mm.then_inc(s_ga, 1)

            def outputs(t):
                pe.wait_ge(s_gas, t + 1)
                pe.wait_ge(s_st, 30)
                if t >= 2:
                    pe.wait_ge(s_gu, t - 1)
                for h in range(4):
                    r = slice(64 * (h % 2), 64 * (h % 2) + 64)
                    o = att[:, 2 * (t % 2) + h % 2, (h // 2) * P:(h // 2 + 1) * P]
                    mm = pe.matmul(o, gv[:, t, h * P:(h + 1) * P], asb[:, t % 2, h * P:(h + 1) * P], start=True, stop=True,
                                   skip_group_check=True)
                    for c in (2 * t, 2 * t + 1):
                        if c == 0:
                            continue
                        cs = (c % 2) * 64
                        mm = pe.matmul(o[:, cs:cs + 64], st[r, c - 1, h // 2, :],
                                       gq[r, h // 2, c * 64:c * 64 + 64], start=False, stop=True, skip_group_check=True)
                mm.then_inc(s_go, 1)

            def stats(t):
                pe.wait_ge(s_gsq, t + 1)
                if t:
                    pe.wait_ge(s_grs, 2 * t)
                pe.matmul(acc[:, 1, 0:512], ones[:, :], osq[:, :], start=True, stop=True).then_inc(s_gst, 1)

            for t in range(NT + 2):
                if t < NT:
                    scores(t)
                if 1 <= t <= NT:
                    outputs(t - 1)
                if t >= 2:
                    stats(t - 2)

        def gla_act(act):
            for tile in range(2):
                act.wait_ge(s_gl, tile + 1)
                act.activation(Eb[:, tile, :], acc[:, tile, :], ACT.Abs, bias=vcol("glab", tile)).then_inc(s_ab, 1)
            for tile in range(2):
                act.wait_ge(s_ab, tile + 1)
                alink(act.activation(Eb[:, tile, :], Eb[:, tile, :], ACT.Exp, scale=-1.0))
                act.activation(Eb[:, tile, :], Eb[:, tile, :], ACT.Ln, bias=ones[:, 0:1]).then_inc(s_lg, 1)
            for tile in range(2):
                act.wait_ge(s_cum, tile + 1)
                act.wait_ge(s_ls, tile + 1)
                act.activation(Eb[:, tile, :], cum[:, tile, :], ACT.Exp, scale=1 / 16.0).then_inc(s_e1, 1)
                act.activation(dec[:, tile, :], cum[:, tile, 63::64], ACT.Exp, scale=1 / 16.0).then_inc(s_dec, 1)
                act.wait_ge(s_qt, tile + 1)
                act.activation(Eb[:, tile, :], cum[:, tile, :], ACT.Exp, scale=-1 / 16.0).then_inc(s_e2, 1)
                act.wait_ge(s_d3, tile + 1)
                act.activation(Eb[:, tile, :], la[:, tile, :], ACT.Exp, scale=1 / 16.0).then_inc(s_e3, 1)
            for hp in range(2):
                act.wait_ge(s_ket, hp + 1)
                act.activation(keT[:, :, hp * P:(hp + 1) * P], acc[:, hp, :].rearrange("p (t c) -> p t c", t=NT), ACT.Copy).then_inc(s_kes, 1)
            for t in range(NT + 1):
                if t < NT:
                    act.wait_ge(s_go, t + 1)
                    if t:
                        act.wait_ge(s_gst, t)
                    act.activation(by_parity(osq), o_banks(t), ACT.Square).then_inc(s_gsq, 1)
                    act.wait_ge(s_gst, t + 1)
                    if t:
                        act.wait_ge(s_gu, t)
                    act.activation(orstd[:, :], acc[:, 1, 0:512], ACT.Ln, scale=1.0 / P, bias=epsc[:, 0:1]).then_inc(s_grs, 1)
                    act.wait_ge(s_grs, 2 * t + 1)
                    act.activation(orstd[:, :], orstd[:, :], ACT.Exp, scale=-0.5).then_inc(s_grs, 1)
                    act.wait_ge(s_gf, t + 1)
                    act.activation(T["ogh"][:, :, t * P:(t + 1) * P], ofull[:, :].rearrange("p (h q) -> p h q", h=4), ACT.Copy).then_inc(s_gh, 1)

        def gla_dve(dve):
            dve.memset(rmask[:, :], 1.0).then_inc(s_set, 1)
            dve.memset(asb[:, :, :], 0.0).then_inc(s_set, 1)
            dve.wait_ge(s_set, 4)
            dlink(dve.memset(rmask[:, 0::64], 0.0))
            for tile in range(2):
                dve.wait_ge(s_ab, tile + 1)
                dve.tensor_scalar(la[:, tile, :], acc[:, tile, :], vcol("glab", tile), 0.0, ALU.add, ALU.min).then_inc(s_mn, 1)
            for tile in range(2):
                dve.wait_ge(s_lg, tile + 1)
                dve.wait_ge(s_mn, 2)
                dve.tensor_tensor(la[:, tile, :], la[:, tile, :], Eb[:, tile, :], ALU.subtract).then_inc(s_ls, 1)
                dve.wait_ge(s_ls, tile + 1)
                dve.wait_ge(s_gl, 2)
                dve.tensor_tensor_scan(cum[:, tile, :], rmask[:, :], la[:, tile, :], 0.0, ALU.mult, ALU.add).then_inc(s_cum, 1)
            for tile in range(2):
                dve.wait_ge(s_e1, tile + 1)
                dve.wait_ge(s_cum, 2)
                dve.scalar_tensor_tensor(out=gq[:, tile, :], in0=gq[:, tile, :], scalar=0.125, in1=Eb[:, tile, :],
                                         op0=ALU.mult, op1=ALU.mult).then_inc(s_qt, 1)
                last = cum[:, tile, 63::64].unsqueeze(2).broadcast_to([P, 16, 64])
                dve.wait_ge(s_e2, tile + 1)
                dve.tensor_tensor(kt_[:, tile, :], gk[:, tile, :], Eb[:, tile, :], ALU.mult).then_inc(s_kt, 1)
                dve.wait_ge(s_kt, tile + 1)
                dve.tensor_tensor(la[:, tile, :].rearrange("p (c i) -> p c i", c=16), last,
                                  cum[:, tile, :].rearrange("p (c i) -> p c i", c=16), ALU.subtract).then_inc(s_d3, 1)
                dve.wait_ge(s_e3, tile + 1)
                dve.tensor_tensor(gk[:, tile, :], gk[:, tile, :], Eb[:, tile, :], ALU.mult).then_inc(s_ke, 1)
            dve.wait_ge(s_dec, 2)
            for c in range(15):
                for hp in range(2):
                    dve.wait_ge(s_ds, c + 1)
                    ds = att[:, c % 4, hp * P:(hp + 1) * P]
                    if c == 0:
                        dve.tensor_copy(st[:, 0, hp, :], ds).then_inc(s_st, 1)
                    else:
                        dve.wait_ge(s_st, 2 * c + hp - 1)
                        dve.scalar_tensor_tensor(out=st[:, c, hp, :], in0=st[:, c - 1, hp, :], scalar=dec[:, hp, c:c + 1], in1=ds,
                                                 op0=ALU.mult, op1=ALU.add).then_inc(s_st, 1)
            for t in range(NT + 1):
                if t < NT:
                    dve.wait_ge(s_ga, t + 1)
                    if t >= 2:
                        dve.wait_ge(s_go, t - 1)
                    dve.copy_predicated(by_parity(asb[:, t % 2, :]),
                                        causal.bitcast(U32).unsqueeze(1).unsqueeze(1).broadcast_to([P, 2, 2, P]),
                                        acc[:, 0, :].rearrange("p (b n i) -> p b n i", b=2, i=P)[:, :, 0:2, :]).then_inc(s_gas, 1)
                if t:
                    u = t - 1
                    dve.wait_ge(s_grs, 2 * u + 2)
                    dve.tensor_tensor(by_parity(ou), o_banks(u), by_parity(orstd), ALU.mult).then_inc(s_gu, 1)
                    dve.wait_ge(s_gu, u + 1)
                    ts = slice(u * P, u * P + P)
                    dve.scalar_tensor_tensor(out=ofull[:, :].rearrange("p (h q) -> p h q", h=4),
                                             in0=ou[:, :].rearrange("p (h q) -> p h q", h=4), scalar=vcol("glan"),
                                             in1=gg[:, :, ts], op0=ALU.mult, op1=ALU.mult).then_inc(s_gf, 1)
                    dve.wait_ge(s_gh, u + 1)
                    dve.tensor_tensor(T["ogl"][:, :, ts], ofull[:, :].rearrange("p (h q) -> p h q", h=4),
                                      T["ogh"][:, :, ts].bitcast(F32), ALU.subtract).then_inc(s_glo, 1)


        def out_sp(sp):
            sp.wait_ge(s_glo, NT)
            sp.dma_start(xb[:, :, :].rearrange("p a b -> p (a b)"), xres.ap()).then_inc(s_xmv, 16)
            for n in range(8):
                for j in range(9):
                    ada_load(sp, NADA + 9 * n + j)
                load_chunk(sp, C_OUT + n + AHEAD + 2)

        def out_pe(pe):
            pe.wait_ge(s_glo, NT)
            def xs(n):
                h, l = (T["ogh"], T["ogl"]) if n < 4 else (T["osh"], T["osl"])
                return h[:, n % 4, :], l[:, n % 4, :]
            for n in range(8):
                product_f(pe, G_OUT + n, C_OUT + n, 0, range(KT), xs)
                ada_sum(pe, 3 + n)
            ada_sum(pe, 11)

        def out_act(act):
            for c in range(C_OUT, C_OUT + 8):
                split_hi(act, c + AHEAD)

        def out_pool(pool):
            for c in range(C_OUT, C_OUT + 8):
                split_lo(pool, c + AHEAD)

        def add_to_x(dve, g, m, gate, gstep=0, extra=0):
            wait_done(dve, g, gstep)
            dve.scalar_tensor_tensor(out=xb[:, m, :], in0=acc[:, g % 2, :], scalar=gate, in1=xb[:, m, :],
                                     op0=ALU.mult, op1=ALU.add).then_inc(acc_free[g % 2], 1)

        def out_dve(dve):
            dve.wait_ge(s_xmv, X_BACK)
            for n in range(9):
                for k in range(8):
                    ada_mult(dve, NADA + 8 * n + k)
                if n < 8:
                    add_to_x(dve, G_OUT + n, n, modcol(0, 2, n))
                ada_mod(dve, 3 + n)
            dve.wait_ge(s_ada_mod, 12)
            for sub in range(1, 4):
                ada_scale(dve, sub)

        ah, al, rbuf, sq1 = T["ah"], T["al"], T["rbuf"], T["sq1"]

        s_ah, s_al = sem("hidden_hi"), sem("hidden_lo")

        def mlp_stage(l, cb, gb, sub):
            N = (N_mlp0, N_mlp1)[l]
            hid0 = l * 4 * NBLK

            def sp_(sp):
                with sp.Fori(0, NBLK - 1) as i:
                    for k in range(AHEAD + 2, AHEAD + 10):
                        load_chunk(sp, cb + k, i=i + k // 8, step=8 * i)
                for k in range(AHEAD + 2, AHEAD + 10):
                    load_chunk(sp, cb + 8 * (NBLK - 1) + k)

            def pe_(pe):
                norm_pe(pe, N)
                def turn(i, first):
                    step, gstep = 8 * i, 6 * i
                    for k in range(4):
                        product_f(pe, gb + k, cb + k, 0, range(KT), lambda n: (hh[:, n, :], hl[:, n, :]), step=step, gstep=gstep,
                                  on_kt=(lambda n: pe.wait_ge(N.out, N.out0 + n + 1)) if first and k == 0 else None)
                    for q in range(4):
                        for mm in range(2):
                            product_f(pe, gb + 4 + 2 * q + mm, cb + 4 + q, mm * P, range(4), lambda n: (ah[:, n, :], al[:, n, :]),
                                      step=step, gstep=gstep, on_kt=(lambda n: pe.wait_ge(s_al, hid0 + 4 * i + n + 1)) if q == mm == 0 else None)
                turn(0, True)
                with pe.Fori(1, NBLK) as i:
                    turn(i, False)

            def act_(act):
                act.wait_ge(s_mul, 4)
                x_complete(act, gb)
                norm_act(act, N, xb, a=lambda kt: mul[:, sub * 8 + kt:sub * 8 + kt + 1], b=lambda kt: modcol(sub, 0, kt))
                def turn(i, first, last):
                    gstep = 6 * i
                    for k in range(8):
                        if not (last and k + AHEAD >= 8 and cb + 8 * NBLK - 8 + k + AHEAD >= C_END):
                            split_hi(act, cb + k + AHEAD, step=8 * i, gstep=gstep)
                        if k < 4:
                            g = gb + k
                            if not (first and k < 2):
                                act.wait_ge(s_al, hid0 + 4 * i + k - 1)
                            wait_done(act, g, gstep)
                            act.activation(rbuf[:, k % 2, :], acc[:, g % 2, :], ACT.Relu).then_inc(acc_free[g % 2], 1)
                            act.wait_ge(acc_free[g % 2], g // 2 + 1 + gstep)
                            act.activation(ah[:, k, :], rbuf[:, k % 2, :], ACT.Square).then_inc(s_ah, 1)
                turn(0, True, False)
                with act.Fori(1, NBLK - 1) as i:
                    turn(i, False, False)
                turn(NBLK - 1, False, True)

            def pool_(pool):
                def turn(i):
                    for k in range(8):
                        split_lo(pool, cb + k + AHEAD, step=8 * i)
                with pool.Fori(0, NBLK - 1) as i:
                    turn(i)
                for k in range(8):
                    split_lo(pool, cb + 8 * (NBLK - 1) + k + AHEAD)

            def dve_(dve):
                norm_dve(dve, N, xb, lambda kt: mul[:, sub * 8 + kt:sub * 8 + kt + 1], lambda kt: modcol(sub, 0, kt), "split")
                def turn(i, n0):
                    gstep = 6 * i
                    for k in range(4):
                        g = gb + k
                        dve.wait_ge(acc_free[g % 2], g // 2 + 1 + gstep)
                        if n0 + k:
                            dve.wait_ge(s_al, hid0 + 4 * i + k)
                        dlink(dve.tensor_tensor(sq1[:, :], rbuf[:, k % 2, :], rbuf[:, k % 2, :], ALU.mult))
                        dve.wait_ge(s_ah, hid0 + 4 * i + k + 1)
                        dve.tensor_tensor(al[:, k, :], sq1[:, :], ah[:, k, :].bitcast(F32), ALU.subtract).then_inc(s_al, 1)
                    for m in range(8):
                        add_to_x(dve, gb + 4 + m, m, modcol(sub, 2, m), gstep)
                turn(0, 0)
                with dve.Fori(1, NBLK) as i:
                    dlink.extra = 4 * i - 4
                    turn(i, 1)
                dlink.extra = 0
                dlink.n += 4 * (NBLK - 2)

            return sp_, act_, pe_, dve_, pool_

        hp = T["hp"]
        s_pb = sem("pool_ready")

        def pool_sp(sp):
            for k in range(2):
                load_chunk(sp, C_PL + k + AHEAD + 2)

        def pool_pe(pe):
            norm_pe(pe, NP_)
            for q in range(2):
                for gi2 in range(2):
                    gi = 2 * q + gi2
                    for mm in range(2):
                        product_f(pe, G_PL + 2 * gi + mm, C_PL + q, mm * P, (2 * gi2, 2 * gi2 + 1),
                                  lambda n: (hh[:, 2 * gi + n, :], hl[:, 2 * gi + n, :]),
                                  on_kt=(lambda n: pe.wait_ge(s_pb, gi + 1)) if mm == 0 else None)

        def pool_act(act):
            x_complete(act, G_PL)
            norm_act(act, NP_, xb, a=lambda kt: mul[:, 16 + kt:17 + kt], b=lambda kt: modcol(2, 0, kt), dest=hp)
            for k in range(2):
                split_hi(act, C_PL + k + AHEAD)

        def pool_pool(pool):
            for k in range(2):
                split_lo(pool, C_PL + k + AHEAD)

        def pool_dve(dve):
            norm_dve(dve, NP_, xb, None, None, "plain")
            dlink(dve.tensor_tensor(pgate[:, :], mod[:, 64:72], vt[:, V["pool"]:V["pool"] + 8], ALU.mult))
            A2, B2 = sqb, tb
            dve.wait_ge(NP_.hi, NP_.hi0 + KT)
            for gi in range(4):
                w = 2 << gi
                src = hp[:, 2 * gi:2 * gi + 2, :]
                cur = src
                bufs = [A2, B2]
                for r in range(gi + 1):
                    sh = 1 << r
                    dst = bufs[r % 2]
                    dlink(dve.tensor_tensor(dst[:, :, sh:], cur[:, :, sh:], cur[:, :, 0:S - sh], ALU.add))
                    dlink(dve.tensor_copy(dst[:, :, 0:sh], cur[:, :, 0:sh]))
                    cur = dst[:, :, :]
                nxt = bufs[(gi + 1) % 2]
                dlink(dve.tensor_tensor(cur[:, :, 0:w - 1], cur[:, :, 0:w - 1],
                                        rcnt[:, 0:w - 1].unsqueeze(1).broadcast_to([P, 2, w - 1]), ALU.mult))
                dlink(dve.tensor_scalar(cur[:, :, w - 1:], cur[:, :, w - 1:], 1.0 / w, None, ALU.mult))
                dlink(dve.tensor_tensor(nxt[:, :, :], cur, src, ALU.subtract))
                dlink(dve.tensor_copy(hh[:, 2 * gi:2 * gi + 2, :], nxt[:, :, :]))
                dve.tensor_tensor(hl[:, 2 * gi:2 * gi + 2, :], nxt[:, :, :], hh[:, 2 * gi:2 * gi + 2, :].bitcast(F32),
                                  ALU.subtract).then_inc(s_pb, 1)
                dve.wait_ge(s_pb, gi + 1)
            for m in range(8):
                add_to_x(dve, G_PL + m, m, pgate[:, m:m + 1])

        win2 = A["w_in_2"][0]
        sbq, sbk, sbv = T["sbq"], T["sbk"], T["sbv"]

        def sbin_sp(sp):
            NF.wait_out(sp, KT)
            sp.dma_start(xres.ap(), xb[:, :, :].rearrange("p a b -> p (a b)")).then_inc(s_xmv, 16)
            for c in range(C_SB, C_SG):
                load_chunk(sp, c + AHEAD + 2)

        def sbin_pe(pe):
            norm_pe(pe, NF)
            norm_pe(pe, N2)
            for n in range(8):
                at = n + 4 if n else 0
                product_f(pe, G_SB + at, C_SB + at, 0, range(KT), lambda k: (hh[:, k, :], hl[:, k, :]),
                          on_kt=(lambda k: N2.wait_out(pe, k + 1)) if n == 0 else None)
                if n == 0:
                    for u in range(4):
                        product_t(pe, G_SB + 1 + u, C_SB + 1 + 2 * (u // 2), 2, 4 * (u % 2), 4)

        def sbin_act(act):
            x_complete(act, G_SB)
            norm_act(act, NF, xb)
            NF.wait_out(act, KT)
            norm_act(act, N2, xb, a=lambda kt: vcol("pre", kt))
            for c in range(C_SB, C_SG):
                split_hi(act, c + AHEAD)
                n = c - C_SB - 4 if c > C_SB else 0
                if n > 0 or c == C_SB:
                    g = G_SB + c - C_SB
                    wait_done(act, g)
                    if n == 0:
                        N2.wait_out(act, KT)
                    dst = sbq[:, n, :] if n < 4 else sbk[:, n - 4, :]
                    act.activation(dst, acc[:, g % 2, :], ACT.Copy, scale=0.125 if n < 4 else 1.0).then_inc(acc_free[g % 2], 1)

        def sbin_pool(pool):
            for c in range(C_SB, C_SG):
                split_lo(pool, c + AHEAD)

        def sbin_dve(dve):
            norm_dve(dve, NF, xb, lambda kt: vcol("final", kt), None, "inplace")
            norm_dve(dve, N2, xb, lambda kt: vcol("pre", kt), None, "split")
            dve.wait_ge(s_xmv, X_OUT2)
            for n in range(4):
                g = G_SB + 1 + n
                wait_done(dve, g)
                t0, c0 = 4 * (n % 2), 256 * (n // 2)
                dve.tensor_copy(sbv[:, t0:t0 + 4, c0:c0 + 256], acc[:, g % 2, :].rearrange("p (t c) -> p t c", t=4))\
                   .then_inc(acc_free[g % 2], 1)

        onesb, lowm, vtmp = T["onesb"], T["lowm"], T["vtmp"]
        s_low = sem("sb_mask")
        et, su, aT = T["sb_e"], T["sb_s"], T["sb_aT"]
        s_z, s_ez, s_cl, s_ln, s_sc_, s_arg, s_a, s_am = (sem("sb_" + x) for x in
            ("z", "exp", "clamp", "ln", "suffix", "arg", "a", "a_masked"))
        s_tr, s_trc, s_sbo, s_sboc = (sem("sb_" + x) for x in ("turned", "turned_sb", "o", "o_sb"))
        UNITS = [(n, h) for n in range(NT) for h in range(8)]
        NU = len(UNITS)
        BUFS = 3

        def groups(n):
            return [range(k, min(k + 4, n + 1)) for k in range(0, n + 1, 4)]

        GRP_AT = []
        _n = 0
        for n, h in UNITS:
            GRP_AT.append(_n)
            _n += len(groups(n))
        GRP_AT.append(_n)

        def zps(u, W):
            return att[:, 2 * (u % 2):2 * (u % 2) + 2, :].rearrange("p b c -> p (b c)")[:, 0:W]

        def sb_pe(pe):
            x_complete(pe, G_SG)
            def z(u):
                n, h = UNITS[u]
                W = (n + 1) * P
                if u >= 2:
                    pe.wait_ge(s_arg, u - 1)
                r = slice(64 * (h % 2), 64 * (h % 2) + 64)
                for k in range(0, W, 512):
                    w = min(512, W - k)
                    mm = pe.matmul(att[:, 2 * (u % 2) + k // 512, 0:w], sbq[r, h // 2, n * P:(n + 1) * P],
                                   sbk[r, h // 2, k:k + w], start=True, stop=True)
                mm.then_inc(s_z, 1)

            def turn(u):
                n, h = UNITS[u]
                pe.wait_ge(s_am, u + 1)
                for gi, grp in enumerate(groups(n)):
                    x = GRP_AT[u] + gi
                    if x >= 2:
                        pe.wait_ge(s_trc, x - 1)
                    for k in grp:
                        mm = pe.transpose(acc[:, 0, (x % 2) * 512 + (k % 4) * P:(x % 2) * 512 + (k % 4 + 1) * P],
                                          su[:, u % BUFS, k * P:(k + 1) * P], ident)
                    mm.then_inc(s_tr, 1)

            def out_(u):
                n, h = UNITS[u]
                r = slice(64 * (h % 2), 64 * (h % 2) + 64)
                if u >= 2:
                    pe.wait_ge(s_sboc, u - 1)
                for gi, grp in enumerate(groups(n)):
                    pe.wait_ge(s_trc, GRP_AT[u] + gi + 1)
                    for k in grp:
                        mm = pe.matmul(acc[r, 1, 512 * ((u // 2) % 2):512 * ((u // 2) % 2) + P], sbv[:, k, h * 64:h * 64 + 64], aT[:, u % 2, k * P:(k + 1) * P],
                                       start=k == 0, stop=k == n)
                mm.then_inc(s_sbo, 1)

            for u in range(NU + 4):
                if u < NU:
                    z(u)
                if 3 <= u < NU + 3:
                    turn(u - 3)
                if u >= 4:
                    out_(u - 4)

        def sb_act(act):
            act.preload_act_table_set("natural_log_exp_and_others")
            def first(u):
                W = (UNITS[u][0] + 1) * P
                act.wait_ge(s_z, u + 1)
                if u >= BUFS:
                    act.wait_ge(s_sc_, u - BUFS + 1)
                act.activation(et[:, u % BUFS, 0:W], zps(u, W), ACT.Exp).then_inc(s_ez, 1)
            def second(u):
                W = (UNITS[u][0] + 1) * P
                act.wait_ge(s_cl, u + 1)
                act.activation(et[:, u % BUFS, 0:W], et[:, u % BUFS, 0:W], ACT.Ln, bias=ones[:, 0:1]).then_inc(s_ln, 1)
            def third(u):
                W = (UNITS[u][0] + 1) * P
                act.wait_ge(s_arg, u + 1)
                act.activation(su[:, u % BUFS, 0:W], su[:, u % BUFS, 0:W], ACT.Exp).then_inc(s_a, 1)
            def copies(u):
                n, h = UNITS[u]
                for gi, grp in enumerate(groups(n)):
                    x = GRP_AT[u] + gi
                    act.wait_ge(s_tr, x + 1)
                    if u >= 2:
                        act.wait_ge(s_sbo, u - 1)
                    w = len(grp) * P
                    act.activation(aT[:, u % 2, grp[0] * P:grp[0] * P + w], acc[:, 0, (x % 2) * 512:(x % 2) * 512 + w], ACT.Copy).then_inc(s_trc, 1)
            for u in range(NU + 3):
                if u < NU:
                    first(u)
                if 1 <= u < NU + 1:
                    second(u - 1)
                if 2 <= u < NU + 2:
                    third(u - 2)
                if u >= 3:
                    copies(u - 3)

        def sb_pool(pool):
            pool.wait_ge(s_xmv, X_OUT2)
            pool.memset(lowm[:, :], 1.0).then_inc(s_low, 1)
            pool.wait_ge(s_low, 1)
            pool.affine_select(out=lowm[:, :], in_=lowm[:, :], compare_op=ALU.is_gt, fill=0.0, base=0,
                               pattern=[[-1, P]], channel_multiplier=1).then_inc(s_low, 1)
            def clamp(u):
                W = (UNITS[u][0] + 1) * P
                pool.wait_ge(s_ez, u + 1)
                pool.tensor_scalar(et[:, u % BUFS, 0:W], et[:, u % BUFS, 0:W], 2.0 ** 60, 0.0, ALU.min, ALU.max).then_inc(s_cl, 1)
            def strictly_before(u):
                pool.wait_ge(s_a, u + 1)
                d = slice(UNITS[u][0] * P, (UNITS[u][0] + 1) * P)
                pool.affine_select(out=su[:, u % BUFS, d], in_=su[:, u % BUFS, d], compare_op=ALU.is_gt, fill=0.0, base=0,
                                   pattern=[[-1, P]], channel_multiplier=1).then_inc(s_am, 1)
            for u in range(NU + 2):
                if u < NU:
                    clamp(u)
                if u >= 2:
                    strictly_before(u - 2)

        def sb_dve(dve):
            def soft(u):
                W = (UNITS[u][0] + 1) * P
                dve.wait_ge(s_ln, u + 1)
                dlink(dve.tensor_tensor(et[:, u % BUFS, 0:W], zps(u, W), et[:, u % BUFS, 0:W], ALU.max))
                dlink(dve.tensor_tensor(et[:, u % BUFS, W - P:W], et[:, u % BUFS, W - P:W], lowm[:, :], ALU.mult))
            def scan(u):
                W = (UNITS[u][0] + 1) * P
                if u >= BUFS:
                    dve.wait_ge(s_tr, GRP_AT[u - BUFS + 1])
                dve.tensor_tensor_scan(su[:, u % BUFS, 0:W][:, ::-1], onesb[:, 0:W], et[:, u % BUFS, 0:W][:, ::-1], 0.0,
                                       ALU.mult, ALU.subtract).then_inc(s_sc_, 1)
                dve.wait_ge(s_sc_, u + 1)
                dve.tensor_tensor(su[:, u % BUFS, 0:W], zps(u, W), su[:, u % BUFS, 0:W], ALU.add).then_inc(s_arg, 1)
            def keep(u):
                n, h = UNITS[u]
                r = slice(64 * (h % 2), 64 * (h % 2) + 64)
                dve.wait_ge(s_sbo, u + 1)
                dve.tensor_copy(sbq[r, h // 2, n * P:(n + 1) * P], acc[r, 1, 512 * ((u // 2) % 2):512 * ((u // 2) % 2) + P]).then_inc(s_sboc, 1)
            dlink(dve.memset(onesb[:, :], 1.0))
            dve.wait_ge(s_low, 2)
            for u in range(1, NU + 4):
                if u <= NU:
                    soft(u - 1)
                    scan(u - 1)
                if u >= 4:
                    keep(u - 4)

        gqF, gkF, gkT, gvT, pad, cv = (T[x] for x in ("gqF", "gkF", "gkT", "gvT", "pad", "cv"))
        sgt = T["sgt"]
        s_sgo = sem("sb_gated")
        s_cv, s_cvd, s_vtr = sem("conv"), sem("conv_silu"), sem("v_turned")
        s_lsq, s_lst, s_lrs, s_ln2, s_ktr, s_kcp = (sem("l2_" + x) for x in ("sq", "stat", "rstd", "out", "k_turned", "k_sb"))
        s_vcp = sem("v_sb")
        s_ab1, s_ab2, s_gx, s_gps2, s_gate, s_dtb = (sem("gates_" + x) for x in
            ("one", "two", "exp", "sums", "ready", "in"))
        s_hmv = sem("h_moved")

        def gin_sp(sp):
            for c in range(C_SG, C_GG):
                load_chunk(sp, c + AHEAD + 2)
            g = G_AB
            sp.wait_ge(acc_done[g % 2], g // 2 + 1)
            wait_done(sp, G_AB - 1)
            sp.dma_start(hres.ap()[0], hh[:, :, :].bitcast(F32).rearrange("p a b -> p (a b)")).then_inc(s_hmv, 16)
            sp.dma_start(hres.ap()[1], hl[:, :, :].bitcast(F32).rearrange("p a b -> p (a b)")).then_inc(s_hmv, 16)
            sp.wait_ge(s_hmv, 32)

        CONV_ORDER = list(range(8, 12)) + list(range(8))

        def gin_pe(pe):
            xs = lambda k: (hh[:, k, :], hl[:, k, :])
            for n in range(4):
                if n == 0:
                    pe.wait_ge(s_sboc, NU)
                product_f(pe, G_SG + n, C_SG + n, 0, range(KT), xs)
            def turn_v(n):
                pe.wait_ge(s_cvd, n + 1)
                if n:
                    pe.wait_ge(s_vcp, n)
                for t in range(NT):
                    mm = pe.transpose(att[:, t // 4, (t % 4) * P:(t % 4 + 1) * P], vtmp[:, t * P:(t + 1) * P], ident)
                mm.then_inc(s_vtr, 1)
            for n in range(12):
                product_f(pe, G_GD + n, C_GD + n, 0, range(KT), xs)
                if 1 <= n <= 4:
                    turn_v(n - 1)
            pe.wait_ge(w_lo, C_AB + 1)
            acc_ready(pe, G_AB)
            for t in range(NT):
                ts = slice(t * P, (t + 1) * P)
                o = acc[:, G_AB % 2, t * 8:t * 8 + 8]
                for kt in range(KT):
                    rh, rl = (w[:, C_AB % SLOTS, kt * 8:kt * 8 + 8] for w in (wh, wl))
                    pe.matmul(o, hh[:, kt, ts], rh, start=kt == 0, stop=False)
                    pe.matmul(o, hh[:, kt, ts], rl, start=False, stop=False)
                    mm = pe.matmul(o, hl[:, kt, ts], rh, start=False, stop=kt == KT - 1)
            mm.then_inc(acc_done[G_AB % 2], 1)
            def turn_k(x):
                pe.wait_ge(s_ln2, x + 1)
                if x > 4:
                    pe.wait_ge(s_kcp, x - 4)
                else:
                    pe.wait_ge(s_vcp, 4)
                for t in range(NT):
                    mm = pe.transpose(att[:, t // 4, (t % 4) * P:(t % 4 + 1) * P], gkF[:, x - 4, t * P:(t + 1) * P], ident)
                mm.then_inc(s_ktr, 1)
            for x in range(9):
                if x < 8:
                    pe.wait_ge(s_lsq, x + 1)
                    if x:
                        pe.wait_ge(s_lrs, 2 * x - 1)
                    for half in range(2):
                        mm = pe.matmul(att[:, 2 + half, :], ones[:, :], cv[:, x % 2, half * 512:half * 512 + 512], start=True, stop=True)
                    mm.then_inc(s_lst, 1)
                if x >= 5:
                    turn_k(x - 1)
            pe.wait_ge(s_ab2, 1)
            pe.matmul(acc[:, 0, 512:544], cst[:, 128:256], gsm[:, 0, :], start=True, stop=True)
            pe.matmul(acc[:, 0, 544:576], T["same"][:, :], gsm[:, 0, :], start=True, stop=True).then_inc(s_gps2, 1)

        def gin_act(act):
            for n in range(4):
                split_hi(act, C_SG + n + AHEAD)
                g = G_SG + n
                wait_done(act, g)
                if n >= 2:
                    act.wait_ge(s_sgo, n - 1)
                act.activation(sgt[:, n % 2, :], acc[:, g % 2, :], ACT.Silu).then_inc(acc_free[g % 2], 1)
            act.dma_start(dtb[:, 0:4], A["dt_bias_2"].broadcast_to([P, 4])).then_inc(s_dtb, 16)
            act.dma_start(dtb[:, 4:8], A["a_log_2"].broadcast_to([P, 4])).then_inc(s_dtb, 16)
            act.dma_start(T["same"][:, :], A["same"]).then_inc(s_dtb, 16)
            def silu(n):
                act.wait_ge(s_cv, n + 1)
                j = CONV_ORDER[n]
                if j >= 8:
                    if n:
                        act.wait_ge(s_vtr, n)
                    dst = vtmp[:, :]
                else:
                    dst = gqF[:, j, :] if j < 4 else gkF[:, j - 4, :]
                act.activation(dst, cv[:, n % 2, :], ACT.Silu).then_inc(s_cvd, 1)
            def copy_v(n):
                act.wait_ge(s_vtr, n + 1)
                act.activation(gvT[:, :, n * P:(n + 1) * P], att[:, 0:2, :].rearrange("p b (t c) -> p (b t) c", c=P), ACT.Copy).then_inc(s_vcp, 1)
            for n in range(13):
                if n < 12:
                    split_hi(act, C_GD + n + AHEAD)
                    g = G_GD + n
                    wait_done(act, g)
                    if n == 0:
                        act.wait_ge(s_sgo, 4)
                        act.wait_ge(s_sboc, NU)
                    if n:
                        act.wait_ge(s_cv, n)
                    act.activation(pad[:, 3:3 + S], acc[:, g % 2, :], ACT.Copy).then_inc(acc_free[g % 2], 1)
                if n:
                    silu(n - 1)
                if 2 <= n <= 5:
                    copy_v(n - 2)
            split_hi(act, C_AB + AHEAD)
            act.preload_act_table_set("natural_log_exp_and_others")
            wait_done(act, G_AB)
            act.activation(gsm[:, 2:4, :].rearrange("p a (t h) -> p t a h", h=4), acc[:, G_AB % 2, 0:64].rearrange("p (t a h) -> p t a h", a=2, h=4), ACT.Copy).then_inc(acc_free[G_AB % 2], 1)
            def sq(x):
                src = gqF[:, x, :] if x < 4 else gkF[:, x - 4, :]
                act.wait_ge(s_cvd, 12)
                if x >= 2:
                    act.wait_ge(s_ln2, x - 1)
                act.activation(cv[:, x % 2, :], src, ACT.Square).then_inc(s_lsq, 1)
            def rs(x):
                act.wait_ge(s_lst, x + 1)
                act.activation(cv[:, x % 2, :], att[:, 2:4, :].rearrange("p a b -> p (a b)"), ACT.Ln, bias=epsc[:, 0:1]).then_inc(s_lrs, 1)
                act.wait_ge(s_lrs, 2 * x + 1)
                act.activation(cv[:, x % 2, :], cv[:, x % 2, :], ACT.Exp, scale=-0.5).then_inc(s_lrs, 1)
            for x in range(9):
                if x < 8:
                    sq(x)
                if x >= 1:
                    rs(x - 1)
                if x - 2 >= 4:
                    act.wait_ge(s_ktr, x - 5)
                    act.activation(gkT[:, :, (x - 6) * P:(x - 5) * P], att[:, 0:2, :].rearrange("p b (t c) -> p (b t) c", c=P), ACT.Copy).then_inc(s_kcp, 1)
            act.wait_ge(s_ktr, 4)
            act.activation(gkT[:, :, 3 * P:4 * P], att[:, 0:2, :].rearrange("p b (t c) -> p (b t) c", c=P), ACT.Copy).then_inc(s_kcp, 1)
            act.wait_ge(s_ab1, 1)
            act.activation(gsm[:, 4, :], gsm[:, 0, :], ACT.Abs).then_inc(s_gx, 1)
            act.wait_ge(s_gx, 1)
            alink(act.activation(gsm[:, 4, :], gsm[:, 4, :], ACT.Exp, scale=-1.0))
            act.activation(gsm[:, 4, :], gsm[:, 4, :], ACT.Ln, bias=ones[:, 0:1]).then_inc(s_gx, 1)
            act.activation(gsm[:, 3, :], gsm[:, 3, :], ACT.Exp, scale=-1.0).then_inc(s_gx, 1)
            act.activation(dtb[:, 4:8], dtb[:, 4:8], ACT.Exp).then_inc(s_gx, 1)
            act.wait_ge(s_gate, 1)
            act.activation(gsm[:, 5, :], gsm[:, 1, :], ACT.Exp).then_inc(s_gx, 1)
            act.activation(gsm[:, 6, :], gsm[:, 6, :], ACT.Exp).then_inc(s_gx, 1)

        def gin_pool(pool):
            for c in range(C_SG, C_GG):
                split_lo(pool, c + AHEAD)

        def gin_dve(dve):
            for n in range(4):
                g = G_SG + n
                dve.wait_ge(acc_free[g % 2], g // 2 + 1)
                dve.wait_ge(s_sboc, NU)
                dve.tensor_tensor(sbq[:, n, :], sbq[:, n, :], sgt[:, n % 2, :], ALU.mult).then_inc(s_sgo, 1)
            dlink(dve.memset(pad[:, 0:3], 0.0))
            for n in range(12):
                j, g = CONV_ORDER[n], G_GD + n
                dve.wait_ge(acc_free[g % 2], g // 2 + 1)
                c = cv[:, n % 2, :]
                if n >= 2:
                    dve.wait_ge(s_cvd, n - 1)
                dlink(dve.tensor_scalar(c, pad[:, 0:S], vcol("conv", j), None, ALU.mult))
                for tap in range(1, 4):
                    ins = dve.scalar_tensor_tensor(out=c, in0=pad[:, tap:tap + S], scalar=vcol("conv", tap * 12 + j), in1=c, op0=ALU.mult, op1=ALU.add)
                    if tap < 3:
                        dlink(ins)
                    else:
                        ins.then_inc(s_cv, 1)
            for x in range(8):
                dve.wait_ge(s_lrs, 2 * x + 2)
                t = gqF[:, x, :] if x < 4 else gkF[:, x - 4, :]
                dve.scalar_tensor_tensor(out=t, in0=t, scalar=float(P) ** -0.5 if x < 4 else 1.0, in1=cv[:, x % 2, :],
                                         op0=ALU.mult, op1=ALU.mult).then_inc(s_ln2, 1)
            bc = lambda ap: ap.unsqueeze(1).broadcast_to([P, NT, 4])
            v3 = lambda k: gsm[:, k, :].rearrange("p (t h) -> p t h", h=4)
            dve.wait_ge(acc_free[G_AB % 2], G_AB // 2 + 1)
            dve.wait_ge(s_dtb, 48)
            dve.tensor_tensor(v3(0), v3(2), bc(dtb[:, 0:4]), ALU.add).then_inc(s_ab1, 1)
            dve.wait_ge(s_gx, 4)
            dlink(dve.scalar_tensor_tensor(out=gsm[:, 0, :], in0=gsm[:, 0, :], scalar=0.0, in1=gsm[:, 4, :], op0=ALU.max, op1=ALU.add))
            dlink(dve.tensor_tensor(v3(0), v3(0), bc(dtb[:, 4:8]), ALU.mult))
            dlink(dve.tensor_scalar(gsm[:, 3, :], gsm[:, 3, :], 1.0, None, ALU.add))
            dlink(dve.reciprocal(gsm[:, 3, :], gsm[:, 3, :]))
            dve.tensor_scalar(gsm[:, 0, :], gsm[:, 0, :], -1.0, None, ALU.mult).then_inc(s_ab2, 1)
            dve.wait_ge(s_gps2, 1)
            dlink(dve.tensor_copy(gsm[:, 1, :], acc[:, 0, 512:544]))
            dve.tensor_tensor(gsm[:, 6, :], acc[:, 0, 544:576], gsm[:, 1, :], ALU.subtract).then_inc(s_gate, 1)
            dve.wait_ge(s_gx, 6)
            dve.tensor_tensor(gsm[:, 7, :], gsm[:, 3, :], gsm[:, 5, :], ALU.mult).then_inc(s_gate, 1)

        dgG, dgB, Dm, U, Us, X, Y, W1, vb, kb, vn, In, kd, wT, qe, Sg, lvl, decg = (T["g_" + x] for x in (
            "dgG", "dgB", "D", "U", "Us", "X", "Y", "W1", "vb", "kb", "vn", "I", "kd", "wT", "qe", "S", "lvl", "dec"))
        (s_dg, s_vkk, s_pp, s_dt, s_de, s_qe, s_dm, s_I, s_U, s_us, s_y, s_xx, s_x1, s_xt, s_la, s_lb, s_w1, s_wt, s_v,
         s_wts, s_r1, s_vn, s_r2, s_S, s_r3, s_of, s_lvl) = (sem("gdn_" + x) for x in (
             "diag", "scaled", "prep", "diff", "exp", "q_decayed", "decay_masked", "intra", "u", "u_masked", "y", "x", "x1",
             "x1_turned", "lx", "xlx", "lx_sb", "w_t", "v", "w_t_sb", "from_state", "v_new", "dstate", "state", "o", "o_sb", "levels"))
        bank = lambda n: acc[:, n // 2, (n % 2) * 512:(n % 2) * 512 + 512]
        hd = lambda t, h: t[:, h * P:(h + 1) * P]
        h4 = lambda t: t.rearrange("p (h i) -> p h i", h=4)
        bc4 = lambda t: t.unsqueeze(1).broadcast_to([P, 4, P])
        col4 = lambda k, p: gsm[:, k, 4 * p:4 * p + 4].unsqueeze(2).broadcast_to([P, 4, P])

        def gdn_plan():
            for p in range(NT + 1):
                q = p - 1
                here, before = p < NT, p > 0
                if here:
                    yield "prep", p, 0
                if before:
                    yield "R1", q, 0
                if here:
                    yield "X", p, 0
                    yield "La", p, 1
                if before:
                    yield "R2", q, 0
                if here:
                    yield "Lb", p, 1
                    yield "La", p, 2
                if before:
                    yield "R1", q, 1
                if here:
                    yield "Lb", p, 2
                    yield "La", p, 3
                if before:
                    yield "R2", q, 1
                if here:
                    yield "Lb", p, 3
                    yield "La", p, 4
                if before:
                    yield "R3", q, 0
                if here:
                    yield "Lb", p, 4
                    yield "La", p, 5
                    yield "Lb", p, 5
                    yield "fin", p, 0

        def gdn_sp(sp):
            sp.wait_ge(s_ln2, 8)
            sp.dma_start(lvl[:, :], A["const"][:, 400:1168]).then_inc(s_lvl, 16)

        def gdn_pe(pe):
            for what, p, n in gdn_plan():
                ps = slice(p * P, (p + 1) * P)
                if what == "prep":
                    if p == 0:
                        pe.wait_ge(s_gate, 1)
                    else:
                        pe.wait_ge(s_w1, 5 * p)
                        pe.wait_ge(s_xx, 4 * p)
                    pe.wait_ge(s_dg, 2 * p + 2)
                    pe.matmul(bank(0), ones[:, :], dgG[:, :], start=True, stop=True).then_inc(s_pp, 1)
                    pe.matmul(bank(1), ones[:, :], dgB[:, :], start=True, stop=True).then_inc(s_pp, 1)
                    if p:
                        pe.wait_ge(s_y, 6 * p)
                        pe.wait_ge(s_wts, p)
                    for h in range(4):
                        mm = pe.matmul(hd(bank(2), h), gkF[:, h, ps], gkF[:, h, ps], start=True, stop=True)
                    mm.then_inc(s_pp, 1)
                    for h in range(4):
                        mm = pe.matmul(hd(bank(3), h), gkF[:, h, ps], gqF[:, h, ps], start=True, stop=True)
                    mm.then_inc(s_pp, 1)
                elif what == "X":
                    pe.wait_ge(s_y, 6 * p + 1)
                    pe.wait_ge(s_de, 3 * p + 3)
                    for h in range(4):
                        mm = pe.transpose(hd(bank(0), h), hd(Y, h), ident)
                    mm.then_inc(s_xt, 1)
                elif what == "La":
                    if n == 1:
                        pe.wait_ge(s_x1, p + 1)
                    else:
                        pe.wait_ge(s_xx, 4 * p + n - 1)
                    pe.wait_ge(s_us, 6 * p + n + 1)
                    for h in range(4):
                        mm = pe.matmul(hd(bank(0), h), hd(Us[:, n % 2, :], h), hd(X, h), start=True, stop=True)
                    mm.then_inc(s_la, 1)
                elif what == "Lb":
                    pe.wait_ge(s_w1, 5 * p + n)
                    pe.wait_ge(s_y, 6 * p + n)
                    if n < 5:
                        for h in range(4):
                            pe.matmul(hd(bank(1), h), hd(Y, h), hd(W1, h), start=True, stop=True)
                    for h in range(4):
                        mm = pe.matmul(hd(bank(2), h), hd(W1, h), hd(Y, h), start=True, stop=True)
                    mm.then_inc(s_lb, 1)
                elif what == "fin":
                    pe.wait_ge(s_y, 6 * p + 6)
                    pe.wait_ge(s_vkk, 3 * p + 3)
                    pe.wait_ge(s_I, p + 1)
                    for h in range(4):
                        mm = pe.matmul(hd(bank(3), h), hd(kb, h), hd(Y, h), start=True, stop=True)
                    mm.then_inc(s_wt, 1)
                    if p >= 2:
                        pe.wait_ge(s_vn, 2 * p - 2)
                    for h in range(4):
                        mm = pe.matmul(hd(att[:, p % 2, :], h), hd(Y, h), hd(vb, h), start=h == 0, stop=True, skip_group_check=True)
                    mm.then_inc(s_v, 1)
                elif what == "R1":
                    if 2 * p + n:
                        pe.wait_ge(s_S, 2 * p + n)
                        if n == 0:
                            pe.wait_ge(s_of, p)
                    pe.wait_ge(s_wts, p + 1)
                    pe.wait_ge(s_qe, p + 1)
                    r = slice(64 * n, 64 * n + 64)
                    if 2 * p + n == 0:
                        pe.matmul(att[0:64, 0, 0:2], zero[:, :], ones[:, 0:2], start=False, stop=True, skip_group_check=True).then_inc(s_r1, 1)
                        continue
                    for h in range(4):
                        mm = pe.matmul(hd(att[r, p % 2, :], h), wT[:, p % 2, h * P + 64 * n:h * P + 64 * n + 64], Sg[:, h, :],
                                       start=False, stop=True, skip_group_check=True)
                    mm.then_inc(s_r1, 1)
                    for h in range(4):
                        c = h * P + 64 * n
                        pe.matmul(att[:, 2, c:c + 64], Sg[:, h, :], qe[:, p % 2, c:c + 64],
                                  start=h == 0 and (n == 0 or p == 0), stop=True, skip_group_check=True)
                elif what == "R2":
                    pe.wait_ge(s_vn, 2 * p + n + 1)
                    r = slice(64 * n, 64 * n + 64)
                    for h in range(4):
                        mm = pe.matmul(hd(att[:, 3, :], h), kd[r, p % 2, h * P:(h + 1) * P], vn[r, h * P:(h + 1) * P], start=True, stop=True)
                    mm.then_inc(s_r2, 1)
                elif what == "R3":
                    for h in range(4):
                        mm = pe.matmul(hd(att[:, 2, :], h), hd(vn, h), hd(In[:, p % 2, :], h), start=False, stop=True, skip_group_check=True)
                    mm.then_inc(s_r3, 1)

        def gdn_act(act):
            for what, p, n in gdn_plan():
                if what == "prep":
                    act.wait_ge(s_dt, p + 1)
                    act.activation(Dm[:, :], Dm[:, :], ACT.Exp).then_inc(s_de, 1)
                    if p >= 2:
                        act.wait_ge(s_r3, p - 1)
                    act.activation(qe[:, p % 2, :], bank(0), ACT.Exp).then_inc(s_de, 1)
                    if p >= 2:
                        act.wait_ge(s_S, 2 * p - 2)
                    act.activation(decg[:, p % 2, :, :], h4(bank(0))[:, :, 63::64], ACT.Exp).then_inc(s_de, 1)
                elif what == "X":
                    act.wait_ge(s_xt, p + 1)
                    act.activation(X[:, :], bank(0), ACT.Copy).then_inc(s_x1, 1)
                elif what == "La":
                    act.wait_ge(s_la, 5 * p + n)
                    if n == 1 and p:
                        act.wait_ge(s_lb, 5 * p)
                    act.activation(W1[:, :], bank(0), ACT.Copy).then_inc(s_w1, 1)
                elif what == "fin":
                    act.wait_ge(s_wt, p + 1)
                    act.activation(wT[:, p % 2, :], bank(3), ACT.Copy, scale=-1.0).then_inc(s_wts, 1)
                elif what == "R1":
                    act.wait_ge(s_r1, 2 * p + n + 1)
                    act.wait_ge(s_v, p + 1)
                    if n == 0 and p:
                        act.wait_ge(s_r3, p)
                    r = slice(64 * n, 64 * n + 64)
                    act.activation(vn[r, :], att[r, p % 2, :], ACT.Copy).then_inc(s_vn, 1)
                elif what == "R3":
                    act.wait_ge(s_r3, p + 1)
                    act.activation(gqF[:, :, p * P:(p + 1) * P], h4(att[:, 2, :]), ACT.Copy).then_inc(s_of, 1)

        def gdn_pool(pool):
            pool.wait_ge(s_ln2, 8)
            pool.wait_ge(s_hmv, 32)
            pool.wait_ge(s_gate, 2)
            pool.wait_ge(s_lvl, 16)
            for what, p, n in gdn_plan():
                if what == "prep":
                    if p:
                        pool.wait_ge(s_pp, 4 * p)
                    pool.tensor_tensor(h4(dgG[:, :]), bc4(ident), col4(1, p), ALU.mult).then_inc(s_dg, 1)
                    pool.tensor_tensor(h4(dgB[:, :]), bc4(ident), col4(3, p), ALU.mult).then_inc(s_dg, 1)
                    pool.wait_ge(s_de, 3 * p + 1)
                    pool.tensor_tensor(h4(Dm[:, :]), h4(Dm[:, :]), bc4(causal), ALU.mult).then_inc(s_dm, 1)
                    pool.wait_ge(s_U, p + 1)
                    if p:
                        pool.wait_ge(s_la, 5 * p)
                    for k in range(2):
                        pool.tensor_tensor(h4(Us[:, k, :]), h4(U[:, :]), bc4(lvl[:, k * P:(k + 1) * P]), ALU.mult).then_inc(s_us, 1)
                elif what == "La":
                    k = n + 1
                    if k <= 5:
                        if k == 2:
                            pool.wait_ge(s_y, 6 * p + 1)
                        else:
                            pool.wait_ge(s_la, 5 * p + k - 2)
                        pool.tensor_tensor(h4(Us[:, k % 2, :]), h4(U[:, :]), bc4(lvl[:, k * P:(k + 1) * P]), ALU.mult).then_inc(s_us, 1)
                    if n == 1:
                        if p:
                            pool.wait_ge(s_v, p)
                        pool.tensor_tensor(h4(vb[:, :]), h4(gvT[:, p, :]), col4(3, p), ALU.mult).then_inc(s_vkk, 1)
                    if n == 2:
                        pool.tensor_tensor(h4(kb[:, :]), h4(gkT[:, p, :]), col4(7, p), ALU.mult).then_inc(s_vkk, 1)
                    if n == 3:
                        if p >= 2:
                            pool.wait_ge(s_r2, 2 * p - 2)
                        pool.tensor_tensor(h4(kd[:, p % 2, :]), h4(gkT[:, p, :]), col4(6, p), ALU.mult).then_inc(s_vkk, 1)

        def gdn_dve(dve):
            dve.memset(zero[:, :], 0.0).then_inc(s_set, 1)
            for what, p, n in gdn_plan():
                ps = slice(p * P, (p + 1) * P)
                if what == "prep":
                    if p == 0:
                        dve.wait_ge(s_hmv, 32)
                        dve.wait_ge(s_gate, 2)
                    else:
                        dve.wait_ge(s_U, p)
                        dve.wait_ge(s_us, 6 * p)
                    dve.wait_ge(s_pp, 4 * p + 1)
                    for h in range(4):
                        ins = dve.tensor_scalar(hd(Dm, h), hd(bank(0), h), gsm[:, 1, 4 * p + h:4 * p + h + 1], 0.0, ALU.subtract, ALU.min)
                    ins.then_inc(s_dt, 1)
                    dve.wait_ge(s_dm, p + 1)
                    dve.wait_ge(s_pp, 4 * p + 4)
                    if p >= 2:
                        dve.wait_ge(s_r3, p - 1)
                    dlink(dve.tensor_tensor(U[:, :], bank(2), Dm[:, :], ALU.mult))
                    dve.tensor_tensor(U[:, :], U[:, :], bank(1), ALU.mult).then_inc(s_U, 1)
                    dve.tensor_tensor(In[:, p % 2, :], bank(3), Dm[:, :], ALU.mult).then_inc(s_I, 1)
                    dve.wait_ge(s_de, 3 * p + 2)
                    dve.tensor_tensor(h4(qe[:, p % 2, :]), gqF[:, :, ps], h4(qe[:, p % 2, :]), ALU.mult).then_inc(s_qe, 1)
                    dve.wait_ge(s_us, 6 * p + 1)
                    if p:
                        dve.wait_ge(s_v, p)
                    dve.tensor_tensor(h4(Y[:, :]), bc4(ident), h4(Us[:, 0, :]), ALU.subtract).then_inc(s_y, 1)
                elif what == "Lb":
                    dve.wait_ge(s_lb, 5 * p + n)
                    dve.tensor_tensor(Y[:, :], Y[:, :], bank(2), ALU.subtract).then_inc(s_y, 1)
                    if n < 5:
                        dve.tensor_tensor(X[:, :], X[:, :], bank(1), ALU.subtract).then_inc(s_xx, 1)
                elif what == "R2":
                    dve.wait_ge(s_r2, 2 * p + n + 1)
                    if p + n == 0:
                        dve.tensor_copy(Sg[:, :, :], h4(att[:, 3, :])).then_inc(s_S, 1)
                    else:
                        dve.wait_ge(s_S, 2 * p + n)
                        dve.wait_ge(s_de, 3 * p + 3)
                        for h in range(4):
                            ins = dve.scalar_tensor_tensor(out=Sg[:, h, :], in0=Sg[:, h, :], scalar=decg[:, p % 2, h, n:n + 1],
                                                           in1=hd(att[:, 3, :], h), op0=ALU.mult, op1=ALU.add)
                        ins.then_inc(s_S, 1)

        rb, sg2 = T["rb"], T["sg2"]
        og2h, og2l, os2h, os2l, mrg, mt6 = (T[x] for x in ("og2h", "og2l", "os2h", "os2l", "mrg", "mt6"))
        s_osq, s_ost, s_ors, s_ond = (sem("onorm_" + x) for x in ("sq", "stat", "rstd", "out"))
        s_gf2, s_gh2, s_gl2, s_sh2, s_sl2 = (sem("merge_" + x) for x in ("gated", "og_hi", "og_lo", "os_hi", "os_lo"))
        s_m2, s_mh, s_ml = (sem("merge_" + x) for x in ("sum", "hi", "lo"))

        def mg_sp(sp):
            sp.wait_ge(s_of, NT)
            sp.wait_ge(s_S, 2 * NT)
            sp.dma_start(hh[:, :, :].bitcast(F32).rearrange("p a b -> p (a b)"), hres.ap()[0]).then_inc(s_hmv, 16)
            sp.dma_start(hl[:, :, :].bitcast(F32).rearrange("p a b -> p (a b)"), hres.ap()[1]).then_inc(s_hmv, 16)
            for c in range(C_GG, C_O2):
                load_chunk(sp, c + AHEAD + 2)

        def mg_pe(pe):
            for x in range(4):
                pe.wait_ge(s_osq, x + 1)
                if x:
                    pe.wait_ge(s_ors, 2 * x - 1)
                for half in range(2):
                    mm = pe.matmul(att[:, half, :], ones[:, :], rb[:, x % 2, half * 512:half * 512 + 512], start=True, stop=True)
                mm.then_inc(s_ost, 1)
            pe.wait_ge(s_hmv, 64)
            xs = lambda k: (hh[:, k, :], hl[:, k, :])
            for n in range(4):
                product_f(pe, G_GG + n, C_GG + n, 0, range(KT), xs)
            osx = lambda k: (os2h[:, k, :], os2l[:, k, :])
            ogx = lambda k: (og2h[:, k, :], og2l[:, k, :])
            g, c = G_MG, C_MG
            for m in range(0, 8, 2):
                for br, src, ready in ((0, osx, s_sl2), (1, ogx, s_gl2)):
                    product_f(pe, g, c, 0, range(KT), xs)
                    if m == 0:
                        pe.wait_ge(ready, 4)
                    product_f(pe, g + 1, c + 1, 0, range(4), src)
                    product_f(pe, g + 2, c + 2, 0, range(KT), xs)
                    product_f(pe, g + 3, c + 1, P, range(4), src)
                    g += 4; c += 3

        def mg_act(act):
            act.wait_ge(s_of, NT)
            act.wait_ge(s_S, 2 * NT)
            for x in range(5):
                if x < 4:
                    if x >= 2:
                        act.wait_ge(s_ond, x - 1)
                    act.activation(rb[:, x % 2, :], gqF[:, x, :], ACT.Square).then_inc(s_osq, 1)
                if x:
                    act.wait_ge(s_ost, x)
                    act.activation(rb[:, (x - 1) % 2, :], att[:, 0:2, :].rearrange("p a b -> p (a b)"), ACT.Ln, scale=1.0 / P, bias=epsc[:, 0:1]).then_inc(s_ors, 1)
                    act.wait_ge(s_ors, 2 * x - 1)
                    act.activation(rb[:, (x - 1) % 2, :], rb[:, (x - 1) % 2, :], ACT.Exp, scale=-0.5).then_inc(s_ors, 1)
            for n in range(4):
                split_hi(act, C_GG + n + AHEAD)
                g = G_GG + n
                wait_done(act, g)
                if n >= 2:
                    act.wait_ge(s_gf2, n - 1)
                act.activation(sg2[:, n % 2, :], acc[:, g % 2, :], ACT.Silu).then_inc(acc_free[g % 2], 1)
                act.wait_ge(s_gf2, n + 1)
                act.activation(og2h[:, n, :], gqF[:, n, :], ACT.Copy).then_inc(s_gh2, 1)
            act.wait_ge(s_gl2, 4)
            for n in range(4):
                act.activation(os2h[:, n, :], sbq[:, n, :], ACT.Copy).then_inc(s_sh2, 1)
            g, c = G_MG, C_MG
            for m in range(0, 8, 2):
                for br in range(2):
                    for k in range(3):
                        split_hi(act, c + k + AHEAD)
                        if k != 1:
                            gg_, mm = (g, m) if k == 0 else (g + 2, m + 1)
                            wait_done(act, gg_)
                            if m == 0 and k == 0 and br == 0:
                                act.wait_ge(s_sl2, 4)
                            dst = mrg[:, mm, :] if br == 0 else (mrg[:, mm + 2, :] if m < 6 else mt6[:, mm - 6, :])
                            if br == 0 and m:
                                act.wait_ge(s_m2, mm - 1)
                            act.activation(dst, acc[:, gg_ % 2, :], ACT.Sigmoid).then_inc(acc_free[gg_ % 2], 1)
                    g += 4; c += 3
            for m in range(8):
                act.wait_ge(s_m2, m + 1)
                x_complete(act, G_O2)
                act.activation(hh[:, m, :], mrg[:, m, :], ACT.Copy).then_inc(s_mh, 1)

        def mg_pool(pool):
            for c in range(C_GG, C_O2):
                split_lo(pool, c + AHEAD)

        def mg_dve(dve):
            for x in range(4):
                dve.wait_ge(s_ors, 2 * x + 2)
                dve.scalar_tensor_tensor(out=gqF[:, x, :], in0=gqF[:, x, :], scalar=vcol("gdnn"), in1=rb[:, x % 2, :],
                                         op0=ALU.mult, op1=ALU.mult).then_inc(s_ond, 1)
            for n in range(4):
                g = G_GG + n
                dve.wait_ge(acc_free[g % 2], g // 2 + 1)
                dve.wait_ge(s_ond, n + 1)
                dve.tensor_tensor(gqF[:, n, :], gqF[:, n, :], sg2[:, n % 2, :], ALU.mult).then_inc(s_gf2, 1)
                dve.wait_ge(s_gh2, n + 1)
                dve.tensor_tensor(og2l[:, n, :], gqF[:, n, :], og2h[:, n, :].bitcast(F32), ALU.subtract).then_inc(s_gl2, 1)
            for n in range(4):
                dve.wait_ge(s_sh2, n + 1)
                dve.tensor_tensor(os2l[:, n, :], sbq[:, n, :], os2h[:, n, :].bitcast(F32), ALU.subtract).then_inc(s_sl2, 1)
            g = G_MG
            for m in range(0, 8, 2):
                for br in range(2):
                    for k in range(2):
                        mm = m + k
                        gs, gb = g + 2 * k, g + 2 * k + 1
                        dst = mrg[:, mm, :] if br == 0 else (mrg[:, mm + 2, :] if m < 6 else mt6[:, mm - 6, :])
                        dve.wait_ge(acc_free[gs % 2], gs // 2 + 1)
                        wait_done(dve, gb)
                        dve.tensor_tensor(dst, dst, acc[:, gb % 2, :], ALU.mult).then_inc(acc_free[gb % 2], 1)
                        if br:
                            dve.wait_ge(acc_free[gb % 2], gb // 2 + 1)
                            dve.tensor_tensor(mrg[:, mm, :], mrg[:, mm, :], dst, ALU.add).then_inc(s_m2, 1)
                    g += 4
            for m in range(8):
                dve.wait_ge(s_mh, m + 1)
                dve.tensor_tensor(hl[:, m, :], mrg[:, m, :], hh[:, m, :].bitcast(F32), ALU.subtract).then_inc(s_ml, 1)

        yF, x5, outb = T["yF"], T["x5"], T["outb"]
        s_ya, s_ot, s_oc2, s_out = sem("y_added"), sem("out_turned"), sem("out_sb"), sem("out")

        def end_sp(sp):
            for c in range(C_O2, C_END):
                load_chunk(sp, c + AHEAD + 2)
            sp.wait_ge(s_ml, 8)
            sp.dma_start(x5[:, :, :].rearrange("p a b -> p (a b)"), xres.ap()).then_inc(s_xmv, 16)
            for t in range(NT):
                sp.wait_ge(s_oc2, t + 1)
                sp.dma_start(out[0, t * P:(t + 1) * P, :], outb[:, t, :]).then_inc(s_out, 16)
            sp.wait_ge(s_out, 16 * NT)

        def end_pe(pe):
            for n in range(8):
                product_f(pe, G_O2 + n, C_O2 + n, 0, range(KT), lambda k: (hh[:, k, :], hl[:, k, :]),
                          on_kt=(lambda k: pe.wait_ge(s_ml, k + 1)) if n == 0 else None)
            norm_pe(pe, NY)
            for t in range(NT):
                if t >= 2:
                    pe.wait_ge(s_oc2, t - 1)
                for ft in range(KT):
                    if t == 0:
                        pe.wait_ge(s_ya, ft + 1)
                    mm = pe.transpose(acc[:, t % 2, ft * P:(ft + 1) * P], yF[:, ft, t * P:(t + 1) * P], ident)
                mm.then_inc(s_ot, 1)

        def end_act(act):
            for n in range(8):
                split_hi(act, C_O2 + n + AHEAD)
            x_complete(act, G_END)
            norm_act(act, NY, yF)
            for t in range(NT):
                act.wait_ge(s_ot, t + 1)
                act.activation(outb[:, t, :], acc[:, t % 2, :], ACT.Copy).then_inc(s_oc2, 1)

        def end_pool(pool):
            for n in range(8):
                split_lo(pool, C_O2 + n + AHEAD)

        def end_dve(dve):
            for n in range(8):
                g = G_O2 + n
                wait_done(dve, g)
                dve.tensor_copy(yF[:, n, :], acc[:, g % 2, :]).then_inc(acc_free[g % 2], 1)
            dve.wait_ge(s_xmv, X_BACK2)
            norm_dve(dve, NY, yF, lambda kt: vcol("post", kt), None, "inplace")
            for kt in range(KT):
                NY.wait_out(dve, kt + 1)
                dve.tensor_tensor(yF[:, kt, :], yF[:, kt, :], x5[:, kt, :], ALU.add).then_inc(s_ya, 1)

        stages = {"start": (start_sp, start_act, start_pe, start_dve, None),
                  "in": (in_sp, in_act, in_pe, in_dve, in_pool),
                  "swa": (None, swa_act, swa_pe, swa_dve, None),
                  "gla": (None, gla_act, gla_pe, gla_dve, None),
                  "out": (out_sp, out_act, out_pe, out_dve, out_pool),
                  "mlp0": mlp_stage(0, C_M0, G_M0, 1),
                  "pool": (pool_sp, pool_act, pool_pe, pool_dve, pool_pool),
                  "mlp1": mlp_stage(1, C_M1, G_M1, 3),
                  "sbin": (sbin_sp, sbin_act, sbin_pe, sbin_dve, sbin_pool),
                  "sb": (None, sb_act, sb_pe, sb_dve, sb_pool),
                  "gin": (gin_sp, gin_act, gin_pe, gin_dve, gin_pool),
                  "gdn": (gdn_sp, gdn_act, gdn_pe, gdn_dve, gdn_pool),
                  "mg": (mg_sp, mg_act, mg_pe, mg_dve, mg_pool),
                  "end": (end_sp, end_act, end_pe, end_dve, end_pool)}
        block = ctx.enter_context(nc.Block())

        @block.sync
        def _(sp):
            for s in stages:
                if stages[s][0]:
                    stages[s][0](sp)

        @block.scalar
        def _(act):
            alink.eng = act
            for s in stages:
                if stages[s][1]:
                    stages[s][1](act)

        @block.tensor
        def _(pe):
            for s in stages:
                if stages[s][2]:
                    stages[s][2](pe)

        @block.vector
        def _(dve):
            dlink.eng = dve
            for s in stages:
                if stages[s][3]:
                    stages[s][3](dve)

        @block.gpsimd
        def _(pool):
            for s in stages:
                if stages[s][4]:
                    stages[s][4](pool)



def kernel(**inputs):
    import concourse.bacc as bacc
    from concourse.bass_utils import run_bass_kernel_spmd

    nc = bacc.Bacc("TRN2", target_bir_lowering=False, num_devices=1)
    tables = dict(zip(("const", "onehot", "same"), constants()))
    arrays, args = {}, {}
    for name, a in list(inputs.items()) + list(tables.items()):
        a = np.ascontiguousarray(a)
        arrays[f"in_{name}_dram"] = a
        args[name] = nc.dram_tensor(f"in_{name}_dram", a.shape, mybir.dt.from_np(a.dtype), kind="ExternalInput").ap()
    out = nc.dram_tensor("out_0_dram", (1, S, D), F32, kind="ExternalOutput").ap()
    build_program(nc, args, out)
    result = run_bass_kernel_spmd(nc, [arrays], core_ids=[0])
    return result.results[0]["out_0_dram"]
```

```python
from contextlib import ExitStack

import numpy as np

import concourse.bass as bass
from concourse import mybir

F32 = mybir.dt.float32
F32R = mybir.dt.float32r
U32 = mybir.dt.uint32
ALU = mybir.AluOpType
ACT = mybir.ActivationFunctionType
AX_X = mybir.AxisListType.X

P = 128
S = 1024
D = 1024
KT = D // P
NT = S // P
EPS = 1e-6
FF = 4 * D
HID = 512
NBLK = FF // HID
NEG = -1e30
SLOTS = 4
RAWS = 2
AHEAD = 3
CH = 1024
NADA = 3 * KT

CONST_AT = {"ident": 0, "causal": 128, "strict": 256, "rcnt": 384, "levels": 400}
CONST_W = 1168


def t5_bucket(dist):
    d = np.maximum(dist, 1).astype(np.float64)
    large = 16 + (np.log(d / 16) / np.log(128 / 16) * 16).astype(np.int32)
    return np.where(dist < 16, dist, np.minimum(large, 31)).astype(np.int32)


def constants():
    c = np.zeros((P, CONST_W), np.float32)
    j, i = np.arange(P)[:, None], np.arange(P)[None, :]
    same = (i // 64) == (j // 64)
    c[:, 0:128] = i == j
    c[:, 128:256] = same & (i >= j)
    c[:, 256:384] = same & (i > j)
    for n in range(6):
        s = 1 << n
        c[:, 400 + 128 * n:528 + 128 * n] = (i // (2 * s) == j // (2 * s)) & (j % (2 * s) < s) & (i % (2 * s) >= s)
    c[:, 384:400] = 1.0 / (1.0 + np.arange(16))
    onehot = np.zeros((32, 384), np.float32)
    m = np.arange(128, 256)
    onehot[t5_bucket(255 - m), m] = 1.0
    return c, onehot, same.astype(np.float32)


def build_program(nc, A, out):
    ctx = ExitStack()
    with ctx:
        def sem(name):
            return ctx.enter_context(nc.semaphore(name))

        def sb(name, shape, dt=F32):
            return ctx.enter_context(nc.sbuf_tensor(name, shape, dt))

        T = {}

        def region(name, kb, *plans):
            for plan in plans:
                with ExitStack() as turn:
                    size = 0
                    for n, shape, dt in plan:
                        T[n] = turn.enter_context(nc.sbuf_tensor(n, shape, dt))
                        size += 4 * int(np.prod(shape[1:]))
                    assert size <= kb * 1024, (name, size)
            sb(name, [P, kb * 256])

        raw = sb("raw", [P, RAWS, CH])
        wh = sb("wh", [P, SLOTS, CH], F32R)
        wl = sb("wl", [P, SLOTS, CH], F32R)
        region("R0", 32,
               [("xT", [P, KT, S], F32)],
               [("sq", [P, 4, S], F32), ("sk", [P, S], F32), ("sv", [P, NT, P], F32), ("bias", [P, 8, 256], F32)],
               [("ogh", [P, 4, S], F32R), ("ogl", [P, 4, S], F32R)],
               [("ah", [P, 4, S], F32R), ("al", [P, 4, S], F32R)],
               [("hp", [P, KT, S], F32)],
               [("sbq", [P, 4, S], F32), ("sbk", [P, 4, S], F32)],
               [("pad3", [P, 4 * S], F32), ("gkF", [P, 4, S], F32)],
               [("mrg", [P, KT, S], F32)],
               [("x5", [P, KT, S], F32)])
        region("H", 64,
               [("G", [P, 8, 384], F32), ("relrep", [32, 8, P], F32), ("onehot", [32, 384], F32), ("rows", [P, 2, P], F32)],
               [("hh", [P, KT, S], F32R), ("hl", [P, KT, S], F32R)],
               [("pad8", [P, 6 * S], F32), ("winA", [P, 2, S], F32), ("pad9", [P, 6 * S], F32), ("winB", [P, 2, S], F32)],
               [("osh", [P, 4, S], F32R), ("osl", [P, 4, S], F32R), ("ssb", [P, 4, 1024], F32), ("pT", [P, 2, 1024], F32)],
               [("pad0", [P, 8 * S], F32), ("kt_", [P, 2, S], F32), ("keT", [P, NT, 256], F32), ("Eb", [P, 2, S], F32),
                ("rmask", [P, S], F32), ("asb", [P, 2, 512], F32)],
               [("g_" + n, [P, 512], F32) for n in ("dgG", "dgB", "D", "U", "X", "Y", "W1", "vb", "kb", "vn")] +
               [("g_" + n, [P, 2, 512], F32) for n in ("Us", "I", "kd", "wT", "qe")],
               [("outb", [P, NT, D], F32)],
               [("pad1", [P, 12 * S], F32), ("osq", [P, 2, 512], F32), ("orstd", [P, 2, 512], F32), ("ofull", [P, 2, 512], F32)])
        region("R3a", 32,
               [("ab0", [P, 4, 1024], F32), ("acc0", [P, 3, 1024], F32)],
               [("gq", [P, 2, S], F32), ("gk", [P, 2, S], F32), ("gv", [P, NT, 512], F32)],
               [("xb", [P, KT, S], F32)],
               [("sbv", [P, NT, 512], F32), ("onesb", [P, S], F32), ("lowm", [P, P], F32)],
               [("pad4", [P, 4 * S], F32), ("sgt", [P, 2, S], F32), ("vtmp", [P, S], F32)],
               [("gvT", [P, NT, 512], F32), ("gkT", [P, NT, 512], F32)],
               [("og2h", [P, 4, S], F32R), ("og2l", [P, 4, S], F32R)],
               [("yF", [P, KT, S], F32)])
        region("R3b", 32,
               [("xin", [P, NT, D], F32)],
               [("rbuf", [P, 2, S], F32), ("sq1", [P, S], F32), ("tb", [P, 2, S], F32), ("rstd", [P, S], F32), ("sqb", [P, 2, S], F32)],
               [("pad7", [P, 3 * S], F32), ("ab2", [P, 4, 1024], F32), ("acc2", [P, 1024], F32)],
               [("gg", [P, 4, S], F32), ("la", [P, 2, S], F32), ("cum", [P, 2, S], F32)],
               [("pad2", [P, 4 * S], F32), ("st", [P, 16, 2, P], F32)],
               [("ab1", [P, 4, 1024], F32), ("acc1", [P, 1024], F32)],
               [("sb_e", [P, 3, S], F32), ("sb_s", [P, 3, S], F32), ("sb_aT", [P, 2, S], F32)],
               [("gqF", [P, 4, S], F32), ("pad", [P, S + 4], F32), ("cv", [P, 2, S], F32)],
               [("pad5", [P, 4 * S], F32), ("g_S", [P, 4, P], F32), ("g_lvl", [P, 768], F32), ("g_dec", [P, 2, 4, 2], F32)],
               [("pad6", [P, 4 * S], F32), ("rb", [P, 2, S], F32), ("sg2", [P, 2, S], F32)],
               [("os2h", [P, 4, S], F32R), ("os2l", [P, 4, S], F32R)],
               [("mt6", [P, 2, S], F32)])
        zero = sb("zero", [P, 64])
        gsm = sb("gsm", [P, 8, 32])
        dtb = sb("dtb", [P, 8])
        T["same"] = sb("same", [P, P])
        cst = sb("cst", [P, 400])
        ones = sb("ones", [P, P])
        vt = sb("vt", [P, 220])
        mod = sb("mod", [P, 96])
        mul = sb("mul", [P, 32])
        sc = sb("sc", [P, 8])
        wgate = sb("wgate", [16, 256])
        pgate = sb("pgate", [P, 8])
        epsc = sb("epsc", [P, 1])
        sinks = sb("sinks", [P, 8])
        relb = sb("relb", [32, 8])
        stat8 = sb("stat8", [P, 2, 5, 8])
        dec = sb("dec", [P, 2, 16])
        xT, xb, rows = T["xT"], T["xb"], T["rows"]
        ident, causal, rcnt = cst[:, 0:128], cst[:, 128:256], cst[:, 384:400]

        acc = ctx.enter_context(nc.psum_tensor("acc", [P, 2, 1024], F32))
        att = ctx.enter_context(nc.psum_tensor("att", [P, 4, 512], F32))
        xres = nc.dram_tensor("xres", [P, KT * S], F32, kind="Internal")
        hres = nc.dram_tensor("hres", [2, P, KT * S], F32, kind="Internal")
        gscr = nc.dram_tensor("gscr", [8 * P * 384], F32, kind="Internal")

        raw_in = [sem(f"raw_in{n}") for n in range(RAWS)]
        w_hi, w_lo = sem("w_hi"), sem("w_lo")
        acc_done = [sem("acc_done0"), sem("acc_done1")]
        acc_free = [sem("acc_free0"), sem("acc_free1")]
        dstep, astep = sem("dstep"), sem("astep")

        class Chain:
            def __init__(self, s):
                self.s, self.n, self.extra = s, 0, 0

            def __call__(self, ins):
                self.n += 1
                ins.then_inc(self.s, 1)
                self.eng.wait_ge(self.s, self.n + self.extra)

        dlink, alink = Chain(dstep), Chain(astep)

        chunks = []
        G = [0]

        def kview(w, cols):
            return w.rearrange("(k p) c -> p k c", p=P)[:, :, cols]

        win = A["attn_w_in"][0]
        G_XT = G[0]; G[0] += 8
        C_IN = len(chunks)
        G_IN = G[0]
        for p in range(4):
            src = [(slice(0, P), slice(0, KT), slice(64 * g, 64 * g + 64), kview(win, slice(1552 + g * 256 + p * 64, 1616 + g * 256 + p * 64)))
                   for g in range(2)]
            chunks.append((src, KT, 128, G[0])); G[0] += 1
        chunks.append((kview(win, slice(2064, 2192)), KT, 128, G[0])); G[0] += 1
        chunks.append((kview(win, slice(2192, 2320)), KT, 128, G[0])); G[0] += 1
        for n in range(4):
            chunks.append((kview(win, slice(n * 128, n * 128 + 128)), KT, 128, G[0])); G[0] += 1
        for n in range(4):
            chunks.append((kview(win, slice(512 + n * 128, 640 + n * 128)), KT, 128, G[0] + 2 * (n // 2) + 1))
        G[0] += 4
        for n in range(4):
            chunks.append((kview(win, slice(1024 + n * 128, 1152 + n * 128)), KT, 128, G[0])); G[0] += 1
        chunks.append((kview(win, slice(1536, 1552)), KT, 16, G[0])); G[0] += 1
        C_OUT, G_OUT = len(chunks), G[0]
        for n in range(8):
            w = A["attn_w_out"][0][:, n * P:(n + 1) * P]
            src = [(slice(0, P), slice(0, 4), slice(0, P), w[0:512, :].rearrange("(k p) c -> p k c", p=P))]
            src += [(slice(64 * g, 64 * g + 64), slice(4, 8), slice(0, P),
                     w[512 + 256 * g:768 + 256 * g, :].rearrange("(k p) c -> p k c", p=64)) for g in range(2)]
            chunks.append((src, KT, P, G[0])); G[0] += 1

        def mlp_src(l, i, k):
            if k < 4:
                return A["mlp_w1"][l].rearrange("(k p) c -> p k c", p=P)[:, :, bass.ds(i * HID + k * P, P)]
            w2 = A["mlp_w2"][l].rearrange("(i k p) c -> i p k c", p=P, k=4)
            return w2[i, :, :, (k - 4) * 256:(k - 3) * 256] if isinstance(i, int) else \
                w2[bass.ds(i, 1), :, :, (k - 4) * 256:(k - 3) * 256].rearrange("i p k c -> (i p) k c")

        def add_mlp(l):
            cb, gb = len(chunks), G[0]
            for i in range(NBLK):
                for k in range(8):
                    chunks.append(((lambda l=l, k=k: (lambda j: mlp_src(l, j, k)))(), KT if k < 4 else 4, 128 if k < 4 else 256,
                                   gb + 12 * i + (k if k < 4 else 5 + 2 * (k - 4))))
            G[0] += 12 * NBLK
            return cb, gb

        C_M0, G_M0 = add_mlp(0)
        C_PL, G_PL = len(chunks), G[0]
        for q in range(2):
            src = A["pool_w"][0].rearrange("g (k p) c -> p (g k) c", p=P)[:, 4 * q:4 * q + 4, :]
            chunks.append((src, 4, 256, G[0] + 3)); G[0] += 4
        C_M1, G_M1 = add_mlp(1)
        win2c = lambda a, n=P: (kview(A["w_in_2"][0], slice(a, a + n)), KT, n)
        C_SB, G_SB = len(chunks), G[0]
        assert (C_SB + 7) % 2 == 0
        for n in range(7):
            chunks.append((*win2c(n * P), G[0])); G[0] += 1
        for n in range(4):
            chunks.append((*win2c(1024 + n * P), G[0] + 2 * (n // 2) + 1))
        G[0] += 4
        chunks.append((*win2c(7 * P), G[0])); G[0] += 1
        C_SG, G_SG = len(chunks), G[0]
        for n in range(4):
            chunks.append((*win2c(1536 + n * P), G[0])); G[0] += 1
        C_GD, G_GD = len(chunks), G[0]
        for n in list(range(8, 12)) + list(range(8)):
            chunks.append((*win2c(2048 + n * P), G[0])); G[0] += 1
        C_AB, G_AB = len(chunks), G[0]
        chunks.append((*win2c(4096, 8), G[0])); G[0] += 1
        C_GG, G_GG = len(chunks), G[0]
        for n in range(4):
            chunks.append((*win2c(3584 + n * P), G[0])); G[0] += 1
        C_MG, G_MG = len(chunks), G[0]
        branch = lambda name, m: (A[name][0].rearrange("(k p) c -> p k c", p=P)[:, :, m * P:(m + 2) * P], 4, 256)
        for m in range(0, 8, 2):
            for name, c0 in (("w_branch_sb_2", 4104), ("w_branch_gdn_2", 5128)):
                chunks.append((*win2c(c0 + m * P), G[0]))
                chunks.append((*branch(name, m), G[0] + 3))
                chunks.append((*win2c(c0 + m * P + P), G[0] + 2))
                G[0] += 4
        C_O2, G_O2 = len(chunks), G[0]
        for n in range(8):
            chunks.append((kview(A["w_out_2"][0], slice(n * P, n * P + P)), KT, P, G[0])); G[0] += 1
        C_END, G_END = len(chunks), G[0]

        def wait_done(eng, g, extra=0):
            eng.wait_ge(acc_done[g % 2], g // 2 + 1 + extra)

        def load_chunk(sp, c, i=None, step=0):
            if c >= C_END:
                return
            src, nk, ncol, _ = chunks[c]
            if callable(src):
                src = src(i if i is not None else (c - (C_M0 if c < C_PL else C_M1)) // 8)
            if c >= RAWS:
                sp.wait_ge(w_lo, c - RAWS + 1 + step)
            if isinstance(src, list):
                view = raw[:, c % RAWS, 0:nk * ncol].rearrange("p (k c) -> p k c", k=nk)
                for ps, ks, cs, s in src:
                    sp.dma_start(view[ps, ks, cs], s).then_inc(raw_in[c % RAWS], 16)
            else:
                sp.dma_start(raw[:, c % RAWS, 0:nk * ncol], src).then_inc(raw_in[c % RAWS], 16)

        def landed(c):
            return sum(16 * (len(chunks[k][0]) if isinstance(chunks[k][0], list) else 1) for k in range(c % RAWS, c + 1, RAWS))

        def split_hi(act, c, step=0, gstep=0):
            if c >= C_END:
                return
            n = chunks[c][1] * chunks[c][2]
            act.wait_ge(raw_in[c % RAWS], landed(c) + step * (16 // RAWS))
            if c >= SLOTS:
                wait_done(act, chunks[c - SLOTS][3], gstep)
            act.activation(wh[:, c % SLOTS, 0:n], raw[:, c % RAWS, 0:n], ACT.Copy).then_inc(w_hi, 1)

        def split_lo(pool, c, step=0):
            if c >= C_END:
                return
            n = chunks[c][1] * chunks[c][2]
            pool.wait_ge(w_hi, c + 1 + step)
            pool.tensor_tensor(wl[:, c % SLOTS, 0:n], raw[:, c % RAWS, 0:n],
                               wh[:, c % SLOTS, 0:n].bitcast(F32), ALU.subtract).then_inc(w_lo, 1)

        def acc_ready(pe, g, extra=0):
            if g >= 2:
                pe.wait_ge(acc_free[g % 2], g // 2 + extra)

        def product_f(pe, g, c, cols, kts, xs, width=P, step=0, gstep=0, on_kt=None):
            pe.wait_ge(w_lo, c + 1 + step)
            acc_ready(pe, g, gstep)
            for n, kt in enumerate(kts):
                if on_kt:
                    on_kt(n)
                xh, xl = xs(n)
                at = kt * chunks[c][2] + cols
                h, l = wh[:, c % SLOTS, at:at + width], wl[:, c % SLOTS, at:at + width]
                for half in range(2):
                    o = acc[0:width, g % 2, half * 512:half * 512 + 512]
                    s = slice(half * 512, half * 512 + 512)
                    first, last = n == 0, n == len(kts) - 1
                    pe.matmul(o, h, xh[:, s], start=first, stop=False)
                    pe.matmul(o, h, xl[:, s], start=False, stop=False)
                    mm = pe.matmul(o, l, xh[:, s], start=False, stop=last)
            mm.then_inc(acc_done[g % 2], 1)

        def product_pair(pe, g, c, xs, on_kt):
            for k in range(2):
                pe.wait_ge(w_lo, c + k + 1)
                acc_ready(pe, g + k)
            for kt in range(KT):
                on_kt(kt)
                xh, xl = xs(kt)
                for k in range(2):
                    lh, ll = (w[:, (c + k) % SLOTS, kt * P:(kt + 1) * P] for w in (wh, wl))
                    for half in range(2):
                        t = slice(half * 512, half * 512 + 512)
                        o = acc[:, (g + k) % 2, t]
                        pe.matmul(o, lh, xh[:, t], start=kt == 0, stop=False)
                        pe.matmul(o, lh, xl[:, t], start=False, stop=False)
                        mm = pe.matmul(o, ll, xh[:, t], start=False, stop=kt == KT - 1)
                    if kt == KT - 1:
                        mm.then_inc(acc_done[(g + k) % 2], 1)

        def product_t(pe, g, c, nch, t0, nt):
            pe.wait_ge(w_lo, c + nch)
            acc_ready(pe, g)
            N = nch * P
            for t in range(nt):
                o = acc[:, g % 2, t * N:(t + 1) * N]
                ts = slice((t0 + t) * P, (t0 + t + 1) * P)
                for kt in range(KT):
                    ks = slice(kt * P, kt * P + P)
                    s0 = c % SLOTS
                    rh, rl = wh[:, s0:s0 + nch, ks], wl[:, s0:s0 + nch, ks]
                    pe.matmul(o, hh[:, kt, ts], rh, start=kt == 0, stop=False)
                    pe.matmul(o, hh[:, kt, ts], rl, start=False, stop=False)
                    mm = pe.matmul(o, hl[:, kt, ts], rh, start=False, stop=kt == KT - 1)
            mm.then_inc(acc_done[g % 2], 1)

        hh, hl = T["hh"], T["hl"]
        sqb, tb, rstd = T["sqb"], T["tb"], T["rstd"]

        norm_sems = {x: sem("norm_" + x) for x in ("sq", "stat", "rs", "t", "hi", "out")}
        norm_at = dict.fromkeys(norm_sems, 0)

        class Norm:
            def __init__(self, mode):
                self.sq, self.stat, self.rs, self.t, self.hi, self.out = norm_sems.values()
                self.sq0, self.stat0, self.rs0, self.t0, self.hi0, self.out0 = norm_at.values()
                of_x = 0 if mode == "second" else KT
                for x, n in (("sq", of_x), ("stat", of_x), ("rs", of_x // KT), ("t", 0 if mode == "inplace" else KT),
                             ("hi", 0 if mode == "inplace" else KT), ("out", 0 if mode == "plain" else KT)):
                    norm_at[x] += n

            def wait_out(self, eng, n):
                eng.wait_ge(self.out, self.out0 + n)

        N0, N_mlp0, NP_, N_mlp1, N2, NF, NY = (Norm(m) for m in ("split", "split", "plain", "split", "second", "inplace", "inplace"))

        def norm_add(dve, N, kt):
            if kt:
                dve.wait_ge(N.sq, N.sq0 + kt + 1)
                if kt > 1:
                    dve.wait_ge(N.stat, N.stat0 + kt - 1)
                dve.tensor_tensor(rstd[:, :], rstd[:, :], sqb[:, kt % 2, :], ALU.add).then_inc(N.stat, 1)

        def norm_sum_tile(pe, N, kt):
            pe.wait_ge(N.sq, N.sq0 + kt + 1)
            for half in range(2):
                t = slice(half * 512, half * 512 + 512)
                mm = pe.matmul(att[:, half, :], ones[:, :], sqb[:, kt % 2, t] if kt else rstd[:, t], start=kt == 0, stop=kt == KT - 1)
            mm.then_inc(N.stat, 1)

        def norm_sum(pe, N):
            pe.wait_ge(N.stat, N.stat0 + KT - 1)
            for half in range(2):
                mm = pe.matmul(att[:, half, :], ones[:, :], rstd[:, half * 512:half * 512 + 512], start=True, stop=True)
            mm.then_inc(N.stat, 1)

        def added(eng, g):
            eng.wait_ge(acc_free[g % 2], g // 2 + 1)

        def x_complete(eng, g):
            for n in (g - 2, g - 1):
                added(eng, n)

        def norm_square(act, N, X, kt, on_pe=False):
            if kt >= 3:
                act.wait_ge(N.stat, N.stat0 + kt - 2 + on_pe)
            act.activation(sqb[:, kt % 2, :] if kt else rstd[:, :], X[:, kt, :], ACT.Square).then_inc(N.sq, 1)

        def norm_rstd(act, N):
            act.wait_ge(N.stat, N.stat0 + KT)
            alink(act.activation(rstd[:, :], att[:, 0:2, :].rearrange("p a b -> p (a b)"), ACT.Ln, scale=1.0 / D, bias=epsc[:, 0:1]))
            act.activation(rstd[:, :], rstd[:, :], ACT.Exp, scale=-0.5).then_inc(N.rs, 1)

        def norm_act(act, N, a=None, b=None, dest=None):
            for kt in range(KT):
                act.wait_ge(N.t, N.t0 + kt + 1)
                bias = b(kt) if b else 0.0
                if dest is not None:
                    act.activation(dest[:, kt, :], tb[:, kt % 2, :], ACT.Identity, bias=bias, scale=a(kt)).then_inc(N.hi, 1)
                    continue
                if kt >= 2:
                    act.wait_ge(N.out, N.out0 + kt - 1)
                alink(act.activation(sqb[:, kt % 2, :], tb[:, kt % 2, :], ACT.Identity, bias=bias, scale=a(kt)))
                act.activation(hh[:, kt, :], sqb[:, kt % 2, :], ACT.Copy).then_inc(N.hi, 1)

        def norm_dve(dve, N, X, a, mode, rs=rstd):
            if rs is rstd:
                dve.wait_ge(N.rs, N.rs0 + 1)
            for kt in range(KT + 1):
                if kt < KT:
                    if mode == "inplace":
                        dve.scalar_tensor_tensor(out=X[:, kt, :], in0=X[:, kt, :], scalar=a(kt), in1=rstd[:, :],
                                                 op0=ALU.mult, op1=ALU.mult).then_inc(N.out, 1)
                        continue
                    if kt >= 2:
                        dve.wait_ge(N.hi, N.hi0 + kt - 1)
                    dve.tensor_tensor(tb[:, kt % 2, :], X[:, kt, :], rs[:, :], ALU.mult).then_inc(N.t, 1)
                if kt >= 1 and mode == "split":
                    j = kt - 1
                    dve.wait_ge(N.hi, N.hi0 + j + 1)
                    dve.tensor_tensor(hl[:, j, :], sqb[:, j % 2, :], hh[:, j, :].bitcast(F32), ALU.subtract).then_inc(N.out, 1)

        def modcol(sub, third, m):
            c = sub * 24 + third * 8 + m
            return mod[:, c:c + 1]

        s_ada_in = [sem(f"ada_in{n}") for n in range(4)]
        s_ada_use, s_ada_sum, s_ada_mod = sem("ada_use"), sem("ada_sum"), sem("ada_mod")
        ADA_ORDER = [0, 1, 3, 2]
        ada = A["ada_w"].rearrange("a b k c -> (a b) k c")

        FIRST = 2 * KT
        GATE_LOADS = {4: range(16, 19), 6: range(19, 21), 7: range(21, 23), 8: range(23, 24)}
        GATE_MULTS = {1: range(16, 19), 2: range(19, 21), 3: range(21, 23), 4: range(23, 24)}

        def ada_buf(n):
            return (T["ab0"], T["acc0"][:, n // 8, :]) if n < NADA else (T["ab1"], T["acc1"][:, :])

        def ada_load(sp, n):
            sub, r = ADA_ORDER[n // NADA], n % NADA
            if n >= 4:
                sp.wait_ge(s_ada_use, n - 3)
            sp.dma_start(ada_buf(n)[0][:, n % 4, :], ada[sub, (r % 8) * P:(r % 8 + 1) * P, (r // 8) * 1024:(r // 8 + 1) * 1024])\
                .then_inc(s_ada_in[n % 4], 16)

        def ada_mult(dve, n):
            ab, ac = ada_buf(n)
            kt = n % 8
            dve.wait_ge(s_ada_in[n % 4], 16 * (n // 4 + 1))
            if kt == 0:
                dve.tensor_scalar(ac, ab[:, n % 4, :], sc[:, 0:1], None, ALU.mult).then_inc(s_ada_use, 1)
            else:
                dve.wait_ge(s_ada_use, n)
                dve.scalar_tensor_tensor(out=ac, in0=ab[:, n % 4, :], scalar=sc[:, kt:kt + 1], in1=ac,
                                         op0=ALU.mult, op1=ALU.add).then_inc(s_ada_use, 1)

        def ada_at(third):
            return 8 * third if third < 3 else 0

        def ada_sum(pe, third):
            pe.wait_ge(s_ada_use, 8 * third + 8)
            if third > 2:
                pe.wait_ge(s_ada_mod, third)
            for m in range(8):
                at = ada_at(third) + m
                mm = pe.matmul(att[:, 3, at:at + 1], ada_buf(8 * third)[1][:, m * P:(m + 1) * P], ones[:, 0:1], start=True, stop=True)
            mm.then_inc(s_ada_sum, 1)

        def ada_mod(dve, third):
            c0 = ADA_ORDER[third // 3] * 24 + (third % 3) * 8
            dve.wait_ge(s_ada_sum, max(third + 1, 2))
            dve.tensor_tensor(mod[:, c0:c0 + 8], att[:, 3, ada_at(third):ada_at(third) + 8], vt[:, c0:c0 + 8], ALU.add).then_inc(s_ada_mod, 1)

        def ada_scale(dve, sub):
            dve.scalar_tensor_tensor(out=mul[:, sub * 8:sub * 8 + 8], in0=mod[:, sub * 24 + 8:sub * 24 + 16], scalar=1.0,
                                     in1=vt[:, 96 + sub * 8:104 + sub * 8], op0=ALU.add, op1=ALU.mult).then_inc(s_mul, 1)

        s_mul = sem("mul_ready")
        s_x, s_row, s_cst, s_vt, s_sc, s_set = sem("x_in"), sem("rows_in"), sem("cst_in"), sem("vt_ready"), sem("silu_c"), sem("set")
        s_vps = sem("rows_turned")
        s_rel, s_gps, s_gsb, s_bias = sem("relrep"), sem("g_ps"), sem("g_sb"), sem("bias_moved")
        s_xmv, X_OUT, X_BACK, X_OUT2, X_BACK2 = sem("x_moved"), 16, 32, 48, 64

        def start_sp(sp):
            for t in range(NT):
                sp.dma_start(T["xin"][:, t, :], A["x"][0, t * P:(t + 1) * P, :]).then_inc(s_x, 16)
            for n in range(FIRST):
                if n == 8:
                    for c in range(2):
                        load_chunk(sp, c)
                ada_load(sp, n)
            for c in (2, 3):
                load_chunk(sp, c)
            for h in range(2):
                sp.wait_ge(acc_free[h], 4)
            sp.dma_start(xres.ap(), xT[:, :, :].rearrange("p a b -> p (a b)")).then_inc(s_xmv, 16)

        def rowsrc():
            v = lambda x, r: x.rearrange("(r c) -> r c", c=P) if r is None else x
            yield 0, 0, 96, A["ada_b"].rearrange("a b (r c) -> (a b r) c", c=P)
            yield 0, 96, 32, A["norm_w"].rearrange("a b (r c) -> (a b r) c", c=P)
            at = 0
            for name, n in (("c", 8), ("final_norm_w", 8), ("pool_scale", 8), ("pre_norm_w_2", 8), ("post_norm_w_2", 8),
                            ("gla_norm_w", 1), ("gdn_norm_w_2", 1), ("gla_b_gate", 2), ("conv_w_2", 48)):
                ap = A[name]
                if name == "final_norm_w":
                    src = ap.rearrange("(r c) -> r c", c=P)
                elif name == "conv_w_2":
                    src = ap.rearrange("a t (r c) -> (a t r) c", c=P)
                else:
                    src = ap.rearrange("a (r c) -> (a r) c", c=P)
                yield 1, at, n, src
                at += n
        V = {"c": 128, "final": 136, "pool": 144, "pre": 152, "post": 160, "glan": 168, "gdnn": 169, "glab": 170, "conv": 172}

        def vcol(name, n=0):
            return vt[:, V[name] + n:V[name] + n + 1]

        def start_act(act):
            act.dma_start(cst[:, :], A["const"][:, 0:400]).then_inc(s_cst, 16)
            for which, at, n, src in rowsrc():
                act.dma_start(rows[at:at + n, which, :], src).then_inc(s_row, 16)
            act.dma_start(wgate[:, :], A["gla_w_gate"][0]).then_inc(s_cst, 16)
            act.dma_start(relb[:, :], A["rel_bias"]).then_inc(s_cst, 16)
            act.dma_start(T["onehot"][:, :], A["onehot"]).then_inc(s_cst, 16)
            act.dma_start(sinks[:, :], A["attn_sinks"].broadcast_to([P, 8])).then_inc(s_cst, 16)
            act.wait_ge(s_vt, 2)
            act.activation(sc[:, :], vt[:, 128:136], ACT.Silu).then_inc(s_sc, 1)
            for ft in range(KT):
                wait_done(act, G_XT + ft)
                act.activation(xT[:, ft, :], acc[:, ft % 2, :], ACT.Copy).then_inc(acc_free[ft % 2], 1)
            for h in range(8):
                act.wait_ge(s_gps, h + 1)
                act.activation(T["G"][:, h, 128:256], att[:, h % 2, 0:128], ACT.Copy).then_inc(s_gsb, 1)
            act.wait_ge(s_gsb, 8)
            act.wait_ge(s_set, 4)
            act.dma_start(gscr.ap().rearrange("(h p m) -> p h m", h=8, p=P), T["G"][:, :, :]).then_inc(s_bias, 16)
            act.preload_act_table_set("natural_log_exp_and_others")
            for kt in range(KT):
                if kt < 2:
                    x_complete(act, G_XT + KT)
                norm_square(act, N0, xT, kt)
                if kt in (3, 5):
                    split_hi(act, (kt - 3) // 2)
            norm_rstd(act, N0)

        def start_dve(dve):
            dve.memset(ones[:, :], 1.0).then_inc(s_set, 1)
            dve.memset(epsc[:, :], EPS).then_inc(s_set, 1)
            dve.memset(T["G"][:, :, 0:128], NEG).then_inc(s_set, 1)
            dve.memset(T["G"][:, :, 256:384], NEG).then_inc(s_set, 1)
            for n, cols in ((0, 128), (1, 92)):
                dve.wait_ge(s_vps, n + 1)
                dve.tensor_copy(vt[:, 128 * n:128 * n + cols], att[:, 2 + n, 0:cols]).then_inc(s_vt, 1)
            dve.wait_ge(s_cst, 80)
            dve.tensor_copy(T["relrep"][:, :, :], relb[:, :].unsqueeze(2).broadcast_to([32, 8, P])).then_inc(s_rel, 1)
            dve.wait_ge(s_sc, 1)
            for piece in range(FIRST):
                ada_mult(dve, piece)
                if piece >= FIRST - KT:
                    norm_add(dve, N0, piece - FIRST + KT)
            for third in range(2):
                ada_mod(dve, third)
            dve.wait_ge(s_ada_mod, 2)
            ada_scale(dve, 0)

        def start_pe(pe):
            pe.wait_ge(s_cst, 80)
            pe.wait_ge(s_row, 16 * 11)
            pe.transpose(att[:, 2, 0:128], rows[:, 0, :], ident).then_inc(s_vps, 1)
            pe.transpose(att[:, 3, 0:92], rows[0:92, 1, :], ident[0:92, 0:92]).then_inc(s_vps, 1)
            pe.wait_ge(s_x, 16 * NT)
            for ft in range(KT):
                acc_ready(pe, G_XT + ft)
                for t in range(NT):
                    mm = pe.transpose(acc[:, ft % 2, t * P:(t + 1) * P], T["xin"][:, t, ft * P:(ft + 1) * P], ident)
                mm.then_inc(acc_done[ft % 2], 1)
            pe.wait_ge(s_rel, 1)
            for h in range(8):
                if h >= 2:
                    pe.wait_ge(s_gsb, h - 1)
                pe.matmul(att[:, h % 2, 0:128], T["relrep"][:, h, :], T["onehot"][:, 128:256], start=True, stop=True).then_inc(s_gps, 1)
            pe.wait_ge(s_set, 1)
            pe.wait_ge(s_vt, 2)
            pe.wait_ge(s_gsb, 8)
            ada_sum(pe, 0)
            norm_sum(pe, N0)
            ada_sum(pe, 1)

        IN_TILES = 19

        def in_pe(pe):
            def seen(n):
                N0.wait_out(pe, n + 1)
            xs = lambda n: (hh[:, n, :], hl[:, n, :])
            g, c = G_IN, C_IN
            product_pair(pe, g, c, xs, seen)
            g += 2; c += 2
            for n in range(2, 10):
                if n == 5:
                    product_t(pe, g, c, 1, 0, 8)
                else:
                    product_f(pe, g, c, 0, range(KT), xs)
                if n == 5:
                    ada_sum(pe, 2)
                g += 1; c += 1
            for n in range(2):
                for u in range(2):
                    product_t(pe, g, c, 2, 4 * u, 4)
                    g += 1
                c += 2
            for n in range(4):
                product_f(pe, g, c, 0, range(KT), xs)
                g += 1; c += 1
            product_f(pe, g, c, 0, range(KT), xs, width=16)

        def in_act(act):
            split_hi(act, 2)
            act.wait_ge(s_bias, 16)
            act.wait_ge(s_mul, 1)
            norm_act(act, N0, a=lambda kt: mul[:, kt:kt + 1], b=lambda kt: modcol(0, 0, kt))
            for c in range(C_IN, C_OUT):
                split_hi(act, c + AHEAD)
                if 14 <= c < 18:
                    g = G_IN + c
                    wait_done(act, g)
                    act.activation(T["gg"][:, c - 14, :], acc[:, g % 2, :], ACT.Silu).then_inc(acc_free[g % 2], 1)

        def in_pool(pool):
            for c in range(AHEAD):
                split_lo(pool, c)
            for c in range(C_IN, C_OUT):
                split_lo(pool, c + AHEAD)

        def in_dve(dve):
            dve.wait_ge(s_mul, 1)
            norm_dve(dve, N0, xT, None, "split")
            dve.wait_ge(s_xmv, X_OUT)
            for n in range(IN_TILES):
                g = G_IN + n
                if 14 <= n < 18:
                    continue
                wait_done(dve, g)
                src = acc[:, g % 2, :]
                if n < 4:
                    dst = T["sq"][:, n, :]
                elif n == 4:
                    dst = T["sk"][:, :]
                elif n == 5:
                    dst, src = T["sv"][:, :, :], src.rearrange("p (t c) -> p t c", t=8)
                elif n < 8:
                    dst = T["gq"][:, n - 6, :]
                elif n < 10:
                    dst = T["gk"][:, n - 8, :]
                elif n < 14:
                    t0, c0 = 4 * (n % 2), 256 * ((n - 10) // 2)
                    dst, src = T["gv"][:, t0:t0 + 4, c0:c0 + 256], src.rearrange("p (t c) -> p t c", t=4)
                else:
                    dst, src = T["cum"][0:16, 0, :], acc[0:16, g % 2, :]
                dve.tensor_copy(dst, src).then_inc(acc_free[g % 2], 1)
                for piece in GATE_MULTS.get(n, ()):
                    ada_mult(dve, piece)
                if n == 5:
                    ada_mod(dve, 2)

        def in_sp(sp):
            for c in range(C_IN + 4, C_OUT + AHEAD + 2):
                load_chunk(sp, c)
                for n in GATE_LOADS.get(c, ()):
                    ada_load(sp, n)
                if c == 4:
                    N0.wait_out(sp, KT)
                    sp.wait_ge(s_xmv, X_OUT)
                    sp.wait_ge(s_bias, 16)
                    src = bass.AP(gscr, 127, [[383, P], [P * 384, 8], [1, 256]])
                    sp.dma_start(T["bias"][:, :, :], src).then_inc(s_bias, 16)

        s_sco, s_scb, s_mx = sem("swa_scores"), sem("swa_scaled"), sem("swa_max")
        s_es, s_pexp, s_pn = sem("swa_exp_sink"), sem("swa_exp"), sem("swa_probs")
        s_ptr, s_pts, s_o, s_oh, s_ol = sem("swa_turned"), sem("swa_turned_sb"), sem("swa_o"), sem("swa_o_hi"), sem("swa_o_lo")
        NB = S // P

        NSU = 2 * NB

        def swa_keys(u):
            return slice(0, 256) if u >= 2 else slice(128, 256)

        def heads4(t, ks):
            return t.rearrange("p (h k) -> p h k", h=4)[:, :, ks]

        def swa_pe(pe):
            def scores(u):
                if u == 0:
                    for g in (4, 5):
                        added(pe, G_IN + g)
                    pe.wait_ge(s_gsb, 8)
                    pe.wait_ge(N0.rs, N0.rs0 + 1)
                    pe.wait_ge(s_ada_mod, 3)
                if u >= 2:
                    pe.wait_ge(s_scb, u - 1)
                n, grp, ks = u // 2, u % 2, swa_keys(u)
                k0 = (n - 1) * P + ks.start
                r = slice(64 * grp, 64 * grp + 64)
                for h in range(4):
                    o = att[:, 2 * (u % 2) + h // 2, (h % 2) * 256 + ks.start:(h % 2) * 256 + 256]
                    mm = pe.matmul(o, T["sq"][r, h, n * P:(n + 1) * P], T["sk"][r, k0:(n + 1) * P], start=True, stop=True)
                mm.then_inc(s_sco, 1)

            def turn(u):
                pe.wait_ge(s_pn, u + 1)
                if u:
                    pe.wait_ge(s_pts, u)
                else:
                    x_complete(pe, G_IN + IN_TILES)
                for h in range(4):
                    for half in ((0, 1) if u >= 2 else (1,)):
                        mm = pe.transpose(acc[:, 0, (2 * h + half) * P:(2 * h + half + 1) * P],
                                          T["ssb"][:, u % 4, h * 256 + half * P:h * 256 + half * P + P], ident)
                mm.then_inc(s_ptr, 1)

            def values(u):
                n, grp = u // 2, u % 2
                if n >= 2:
                    pe.wait_ge(s_ol, n - 1)
                pe.wait_ge(s_pts, u + 1)
                halves = (0, 1) if n else (1,)
                r = slice(64 * grp, 64 * grp + 64)
                for h in range(4):
                    for half in halves:
                        mm = pe.matmul(acc[r, 1, 512 * (n % 2) + h * P:512 * (n % 2) + (h + 1) * P], T["sv"][:, n - 1 + half, r],
                                       T["pT"][:, u % 2, (2 * h + half) * P:(2 * h + half + 1) * P],
                                       start=half == halves[0], stop=half == 1)
                mm.then_inc(s_o, 1)

            for u in range(NSU + 3):
                if u < NSU:
                    scores(u)
                if 2 <= u < NSU + 2:
                    turn(u - 2)
                if u >= 3:
                    values(u - 3)

        def swa_dve(dve):
            s8 = lambda u, k: stat8[:, (u // 2) % 2, k, 4 * (u % 2):4 * (u % 2) + 4]

            def scaled(u):
                ks, hs = swa_keys(u), slice(4 * (u % 2), 4 * (u % 2) + 4)
                dve.wait_ge(s_sco, u + 1)
                if u == 0:
                    dve.wait_ge(s_bias, 32)
                    dve.wait_ge(s_cst, 80)
                if u >= 4:
                    dve.wait_ge(s_ptr, u - 3)
                src = att[:, 2 * (u % 2):2 * (u % 2) + 2, :].rearrange("p b (h k) -> p (b h) k", h=2)[:, :, ks]
                dst = heads4(T["ssb"][:, u % 4, :], ks)
                dve.scalar_tensor_tensor(out=dst, in0=src, scalar=0.125, in1=T["bias"][:, hs, ks],
                                         op0=ALU.mult, op1=ALU.add).then_inc(s_scb, 1)
                dve.wait_ge(s_scb, u + 1)
                dlink(dve.tensor_reduce(s8(u, 0), dst, AX_X, ALU.max))
                dlink(dve.tensor_tensor(s8(u, 0), s8(u, 0), sinks[:, hs], ALU.max))
                dlink(dve.tensor_tensor(s8(u, 1), sinks[:, hs], s8(u, 0), ALU.subtract))
                dve.tensor_scalar(s8(u, 0), s8(u, 0), -1.0, None, ALU.mult).then_inc(s_mx, 1)

            def normal(u):
                ks = swa_keys(u)
                dve.wait_ge(s_pexp, 4 * (u + 1))
                dlink(dve.tensor_tensor(s8(u, 4), s8(u, 2), s8(u, 3), ALU.add))
                dlink(dve.reciprocal(s8(u, 4), s8(u, 4)))
                dst = heads4(T["ssb"][:, u % 4, :], ks)
                dve.tensor_tensor(dst, dst, s8(u, 4).unsqueeze(2).broadcast_to([P, 4, ks.stop - ks.start]), ALU.mult).then_inc(s_pn, 1)

            def out_lo(n):
                dve.wait_ge(s_oh, n + 1)
                t = slice(n * P, n * P + P)
                dve.tensor_tensor(T["osl"][:, :, t], acc[:, 1, 512 * (n % 2):512 * (n % 2) + 512].rearrange("p (h q) -> p h q", h=4),
                                  T["osh"][:, :, t].bitcast(F32), ALU.subtract).then_inc(s_ol, 1)

            for u in range(NSU + 3):
                if u < NSU:
                    scaled(u)
                if 1 <= u < NSU + 1:
                    normal(u - 1)
                if u >= 4 and u % 2 == 0:
                    out_lo(u // 2 - 2)

        def swa_act(act):
            def exps(u):
                ks, (n, grp) = swa_keys(u), divmod(u, 2)
                hs = slice(4 * grp, 4 * grp + 4)
                act.wait_ge(s_mx, u + 1)
                act.activation(stat8[:, n % 2, 3, hs], stat8[:, n % 2, 1, hs], ACT.Exp).then_inc(s_es, 1)
                act.wait_ge(s_es, u + 1)
                for h in range(4):
                    v = T["ssb"][:, u % 4, h * 256 + ks.start:h * 256 + 256]
                    act.activation(v, v, ACT.Exp, bias=stat8[:, n % 2, 0, 4 * grp + h:4 * grp + h + 1],
                                   accum_out=stat8[:, n % 2, 2, 4 * grp + h:4 * grp + h + 1]).then_inc(s_pexp, 1)

            def turned(u):
                act.wait_ge(s_ptr, u + 1)
                if u >= 2:
                    act.wait_ge(s_o, u - 1)
                halves = slice(0, 2) if u >= 2 else slice(1, 2)
                dst = T["pT"][:, u % 2, :].rearrange("p (h k q) -> p h k q", h=4, k=2)[:, :, halves, :]
                src = acc[:, 0, :].rearrange("p (h k q) -> p h k q", h=4, k=2)[:, :, halves, :]
                act.activation(dst, src, ACT.Copy).then_inc(s_pts, 1)

            def out_hi(n):
                act.wait_ge(s_o, 2 * n + 2)
                act.activation(T["osh"][:, :, n * P:(n + 1) * P],
                               acc[:, 1, 512 * (n % 2):512 * (n % 2) + 512].rearrange("p (h q) -> p h q", h=4), ACT.Copy).then_inc(s_oh, 1)

            act.preload_act_table_set("natural_log_exp_and_others")
            for u in range(NSU + 3):
                if u < NSU:
                    exps(u)
                if 2 <= u < NSU + 2:
                    turned(u - 2)
                if u >= 4 and u % 2 == 0:
                    out_hi(u // 2 - 2)

        kt_, keT, Eb, rmask, asb = (T[x] for x in ("kt_", "keT", "Eb", "rmask", "asb"))
        gq, gk, gv, gg, la, cum, st = (T[x] for x in ("gq", "gk", "gv", "gg", "la", "cum", "st"))
        osq, orstd, ofull = (T[x] for x in ("osq", "orstd", "ofull"))
        s_gl, s_ab, s_mn, s_lg, s_ls, s_cum = (sem("gla_" + x) for x in ("logits", "abs", "min", "ln", "logsig", "cum"))
        s_e1, s_e2, s_d3, s_e3, s_qt, s_kt, s_ke, s_dec = (sem("gla_" + x) for x in
            ("exp_b", "exp_nb", "diff", "exp_end", "q", "k", "k_end", "decay"))
        s_ket, s_kes, s_ds, s_st = (sem("gla_" + x) for x in ("k_turned", "k_turned_sb", "dstate", "state"))
        s_ga, s_gas, s_go, s_gsq, s_gst, s_grs, s_gu, s_gf, s_gh, s_glo = (sem("gla_" + x) for x in
            ("scores", "scores_sb", "o", "sq", "stat", "rstd", "u", "full", "hi", "lo"))
        glr = T["cum"]

        def by_parity(t):
            return t[:, :].rearrange("p (n b i) -> p b n i", b=2, i=P)

        def o_banks(t):
            return att[:, 2 * (t % 2):2 * (t % 2) + 2, 0:256].rearrange("p b (n i) -> p b n i", i=P)

        def gla_pe(pe):
            for tile in range(2):
                pe.wait_ge(s_ol, NB)
                for half in range(2):
                    mm = pe.matmul(acc[:, tile, half * 512:half * 512 + 512], wgate[:, tile * P:(tile + 1) * P],
                                   glr[0:16, 0, half * 512:half * 512 + 512], start=True, stop=True)
                mm.then_inc(s_gl, 1)
            for hp in range(2):
                pe.wait_ge(s_ke, hp + 1)
                pe.wait_ge(s_mn, 2)
                for t in range(NT):
                    mm = pe.transpose(acc[:, hp, t * P:(t + 1) * P], gk[:, hp, t * P:(t + 1) * P], ident)
                mm.then_inc(s_ket, 1)
            for c in range(15):
                if c == 0:
                    pe.wait_ge(s_kes, 2)
                if c >= 4:
                    pe.wait_ge(s_st, 2 * (c - 3))
                r = slice(64 * (c % 2), 64 * (c % 2) + 64)
                for h in range(4):
                    mm = pe.matmul(att[64 * (h % 2):64 * (h % 2) + 64, c % 4, (h // 2) * P:(h // 2 + 1) * P],
                                   keT[r, c // 2, h * 64:h * 64 + 64], gv[r, c // 2, h * P:(h + 1) * P], start=True, stop=True)
                mm.then_inc(s_ds, 1)
            def scores(t):
                if t == 0:
                    pe.wait_ge(s_qt, 2)
                    pe.wait_ge(s_kt, 2)
                if t:
                    pe.wait_ge(s_gas, t)
                for h in range(4):
                    r = slice(64 * (h % 2), 64 * (h % 2) + 64)
                    mm = pe.matmul(acc[:, 0, 512 * (h % 2) + (h // 2) * P:512 * (h % 2) + (h // 2 + 1) * P], kt_[r, h // 2, t * P:(t + 1) * P],
                                   gq[r, h // 2, t * P:(t + 1) * P], start=True, stop=True)
                mm.then_inc(s_ga, 1)

            def outputs(t):
                pe.wait_ge(s_gas, t + 1)
                pe.wait_ge(s_st, 30)
                if t >= 2:
                    pe.wait_ge(s_gu, t - 1)
                for h in range(4):
                    r = slice(64 * (h % 2), 64 * (h % 2) + 64)
                    o = att[:, 2 * (t % 2) + h % 2, (h // 2) * P:(h // 2 + 1) * P]
                    mm = pe.matmul(o, gv[:, t, h * P:(h + 1) * P], asb[:, t % 2, h * P:(h + 1) * P], start=True, stop=True,
                                   skip_group_check=True)
                    for c in (2 * t, 2 * t + 1):
                        if c == 0:
                            continue
                        cs = (c % 2) * 64
                        mm = pe.matmul(o[:, cs:cs + 64], st[r, c - 1, h // 2, :],
                                       gq[r, h // 2, c * 64:c * 64 + 64], start=False, stop=True, skip_group_check=True)
                mm.then_inc(s_go, 1)

            def stats(t):
                pe.wait_ge(s_gsq, t + 1)
                if t >= 2:
                    pe.wait_ge(s_grs, 2 * t - 3)
                pe.matmul(acc[:, 1, 512 * (t % 2):512 * (t % 2) + 512], ones[:, :], osq[:, t % 2, :], start=True, stop=True).then_inc(s_gst, 1)

            for t in range(NT + 2):
                if t < NT:
                    scores(t)
                if 1 <= t <= NT:
                    outputs(t - 1)
                if t >= 2:
                    stats(t - 2)

        def gla_act(act):
            for tile in range(2):
                act.wait_ge(s_gl, tile + 1)
                act.activation(Eb[:, tile, :], acc[:, tile, :], ACT.Abs, bias=vcol("glab", tile)).then_inc(s_ab, 1)
            act.preload_act_table_set("natural_log_exp_and_others")
            for tile in range(2):
                act.wait_ge(s_ab, tile + 1)
                alink(act.activation(Eb[:, tile, :], Eb[:, tile, :], ACT.Exp, scale=-1.0))
                act.activation(Eb[:, tile, :], Eb[:, tile, :], ACT.Ln, bias=ones[:, 0:1]).then_inc(s_lg, 1)
            for tile in range(2):
                act.wait_ge(s_cum, tile + 1)
                act.wait_ge(s_ls, tile + 1)
                act.activation(Eb[:, tile, :], cum[:, tile, :], ACT.Exp, scale=1 / 16.0).then_inc(s_e1, 1)
                act.activation(dec[:, tile, :], cum[:, tile, 63::64], ACT.Exp, scale=1 / 16.0).then_inc(s_dec, 1)
                act.wait_ge(s_qt, tile + 1)
                act.activation(Eb[:, tile, :], cum[:, tile, :], ACT.Exp, scale=-1 / 16.0).then_inc(s_e2, 1)
                act.wait_ge(s_d3, tile + 1)
                act.activation(Eb[:, tile, :], la[:, tile, :], ACT.Exp, scale=1 / 16.0).then_inc(s_e3, 1)
            for hp in range(2):
                act.wait_ge(s_ket, hp + 1)
                act.activation(keT[:, :, hp * P:(hp + 1) * P], acc[:, hp, :].rearrange("p (t c) -> p t c", t=NT), ACT.Copy).then_inc(s_kes, 1)
            act.preload_act_table_set("natural_log_exp_and_others")
            for t in range(NT + 2):
                if t < NT:
                    act.wait_ge(s_go, t + 1)
                    if t >= 2:
                        act.wait_ge(s_gst, t - 1)
                    act.activation(by_parity(osq[:, t % 2, :]), o_banks(t), ACT.Square).then_inc(s_gsq, 1)
                if 1 <= t <= NT:
                    u = t - 1
                    act.wait_ge(s_gst, u + 1)
                    if u >= 2:
                        act.wait_ge(s_gf, u - 1)
                    act.activation(orstd[:, u % 2, :], acc[:, 1, 512 * (u % 2):512 * (u % 2) + 512], ACT.Ln, scale=1.0 / P,
                                   bias=epsc[:, 0:1]).then_inc(s_grs, 1)
                    act.wait_ge(s_grs, 2 * u + 1)
                    act.activation(orstd[:, u % 2, :], orstd[:, u % 2, :], ACT.Exp, scale=-0.5).then_inc(s_grs, 1)
                if t >= 2:
                    u = t - 2
                    act.wait_ge(s_gf, u + 1)
                    act.activation(T["ogh"][:, :, u * P:(u + 1) * P], ofull[:, u % 2, :].rearrange("p (h q) -> p h q", h=4), ACT.Copy).then_inc(s_gh, 1)

        def gla_dve(dve):
            dve.memset(rmask[:, :], 1.0).then_inc(s_set, 1)
            dve.memset(asb[:, :, :], 0.0).then_inc(s_set, 1)
            dve.wait_ge(s_set, 6)
            dlink(dve.memset(rmask[:, 0::64], 0.0))
            for tile in range(2):
                dve.wait_ge(s_ab, tile + 1)
                dve.tensor_scalar(la[:, tile, :], acc[:, tile, :], vcol("glab", tile), 0.0, ALU.add, ALU.min).then_inc(s_mn, 1)
            for tile in range(2):
                dve.wait_ge(s_lg, tile + 1)
                dve.wait_ge(s_mn, 2)
                dve.tensor_tensor(la[:, tile, :], la[:, tile, :], Eb[:, tile, :], ALU.subtract).then_inc(s_ls, 1)
                dve.wait_ge(s_ls, tile + 1)
                dve.wait_ge(s_gl, 2)
                dve.tensor_tensor_scan(cum[:, tile, :], rmask[:, :], la[:, tile, :], 0.0, ALU.mult, ALU.add).then_inc(s_cum, 1)
            for tile in range(2):
                dve.wait_ge(s_e1, tile + 1)
                dve.wait_ge(s_cum, 2)
                dve.scalar_tensor_tensor(out=gq[:, tile, :], in0=gq[:, tile, :], scalar=0.125, in1=Eb[:, tile, :],
                                         op0=ALU.mult, op1=ALU.mult).then_inc(s_qt, 1)
                last = cum[:, tile, 63::64].unsqueeze(2).broadcast_to([P, 16, 64])
                dve.wait_ge(s_e2, tile + 1)
                dve.tensor_tensor(kt_[:, tile, :], gk[:, tile, :], Eb[:, tile, :], ALU.mult).then_inc(s_kt, 1)
                dve.wait_ge(s_kt, tile + 1)
                dve.tensor_tensor(la[:, tile, :].rearrange("p (c i) -> p c i", c=16), last,
                                  cum[:, tile, :].rearrange("p (c i) -> p c i", c=16), ALU.subtract).then_inc(s_d3, 1)
                dve.wait_ge(s_e3, tile + 1)
                dve.tensor_tensor(gk[:, tile, :], gk[:, tile, :], Eb[:, tile, :], ALU.mult).then_inc(s_ke, 1)
            dve.wait_ge(s_dec, 2)
            for c in range(15):
                for hp in range(2):
                    dve.wait_ge(s_ds, c + 1)
                    ds = att[:, c % 4, hp * P:(hp + 1) * P]
                    if c == 0:
                        dve.tensor_copy(st[:, 0, hp, :], ds).then_inc(s_st, 1)
                    else:
                        dve.wait_ge(s_st, 2 * c + hp - 1)
                        dve.scalar_tensor_tensor(out=st[:, c, hp, :], in0=st[:, c - 1, hp, :], scalar=dec[:, hp, c:c + 1], in1=ds,
                                                 op0=ALU.mult, op1=ALU.add).then_inc(s_st, 1)
            for t in range(NT + 3):
                if t < NT:
                    dve.wait_ge(s_ga, t + 1)
                    if t >= 2:
                        dve.wait_ge(s_go, t - 1)
                    dve.copy_predicated(by_parity(asb[:, t % 2, :]),
                                        causal.bitcast(U32).unsqueeze(1).unsqueeze(1).broadcast_to([P, 2, 2, P]),
                                        acc[:, 0, :].rearrange("p (b n i) -> p b n i", b=2, i=P)[:, :, 0:2, :]).then_inc(s_gas, 1)
                if 2 <= t < NT + 2:
                    u = t - 2
                    ts = slice(u * P, u * P + P)
                    dve.wait_ge(s_grs, 2 * u + 2)
                    dve.tensor_tensor(by_parity(orstd[:, u % 2, :]), o_banks(u), by_parity(orstd[:, u % 2, :]), ALU.mult).then_inc(s_gu, 1)
                    dve.wait_ge(s_gu, u + 1)
                    if u >= 2:
                        dve.wait_ge(s_glo, u - 1)
                    dve.scalar_tensor_tensor(out=ofull[:, u % 2, :].rearrange("p (h q) -> p h q", h=4),
                                             in0=orstd[:, u % 2, :].rearrange("p (h q) -> p h q", h=4), scalar=vcol("glan"),
                                             in1=gg[:, :, ts], op0=ALU.mult, op1=ALU.mult).then_inc(s_gf, 1)
                if t >= 3:
                    u = t - 3
                    ts = slice(u * P, u * P + P)
                    dve.wait_ge(s_gh, u + 1)
                    dve.tensor_tensor(T["ogl"][:, :, ts], ofull[:, u % 2, :].rearrange("p (h q) -> p h q", h=4),
                                      T["ogh"][:, :, ts].bitcast(F32), ALU.subtract).then_inc(s_glo, 1)


        def out_sp(sp):
            sp.wait_ge(s_glo, NT)
            sp.dma_start(xb[:, :, :].rearrange("p a b -> p (a b)"), xres.ap()).then_inc(s_xmv, 16)
            for n in range(8):
                for j in range(3):
                    ada_load(sp, NADA + 3 * n + j)
                load_chunk(sp, C_OUT + n + AHEAD + 2)

        def out_pe(pe):
            pe.wait_ge(s_glo, NT)
            def xs(n):
                h, l = (T["ogh"], T["ogl"]) if n < 4 else (T["osh"], T["osl"])
                return h[:, n % 4, :], l[:, n % 4, :]
            for n in range(8):
                product_f(pe, G_OUT + n, C_OUT + n, 0, range(KT), xs)
                if n in (2, 5, 7):
                    ada_sum(pe, 3 + n // 3)
            norm_sum(pe, N_mlp0)

        def out_act(act):
            act.preload_act_table_set("natural_log_exp_and_others")
            for n in range(8):
                split_hi(act, C_OUT + n + AHEAD)
                if n:
                    added(act, G_OUT + n - 1)
                    norm_square(act, N_mlp0, xb, n - 1)
            added(act, G_OUT + 7)
            norm_square(act, N_mlp0, xb, 7)
            norm_rstd(act, N_mlp0)

        def out_pool(pool):
            for c in range(C_OUT, C_OUT + 8):
                split_lo(pool, c + AHEAD)

        def add_to_x(dve, g, m, gate, gstep=0, extra=0):
            wait_done(dve, g, gstep)
            dve.scalar_tensor_tensor(out=xb[:, m, :], in0=acc[:, g % 2, :], scalar=gate, in1=xb[:, m, :],
                                     op0=ALU.mult, op1=ALU.add).then_inc(acc_free[g % 2], 1)

        def out_dve(dve):
            dve.wait_ge(s_xmv, X_BACK)
            for n in range(8):
                for k in range(3):
                    piece = NADA + 3 * n + k
                    ada_mult(dve, piece)
                    if piece % 8 == 7:
                        ada_mod(dve, piece // 8)
                add_to_x(dve, G_OUT + n, n, modcol(0, 2, n))
                if n:
                    norm_add(dve, N_mlp0, n - 1)
            norm_add(dve, N_mlp0, 7)
            dve.wait_ge(s_ada_mod, 6)
            ada_scale(dve, 1)

        ah, al, rbuf, sq1 = T["ah"], T["al"], T["rbuf"], T["sq1"]

        s_ah, s_al = sem("hidden_hi"), sem("hidden_lo")

        LAST = NBLK - 1
        ADA_SLOTS = {1: (0, 2), 2: (2, 4), 3: (4, 6), 4: (6, 8), 6: (8, 10), 7: (10, 11), 8: (11, 13), 9: (13, 14), 10: (14, 16)}
        ab2, acc2 = T["ab2"], T["acc2"]

        def later_load(sp, i, r):
            j, n = i - 1, 2 * NADA + r
            sub = 3 if r < 8 else 2
            sp.wait_ge(s_ada_use, n - 3 + 16 * j)
            sp.dma_start(ab2[:, n % 4, :], ada[sub, (r % 8) * P:(r % 8 + 1) * P, bass.ds(j * 1024, 1024)]).then_inc(s_ada_in[n % 4], 16)

        def later_mult(dve, i, r):
            j, n = i - 1, 2 * NADA + r
            kt = r % 8
            dve.wait_ge(s_ada_in[n % 4], 16 * (n // 4 + 1) + 64 * j)
            if kt == 0:
                dve.tensor_scalar(acc2[:, :], ab2[:, n % 4, :], sc[:, 0:1], None, ALU.mult).then_inc(s_ada_use, 1)
            else:
                dve.wait_ge(s_ada_use, n + 16 * j)
                dve.scalar_tensor_tensor(out=acc2[:, :], in0=ab2[:, n % 4, :], scalar=sc[:, kt:kt + 1], in1=acc2[:, :],
                                         op0=ALU.mult, op1=ALU.add).then_inc(s_ada_use, 1)

        def later_sum(pe, i, k):
            third = 6 + k
            pe.wait_ge(s_ada_use, 8 * third + 8 + 16 * (i - 1))
            pe.wait_ge(s_ada_mod, third + 2 * (i - 1))
            for m in range(8):
                mm = pe.matmul(att[:, 3, m:m + 1], acc2[:, m * P:(m + 1) * P], ones[:, 0:1], start=True, stop=True)
            mm.then_inc(s_ada_sum, 1)

        def later_mod(dve, i, k):
            third, c0 = 6 + k, (3 - k) * 24
            dve.wait_ge(s_ada_sum, third + 1 + 2 * (i - 1))
            at = bass.ds((i - 1) * 8 + c0, 8)
            dve.tensor_tensor(mod[:, at], att[:, 3, 0:8], vt[:, at], ALU.add).then_inc(s_ada_mod, 1)

        s_fsq, s_fst = sem("final_sq"), sem("final_stat")

        def final_square(act, kt):
            if kt >= 2:
                act.wait_ge(s_fst, kt - 1)
            act.activation(tb[:, 1 if kt else 0, :], xb[:, kt, :], ACT.Square, scale=vcol("final", kt)).then_inc(s_fsq, 1)

        def final_add(dve, kt):
            if kt:
                dve.wait_ge(s_fsq, kt + 1)
                if kt > 1:
                    dve.wait_ge(s_fst, kt - 1)
                dve.tensor_tensor(tb[:, 0, :], tb[:, 0, :], tb[:, 1, :], ALU.add).then_inc(s_fst, 1)

        def final_sum(pe):
            pe.wait_ge(s_fst, KT - 1)
            for half in range(2):
                mm = pe.matmul(att[:, 2 + half, :], ones[:, :], tb[:, 0, half * 512:half * 512 + 512], start=True, stop=True)
            mm.then_inc(s_fst, 1)

        def mlp_stage(l, cb, gb, sub):
            N, N_next = ((N_mlp0, NP_), (N_mlp1, NF))[l]
            hid0 = l * 4 * NBLK


            def sp_(sp):
                def turn(i, later=False):
                    for k in range(AHEAD + 2, AHEAD + 10):
                        load_chunk(sp, cb + k, i=i + k // 8, step=8 * i)
                        if later:
                            for r in (2 * (k - AHEAD - 2), 2 * (k - AHEAD - 2) + 1):
                                later_load(sp, i, r)
                turn(0)
                if l == 0:
                    N.wait_out(sp, KT)
                    with sp.Fori(1, 4) as i:
                        turn(i, True)
                with sp.Fori(1 if l else 4, LAST) as i:
                    turn(i)
                for k in range(AHEAD + 2, AHEAD + 10):
                    load_chunk(sp, cb + 8 * LAST + k)

            def pe_(pe):
                xs = lambda n: (hh[:, n, :], hl[:, n, :])
                def turn(i, first=False, later=False):
                    step, gstep = 8 * i, 6 * i
                    if first:
                        product_pair(pe, gb, cb, xs, lambda n: N.wait_out(pe, n + 1))
                    for k in range(2 if first else 0, 4):
                        product_f(pe, gb + k, cb + k, 0, range(KT), xs, step=step, gstep=gstep)
                    for m in range(8):
                        product_f(pe, gb + 4 + m, cb + 4 + m // 2, (m % 2) * P, range(4), lambda n: (ah[:, n, :], al[:, n, :]),
                                  step=step, gstep=gstep, on_kt=(lambda n: pe.wait_ge(s_al, hid0 + 4 * i + n + 1)) if m == 0 else None)
                        if later and m == 1:
                            later_sum(pe, i, 0)
                    if later:
                        later_sum(pe, i, 1)
                turn(0, first=True)
                if l == 0:
                    with pe.Fori(1, 4) as i:
                        turn(i, later=True)
                with pe.Fori(1 if l else 4, LAST) as i:
                    turn(i)
                turn(LAST)
                norm_sum(pe, N_next)
                if l:
                    final_sum(pe)

            def act_(act):
                act.wait_ge(s_mul, 4 if l else 2)
                norm_act(act, N, a=lambda kt: mul[:, sub * 8 + kt:sub * 8 + kt + 1], b=lambda kt: modcol(sub, 0, kt))
                def turn(i, first=False, last=False):
                    gstep = 6 * i
                    for k in range(8):
                        split_hi(act, cb + k + AHEAD + (8 * i if last else 0), step=0 if last else 8 * i, gstep=0 if last else gstep)
                        if k < 4:
                            g = gb + k
                            if not (first and k < 2):
                                act.wait_ge(s_al, hid0 + 4 * i + k - 1)
                            wait_done(act, g, gstep)
                            act.activation(rbuf[:, k % 2, :], acc[:, g % 2, :], ACT.Relu).then_inc(acc_free[g % 2], 1)
                            act.wait_ge(acc_free[g % 2], g // 2 + 1 + gstep)
                            act.activation(ah[:, k, :], rbuf[:, k % 2, :], ACT.Square).then_inc(s_ah, 1)
                        if last and k > 4:
                            for m in (2 * k - 10, 2 * k - 9):
                                squares(m)
                def squares(m):
                    added(act, gb + 12 * LAST + 4 + m)
                    norm_square(act, N_next, xb, m)
                    if l:
                        final_square(act, m)
                turn(0, first=True)
                with act.Fori(1, LAST) as i:
                    turn(i)
                turn(LAST, last=True)
                act.preload_act_table_set("natural_log_exp_and_others")
                for m in (6, 7):
                    squares(m)
                norm_rstd(act, N_next)

            def pool_(pool):
                with pool.Fori(0, LAST) as i:
                    for k in range(8):
                        split_lo(pool, cb + k + AHEAD, step=8 * i)
                for k in range(8):
                    split_lo(pool, cb + 8 * LAST + k + AHEAD)

            def dve_(dve):
                norm_dve(dve, N, xb, None, "split")
                def turn(i, first=False, last=False, later=False):
                    gstep = 6 * i
                    for k in range(12):
                        g = gb + k
                        if k < 4:
                            dve.wait_ge(acc_free[g % 2], g // 2 + 1 + gstep)
                            if not first or k or l:
                                dve.wait_ge(s_al, hid0 + 4 * i + k)
                            dlink(dve.tensor_tensor(sq1[:, :], rbuf[:, k % 2, :], rbuf[:, k % 2, :], ALU.mult))
                            dve.wait_ge(s_ah, hid0 + 4 * i + k + 1)
                            dve.tensor_tensor(al[:, k, :], sq1[:, :], ah[:, k, :].bitcast(F32), ALU.subtract).then_inc(s_al, 1)
                        else:
                            add_to_x(dve, g, k - 4, modcol(sub, 2, k - 4), gstep)
                            if last and k > 4:
                                sums(k - 5)
                        if later:
                            if k == 6:
                                later_mod(dve, i, 0)
                            for piece in range(*ADA_SLOTS.get(k, (0, 0))):
                                later_mult(dve, i, piece)
                    if later:
                        later_mod(dve, i, 1)
                def loop(lo, hi, later=False):
                    with dve.Fori(lo, hi) as i:
                        dlink.extra = 4 * i - 4 * lo
                        turn(i, later=later)
                    dlink.extra = 0
                    dlink.n += 4 * (hi - lo - 1)
                turn(0, first=True)
                if l == 0:
                    loop(1, 4, later=True)
                    dve.wait_ge(s_ada_mod, 12)
                    for n in (2, 3):
                        ada_scale(dve, n)
                def sums(m):
                    norm_add(dve, N_next, m)
                    if l:
                        final_add(dve, m)
                loop(1 if l else 4, LAST)
                turn(LAST, last=True)
                sums(7)

            return sp_, act_, pe_, dve_, pool_

        hp = T["hp"]
        s_pw, s_pwh, s_pb = sem("pool_windows"), sem("pool_hi"), sem("pool_ready")
        s_p3 = sem("pool_steps")

        def pool_sp(sp):
            for k in range(2):
                load_chunk(sp, C_PL + k + AHEAD + 2)

        def pool_pe(pe):
            for q in range(2):
                for gi2 in range(2):
                    gi = 2 * q + gi2
                    for mm in range(2):
                        product_f(pe, G_PL + 2 * gi + mm, C_PL + q, mm * P, (2 * gi2, 2 * gi2 + 1),
                                  lambda n: (hh[:, 2 * gi + n, :], hl[:, 2 * gi + n, :]),
                                  on_kt=(lambda n: pe.wait_ge(s_pb, gi + 1)) if mm == 0 else None)
                        if gi:
                            norm_sum_tile(pe, N_mlp1, 2 * gi + mm - 2)
            for kt in (6, 7):
                norm_sum_tile(pe, N_mlp1, kt)

        def pool_act(act):
            act.wait_ge(s_mul, 4)
            norm_act(act, NP_, a=lambda kt: mul[:, 16 + kt:17 + kt], b=lambda kt: modcol(2, 0, kt), dest=hp)
            split_hi(act, C_PL + AHEAD)
            for gi in range(4):
                act.wait_ge(s_pw, gi + 1)
                act.activation(hh[:, 2 * gi:2 * gi + 2, :], wins(gi)[1], ACT.Copy).then_inc(s_pwh, 1)
                if gi == 2:
                    split_hi(act, C_PL + 1 + AHEAD)
                if gi:
                    for m in (2 * gi - 2, 2 * gi - 1):
                        added(act, G_PL + m)
                        norm_square(act, N_mlp1, xb, m, on_pe=True)
            for m in (6, 7):
                added(act, G_PL + m)
                norm_square(act, N_mlp1, xb, m, on_pe=True)
            norm_rstd(act, N_mlp1)

        def wins(gi):
            A, B = T["rbuf"][:, :, :], tb[:, :, :]
            return (A, B) if gi % 2 == 0 else (B, A)

        def window_sums(eng, step, gi, bufs, b_free=None):
            cur = hp[:, 2 * gi:2 * gi + 2, :]
            for r in range(gi + 1):
                sh, dst = 1 << r, bufs[(gi - r + 1) % 2]
                if r == 1 and b_free:
                    b_free()
                step(eng.tensor_tensor(dst[:, :, sh:], cur[:, :, sh:], cur[:, :, 0:S - sh], ALU.add))
                step(eng.tensor_copy(dst[:, :, 0:sh], cur[:, :, 0:sh]))
                cur = dst[:, :, :]
            return cur

        def pool_pool(pool):
            split_lo(pool, C_PL + AHEAD)
            pool.wait_ge(NP_.hi, NP_.hi0 + KT)
            done = [0]
            def step(ins):
                done[0] += 1
                ins.then_inc(s_p3, 1)
                pool.wait_ge(s_p3, done[0])
            window_sums(pool, step, 2, (T["winA"], T["winB"]))
            window_sums(pool, step, 3, (T["winA"], T["winB"]), lambda: pool.wait_ge(s_pw, 3))
            split_lo(pool, C_PL + 1 + AHEAD)

        def pool_dve(dve):
            norm_dve(dve, NP_, xb, None, "plain")
            dlink(dve.tensor_tensor(pgate[:, :], mod[:, 64:72], vt[:, V["pool"]:V["pool"] + 8], ALU.mult))
            dve.wait_ge(NP_.hi, NP_.hi0 + KT)
            for gi in range(4):
                w = 2 << gi
                src = hp[:, 2 * gi:2 * gi + 2, :]
                last, diff = wins(gi)
                if gi < 2:
                    cur = window_sums(dve, dlink, gi, (diff, last))
                else:
                    cur = T["winB"][:, :, :]
                    dve.wait_ge(s_p3, 6 if gi == 2 else 14)
                dlink(dve.tensor_tensor(cur[:, :, 0:w - 1], cur[:, :, 0:w - 1],
                                        rcnt[:, 0:w - 1].unsqueeze(1).broadcast_to([P, 2, w - 1]), ALU.mult))
                dlink(dve.tensor_tensor(diff[:, :, 0:w - 1], cur[:, :, 0:w - 1], src[:, :, 0:w - 1], ALU.subtract))
                dve.scalar_tensor_tensor(out=diff[:, :, w - 1:], in0=cur[:, :, w - 1:], scalar=1.0 / w, in1=src[:, :, w - 1:],
                                         op0=ALU.mult, op1=ALU.subtract).then_inc(s_pw, 1)
                if gi:
                    for m in (2 * gi - 2, 2 * gi - 1):
                        add_to_x(dve, G_PL + m, m, pgate[:, m:m + 1])
                dve.wait_ge(s_pwh, gi + 1)
                dve.tensor_tensor(hl[:, 2 * gi:2 * gi + 2, :], diff[:, :, :], hh[:, 2 * gi:2 * gi + 2, :].bitcast(F32),
                                  ALU.subtract).then_inc(s_pb, 1)
                dve.wait_ge(s_pb, gi + 1)
            for m in (6, 7):
                add_to_x(dve, G_PL + m, m, pgate[:, m:m + 1])

        win2 = A["w_in_2"][0]
        sbq, sbk, sbv = T["sbq"], T["sbk"], T["sbv"]

        fpre = sb("fpre", [P, 8])
        s_frr = sem("final_rstd2")

        def sbin_sp(sp):
            for c in range(C_SB, C_SG):
                if c == C_SB + 2:
                    NF.wait_out(sp, KT)
                    sp.dma_start(xres.ap(), xb[:, :, :].rearrange("p a b -> p (a b)")).then_inc(s_xmv, 16)
                load_chunk(sp, c + AHEAD + 2)

        def sbin_pe(pe):
            xs = lambda k: (hh[:, k, :], hl[:, k, :])
            product_pair(pe, G_SB, C_SB, xs, lambda k: N2.wait_out(pe, k + 1))
            for n in range(2, 7):
                product_f(pe, G_SB + n, C_SB + n, 0, range(KT), xs)
            for u in range(4):
                product_t(pe, G_SB + 7 + u, C_SB + 7 + 2 * (u // 2), 2, 4 * (u % 2), 4)
            product_f(pe, G_SB + 11, C_SB + 11, 0, range(KT), xs)

        def sbin_act(act):
            act.wait_ge(s_frr, 1)
            alink(act.activation(tb[:, 0, :], tb[:, 0, :], ACT.Ln, scale=1.0 / D, bias=epsc[:, 0:1]))
            act.activation(tb[:, 0, :], tb[:, 0, :], ACT.Exp, scale=-0.5).then_inc(s_frr, 1)
            norm_act(act, N2, a=lambda kt: fpre[:, kt:kt + 1])
            for c in range(C_SB, C_SG):
                split_hi(act, c + AHEAD)
                if c - C_SB < 7 or c == C_SG - 1:
                    g = G_SB + c - C_SB
                    n = min(c - C_SB, 7)
                    wait_done(act, g)
                    if n == 0:
                        N2.wait_out(act, KT)
                        NF.wait_out(act, KT)
                    dst = sbq[:, n, :] if n < 4 else sbk[:, n - 4, :]
                    act.activation(dst, acc[:, g % 2, :], ACT.Copy, scale=0.125 if n < 4 else 1.0).then_inc(acc_free[g % 2], 1)

        def sbin_pool(pool):
            for c in range(C_SB, C_SG):
                split_lo(pool, c + AHEAD)

        def sbin_dve(dve):
            dlink(dve.tensor_tensor(fpre[:, :], vt[:, V["final"]:V["final"] + 8], vt[:, V["pre"]:V["pre"] + 8], ALU.mult))
            dve.wait_ge(NF.rs, NF.rs0 + 1)
            dve.wait_ge(s_fst, KT)
            dlink(dve.tensor_tensor(tb[:, 0, :], att[:, 2:4, :].rearrange("p a b -> p (a b)"), rstd[:, :], ALU.mult))
            dve.tensor_tensor(tb[:, 0, :], tb[:, 0, :], rstd[:, :], ALU.mult).then_inc(s_frr, 1)
            dve.wait_ge(s_frr, 2)
            dlink(dve.tensor_tensor(sq1[:, :], tb[:, 0, :], rstd[:, :], ALU.mult))
            norm_dve(dve, N2, xb, None, "split", rs=sq1)
            norm_dve(dve, NF, xb, lambda kt: vcol("final", kt), "inplace")
            dve.wait_ge(s_xmv, X_OUT2)
            for n in range(4):
                g = G_SB + 7 + n
                wait_done(dve, g)
                t0, c0 = 4 * (n % 2), 256 * (n // 2)
                dve.tensor_copy(sbv[:, t0:t0 + 4, c0:c0 + 256], acc[:, g % 2, :].rearrange("p (t c) -> p t c", t=4))\
                   .then_inc(acc_free[g % 2], 1)

        onesb, lowm, vtmp = T["onesb"], T["lowm"], T["vtmp"]
        et, su, aT = T["sb_e"], T["sb_s"], T["sb_aT"]
        s_z, s_ez, s_cl, s_ln, s_sc_, s_arg, s_a, s_am = (sem("sb_" + x) for x in
            ("z", "exp", "clamp", "ln", "suffix", "arg", "a", "a_masked"))
        s_tr, s_trc, s_sbo, s_sboc = (sem("sb_" + x) for x in ("turned", "turned_sb", "o", "o_sb"))
        UNITS = [(n, h) for n in range(NT) for h in range(8)]
        NU = len(UNITS)
        BUFS = 3

        def groups(n):
            return [range(k, min(k + 4, n + 1)) for k in range(0, n + 1, 4)]

        GRP_AT = []
        _n = 0
        for n, h in UNITS:
            GRP_AT.append(_n)
            _n += len(groups(n))
        GRP_AT.append(_n)

        def zps(u, W):
            if u % 3 == 2:
                return acc[:, 0, 0:W]
            return att[:, 2 * (u % 3):2 * (u % 3) + 2, :].rearrange("p b c -> p (b c)")[:, 0:W]

        turned, ops = acc[:, 1, 0:512], acc[:, 1, 512:512 + P]

        def sb_pe(pe):
            x_complete(pe, G_SG)
            def z(u):
                n, h = UNITS[u]
                W = (n + 1) * P
                if u >= 3:
                    pe.wait_ge(s_arg, u - 2)
                r = slice(64 * (h % 2), 64 * (h % 2) + 64)
                for k in range(0, W, 512):
                    w = min(512, W - k)
                    mm = pe.matmul(zps(u, S)[:, k:k + w], sbq[r, h // 2, n * P:(n + 1) * P],
                                   sbk[r, h // 2, k:k + w], start=True, stop=True)
                mm.then_inc(s_z, 1)

            def turn(u, gi):
                n, h = UNITS[u]
                if gi == 0:
                    pe.wait_ge(s_am, u + 1)
                if gi < len(groups(n)):
                    x = GRP_AT[u] + gi
                    if x:
                        pe.wait_ge(s_trc, x)
                    for k in groups(n)[gi]:
                        mm = pe.transpose(turned[:, (k % 4) * P:(k % 4 + 1) * P], su[:, u % BUFS, k * P:(k + 1) * P], ident)
                    mm.then_inc(s_tr, 1)

            def out_(u):
                n, h = UNITS[u]
                r = slice(64 * (h % 2), 64 * (h % 2) + 64)
                if u >= 2 and u % 2 == 0:
                    pe.wait_ge(s_sboc, u // 2)
                for gi, grp in enumerate(groups(n)):
                    pe.wait_ge(s_trc, GRP_AT[u] + gi + 1)
                    for k in grp:
                        mm = pe.matmul(ops[r, :], sbv[:, k, h * 64:h * 64 + 64], aT[:, u % 2, k * P:(k + 1) * P],
                                       start=k == 0, stop=k == n)
                mm.then_inc(s_sbo, 1)

            z(0)
            for u in range(NU + 4):
                if 3 <= u < NU + 3:
                    turn(u - 3, 0)
                if u + 1 < NU:
                    z(u + 1)
                if u >= 4:
                    out_(u - 4)
                if 3 <= u < NU + 3:
                    turn(u - 3, 1)

        def sb_act(act):
            act.preload_act_table_set("natural_log_exp_and_others")
            def first(u):
                W = (UNITS[u][0] + 1) * P
                act.wait_ge(s_z, u + 1)
                if u >= BUFS:
                    act.wait_ge(s_sc_, u - BUFS + 1)
                act.activation(et[:, u % BUFS, 0:W], zps(u, W), ACT.Exp).then_inc(s_ez, 1)
            def second(u):
                W = (UNITS[u][0] + 1) * P
                act.wait_ge(s_cl, u + 1)
                act.activation(et[:, u % BUFS, 0:W], et[:, u % BUFS, 0:W], ACT.Ln, bias=ones[:, 0:1]).then_inc(s_ln, 1)
            def third(u):
                W = (UNITS[u][0] + 1) * P
                act.wait_ge(s_arg, u + 1)
                act.activation(su[:, u % BUFS, 0:W], su[:, u % BUFS, 0:W], ACT.Exp).then_inc(s_a, 1)
            def copies(u, gi):
                n, h = UNITS[u]
                for grp in groups(n)[gi:gi + 1]:
                    x = GRP_AT[u] + gi
                    act.wait_ge(s_tr, x + 1)
                    if u >= 2:
                        act.wait_ge(s_sbo, u - 1)
                    w = len(grp) * P
                    act.activation(aT[:, u % 2, grp[0] * P:grp[0] * P + w], turned[:, 0:w], ACT.Copy).then_inc(s_trc, 1)
            for u in range(NU + 3):
                if u < NU:
                    first(u)
                if 1 <= u < NU + 1:
                    second(u - 1)
                if 2 <= u < NU + 2:
                    third(u - 2)
                if u >= 3:
                    copies(u - 3, 0)
                    copies(u - 3, 1)

        def sb_pool(pool):
            pool.wait_ge(s_xmv, X_OUT2)
            pool.memset(lowm[:, :], 1.0).then_inc(s_p3, 1)
            pool.wait_ge(s_p3, 15)
            pool.affine_select(out=lowm[:, :], in_=lowm[:, :], compare_op=ALU.is_gt, fill=0.0, base=0,
                               pattern=[[-1, P]], channel_multiplier=1).then_inc(s_p3, 1)
            def clamp(u):
                W = (UNITS[u][0] + 1) * P
                pool.wait_ge(s_ez, u + 1)
                pool.tensor_scalar(et[:, u % BUFS, 0:W], et[:, u % BUFS, 0:W], 2.0 ** 60, 0.0, ALU.min, ALU.max).then_inc(s_cl, 1)
            def strictly_before(u):
                pool.wait_ge(s_a, u + 1)
                d = slice(UNITS[u][0] * P, (UNITS[u][0] + 1) * P)
                pool.affine_select(out=su[:, u % BUFS, d], in_=su[:, u % BUFS, d], compare_op=ALU.is_gt, fill=0.0, base=0,
                                   pattern=[[-1, P]], channel_multiplier=1).then_inc(s_am, 1)
            for u in range(NU + 2):
                if u < NU:
                    clamp(u)
                if u >= 2:
                    strictly_before(u - 2)

        def sb_dve(dve):
            def soft(u):
                W = (UNITS[u][0] + 1) * P
                dve.wait_ge(s_ln, u + 1)
                dlink(dve.tensor_tensor(et[:, u % BUFS, 0:W], zps(u, W), et[:, u % BUFS, 0:W], ALU.max))
                dlink(dve.tensor_tensor(et[:, u % BUFS, W - P:W], et[:, u % BUFS, W - P:W], lowm[:, :], ALU.mult))
            def scan(u):
                W = (UNITS[u][0] + 1) * P
                if u >= BUFS:
                    dve.wait_ge(s_tr, GRP_AT[u - BUFS + 1])
                dve.tensor_tensor_scan(su[:, u % BUFS, 0:W][:, ::-1], onesb[:, 0:W], et[:, u % BUFS, 0:W][:, ::-1], 0.0,
                                       ALU.mult, ALU.subtract).then_inc(s_sc_, 1)
                dve.wait_ge(s_sc_, u + 1)
                dve.tensor_tensor(su[:, u % BUFS, 0:W], zps(u, W), su[:, u % BUFS, 0:W], ALU.add).then_inc(s_arg, 1)
            def keep(u):
                n, h = UNITS[u]
                if u % 2:
                    dve.wait_ge(s_sbo, u + 1)
                    dve.tensor_copy(sbq[:, h // 2, n * P:(n + 1) * P], ops).then_inc(s_sboc, 1)
            dlink(dve.memset(onesb[:, :], 1.0))
            dve.wait_ge(s_p3, 16)
            for u in range(1, NU + 4):
                if u <= NU:
                    soft(u - 1)
                    scan(u - 1)
                if u >= 4:
                    keep(u - 4)

        gqF, gkF, gkT, gvT, pad, cv = (T[x] for x in ("gqF", "gkF", "gkT", "gvT", "pad", "cv"))
        sgt = T["sgt"]
        s_sgo = sem("sb_gated")
        s_cv, s_cvd, s_vtr = sem("conv"), sem("conv_silu"), sem("v_turned")
        s_lsq, s_lst, s_lrs, s_ln2, s_ktr, s_kcp = (sem("l2_" + x) for x in ("sq", "stat", "rstd", "out", "k_turned", "k_sb"))
        s_vcp = sem("v_sb")
        s_ab1, s_ab2, s_gx, s_gps2, s_gate, s_dtb = (sem("gates_" + x) for x in
            ("one", "two", "exp", "sums", "ready", "in"))
        s_hmv = sem("h_moved")

        l2bank = lambda x: 0 if x % 2 else 2

        def l2buf(x):
            return sgt[:, x % 3, :] if x % 3 < 2 else vtmp[:, :]

        def gin_sp(sp):
            for c in range(C_SG, C_GG):
                load_chunk(sp, c + AHEAD + 2)
            g = G_AB
            sp.wait_ge(acc_done[g % 2], g // 2 + 1)
            wait_done(sp, G_AB - 1)
            sp.dma_start(hres.ap()[0], hh[:, :, :].bitcast(F32).rearrange("p a b -> p (a b)")).then_inc(s_hmv, 16)
            sp.dma_start(hres.ap()[1], hl[:, :, :].bitcast(F32).rearrange("p a b -> p (a b)")).then_inc(s_hmv, 16)
            sp.wait_ge(s_hmv, 32)

        CONV_ORDER = list(range(8, 12)) + list(range(8))

        def gin_pe(pe):
            xs = lambda k: (hh[:, k, :], hl[:, k, :])
            for n in range(4):
                if n == 0:
                    pe.wait_ge(s_sboc, NU // 2)
                product_f(pe, G_SG + n, C_SG + n, 0, range(KT), xs)
            def turn_v(n):
                pe.wait_ge(s_cvd, n + 1)
                if n:
                    pe.wait_ge(s_vcp, n)
                for t in range(NT):
                    mm = pe.transpose(att[:, t // 4, (t % 4) * P:(t % 4 + 1) * P], vtmp[:, t * P:(t + 1) * P], ident)
                mm.then_inc(s_vtr, 1)
            def l2_sum(x):
                pe.wait_ge(s_lsq, x + 1)
                if x >= 2:
                    pe.wait_ge(s_lrs, 2 * x - 3)
                elif x:
                    pe.wait_ge(s_vcp, 4)
                for half in range(2):
                    mm = pe.matmul(att[:, l2bank(x) + half, :], ones[:, :], l2buf(x)[:, half * 512:half * 512 + 512], start=True, stop=True)
                mm.then_inc(s_lst, 1)
            for n in range(12):
                product_f(pe, G_GD + n, C_GD + n, 0, range(KT), xs)
                if 2 <= n <= 5:
                    turn_v(n - 2)
                if n >= 6:
                    l2_sum(n - 6)
            pe.wait_ge(w_lo, C_AB + 1)
            acc_ready(pe, G_AB)
            for t in range(NT):
                ts = slice(t * P, (t + 1) * P)
                o = acc[:, G_AB % 2, t * 8:t * 8 + 8]
                for kt in range(KT):
                    rh, rl = (w[:, C_AB % SLOTS, kt * 8:kt * 8 + 8] for w in (wh, wl))
                    pe.matmul(o, hh[:, kt, ts], rh, start=kt == 0, stop=False)
                    pe.matmul(o, hh[:, kt, ts], rl, start=False, stop=False)
                    mm = pe.matmul(o, hl[:, kt, ts], rh, start=False, stop=kt == KT - 1)
            mm.then_inc(acc_done[G_AB % 2], 1)
            for x in (6, 7):
                l2_sum(x)
            for x in range(4, 8):
                b = 2 * (x % 2)
                pe.wait_ge(s_ln2, x + 1)
                if x >= 6:
                    pe.wait_ge(s_kcp, x - 5)
                elif x == 4:
                    pe.wait_ge(s_lrs, 15)
                for t in range(NT):
                    mm = pe.transpose(att[:, b + t // 4, (t % 4) * P:(t % 4 + 1) * P], gkF[:, x - 4, t * P:(t + 1) * P], ident)
                mm.then_inc(s_ktr, 1)
            pe.wait_ge(s_ab2, 1)
            pe.matmul(acc[:, 0, 512:544], cst[:, 128:256], gsm[:, 0, :], start=True, stop=True)
            pe.matmul(acc[:, 0, 544:576], T["same"][:, :], gsm[:, 0, :], start=True, stop=True).then_inc(s_gps2, 1)

        def gin_act(act):
            for n in range(4):
                split_hi(act, C_SG + n + AHEAD)
                g = G_SG + n
                wait_done(act, g)
                if n >= 2:
                    act.wait_ge(s_sgo, n - 1)
                act.activation(sgt[:, n % 2, :], acc[:, g % 2, :], ACT.Silu).then_inc(acc_free[g % 2], 1)
            act.dma_start(dtb[:, 0:4], A["dt_bias_2"].broadcast_to([P, 4])).then_inc(s_dtb, 16)
            act.dma_start(dtb[:, 4:8], A["a_log_2"].broadcast_to([P, 4])).then_inc(s_dtb, 16)
            act.dma_start(T["same"][:, :], A["same"]).then_inc(s_dtb, 16)
            def silu(n):
                act.wait_ge(s_cv, n + 1)
                j = CONV_ORDER[n]
                if j >= 8:
                    if n:
                        act.wait_ge(s_vtr, n)
                    dst = vtmp[:, :]
                else:
                    dst = gqF[:, j, :] if j < 4 else gkF[:, j - 4, :]
                act.activation(dst, cv[:, n % 2, :], ACT.Silu).then_inc(s_cvd, 1)
            def copy_v(n):
                act.wait_ge(s_vtr, n + 1)
                act.activation(gvT[:, :, n * P:(n + 1) * P], att[:, 0:2, :].rearrange("p b (t c) -> p (b t) c", c=P), ACT.Copy).then_inc(s_vcp, 1)
            def sq(x):
                src = gqF[:, x, :] if x < 4 else gkF[:, x - 4, :]
                act.wait_ge(s_cvd, x + 5)
                if x >= 3:
                    act.wait_ge(s_ln2, x - 2)
                act.activation(l2buf(x), src, ACT.Square).then_inc(s_lsq, 1)
            def rs(x):
                act.wait_ge(s_lst, x + 1)
                act.activation(l2buf(x), att[:, l2bank(x):l2bank(x) + 2, :].rearrange("p a b -> p (a b)"), ACT.Ln, bias=epsc[:, 0:1]).then_inc(s_lrs, 1)
                act.wait_ge(s_lrs, 2 * x + 1)
                act.activation(l2buf(x), l2buf(x), ACT.Exp, scale=-0.5).then_inc(s_lrs, 1)
            for n in range(15):
                if n < 12:
                    split_hi(act, C_GD + n + AHEAD)
                    g = G_GD + n
                    wait_done(act, g)
                    if n == 0:
                        act.wait_ge(s_sgo, 4)
                        act.wait_ge(s_sboc, NU // 2)
                    if n:
                        act.wait_ge(s_cv, n)
                    act.activation(pad[:, 3:3 + S], acc[:, g % 2, :], ACT.Copy).then_inc(acc_free[g % 2], 1)
                if 1 <= n <= 12:
                    silu(n - 1)
                if 2 <= n <= 5:
                    copy_v(n - 2)
                if n == 12:
                    split_hi(act, C_AB + AHEAD)
                if n >= 7:
                    if n < 12:
                        act.preload_act_table_set("natural_log_exp_and_others")
                    rs(n - 7)
                if n == 12:
                    act.preload_act_table_set("natural_log_exp_and_others")
                    wait_done(act, G_AB)
                    act.activation(gsm[:, 2:4, :].rearrange("p a (t h) -> p t a h", h=4), acc[:, G_AB % 2, 0:64].rearrange("p (t a h) -> p t a h", a=2, h=4), ACT.Copy).then_inc(acc_free[G_AB % 2], 1)
                if 5 <= n <= 12:
                    sq(n - 5)
            for x in range(4, 8):
                act.wait_ge(s_ktr, x - 3)
                act.wait_ge(s_ln2, 8)
                b = 2 * (x % 2)
                act.activation(gkT[:, :, (x - 4) * P:(x - 3) * P], att[:, b:b + 2, :].rearrange("p b (t c) -> p (b t) c", c=P), ACT.Copy).then_inc(s_kcp, 1)
            act.wait_ge(s_ab1, 1)
            act.activation(gsm[:, 4, :], gsm[:, 0, :], ACT.Abs).then_inc(s_gx, 1)
            act.wait_ge(s_gx, 1)
            alink(act.activation(gsm[:, 4, :], gsm[:, 4, :], ACT.Exp, scale=-1.0))
            act.activation(gsm[:, 4, :], gsm[:, 4, :], ACT.Ln, bias=ones[:, 0:1]).then_inc(s_gx, 1)
            act.activation(gsm[:, 3, :], gsm[:, 3, :], ACT.Exp, scale=-1.0).then_inc(s_gx, 1)
            act.activation(dtb[:, 4:8], dtb[:, 4:8], ACT.Exp).then_inc(s_gx, 1)
            act.wait_ge(s_gate, 1)
            act.activation(gsm[:, 5, :], gsm[:, 1, :], ACT.Exp).then_inc(s_gx, 1)
            act.activation(gsm[:, 6, :], gsm[:, 6, :], ACT.Exp).then_inc(s_gx, 1)

        def gin_pool(pool):
            for c in range(C_SG, C_GG):
                split_lo(pool, c + AHEAD)

        def gin_dve(dve):
            for n in range(4):
                g = G_SG + n
                dve.wait_ge(acc_free[g % 2], g // 2 + 1)
                dve.wait_ge(s_sboc, NU // 2)
                dve.tensor_tensor(sbq[:, n, :], sbq[:, n, :], sgt[:, n % 2, :], ALU.mult).then_inc(s_sgo, 1)
            dlink(dve.memset(pad[:, 0:3], 0.0))
            def unit(x):
                dve.wait_ge(s_lrs, 2 * x + 2)
                t = gqF[:, x, :] if x < 4 else gkF[:, x - 4, :]
                dve.scalar_tensor_tensor(out=t, in0=t, scalar=float(P) ** -0.5 if x < 4 else 1.0, in1=l2buf(x),
                                         op0=ALU.mult, op1=ALU.mult).then_inc(s_ln2, 1)
            for n in range(15):
                if n >= 12:
                    unit(n - 7)
                    continue
                j, g = CONV_ORDER[n], G_GD + n
                dve.wait_ge(acc_free[g % 2], g // 2 + 1)
                c = cv[:, n % 2, :]
                if n >= 2:
                    dve.wait_ge(s_cvd, n - 1)
                dlink(dve.tensor_scalar(c, pad[:, 0:S], vcol("conv", j), None, ALU.mult))
                for tap in range(1, 4):
                    ins = dve.scalar_tensor_tensor(out=c, in0=pad[:, tap:tap + S], scalar=vcol("conv", tap * 12 + j), in1=c, op0=ALU.mult, op1=ALU.add)
                    if tap < 3:
                        dlink(ins)
                    else:
                        ins.then_inc(s_cv, 1)
                if n >= 7:
                    unit(n - 7)
            bc = lambda ap: ap.unsqueeze(1).broadcast_to([P, NT, 4])
            v3 = lambda k: gsm[:, k, :].rearrange("p (t h) -> p t h", h=4)
            dve.wait_ge(acc_free[G_AB % 2], G_AB // 2 + 1)
            dve.wait_ge(s_dtb, 48)
            dve.tensor_tensor(v3(0), v3(2), bc(dtb[:, 0:4]), ALU.add).then_inc(s_ab1, 1)
            dve.wait_ge(s_gx, 4)
            dlink(dve.scalar_tensor_tensor(out=gsm[:, 0, :], in0=gsm[:, 0, :], scalar=0.0, in1=gsm[:, 4, :], op0=ALU.max, op1=ALU.add))
            dlink(dve.tensor_tensor(v3(0), v3(0), bc(dtb[:, 4:8]), ALU.mult))
            dlink(dve.tensor_scalar(gsm[:, 3, :], gsm[:, 3, :], 1.0, None, ALU.add))
            dlink(dve.reciprocal(gsm[:, 3, :], gsm[:, 3, :]))
            dve.tensor_scalar(gsm[:, 0, :], gsm[:, 0, :], -1.0, None, ALU.mult).then_inc(s_ab2, 1)
            dve.wait_ge(s_gps2, 1)
            dlink(dve.tensor_copy(gsm[:, 1, :], acc[:, 0, 512:544]))
            dve.tensor_tensor(gsm[:, 6, :], acc[:, 0, 544:576], gsm[:, 1, :], ALU.subtract).then_inc(s_gate, 1)
            dve.wait_ge(s_gx, 6)
            dve.tensor_tensor(gsm[:, 7, :], gsm[:, 3, :], gsm[:, 5, :], ALU.mult).then_inc(s_gate, 1)

        dgG, dgB, Dm, U, Us, X, Y, W1, vb, kb, vn, In, kd, wT, qe, Sg, lvl, decg = (T["g_" + x] for x in (
            "dgG", "dgB", "D", "U", "Us", "X", "Y", "W1", "vb", "kb", "vn", "I", "kd", "wT", "qe", "S", "lvl", "dec"))
        (s_dg, s_vkk, s_pp, s_dt, s_de, s_qe, s_dm, s_I, s_U, s_us, s_y, s_xx, s_x1, s_xt, s_la, s_lb, s_w1, s_wt, s_v,
         s_wts, s_r1, s_vn, s_r2, s_S, s_r3, s_of, s_lvl) = (sem("gdn_" + x) for x in (
             "diag", "scaled", "prep", "diff", "exp", "q_decayed", "decay_masked", "intra", "u", "u_masked", "y", "x", "x1",
             "x1_turned", "lx", "xlx", "lx_sb", "w_t", "v", "w_t_sb", "from_state", "v_new", "dstate", "state", "o", "o_sb", "levels"))
        bank = lambda n: acc[:, n // 2, (n % 2) * 512:(n % 2) * 512 + 512]
        hd = lambda t, h: t[:, h * P:(h + 1) * P]
        h4 = lambda t: t.rearrange("p (h i) -> p h i", h=4)
        bc4 = lambda t: t.unsqueeze(1).broadcast_to([P, 4, P])
        col4 = lambda k, p: gsm[:, k, 4 * p:4 * p + 4].unsqueeze(2).broadcast_to([P, 4, P])

        hf2 = lambda t, f: t[:, 256 * f:256 * f + 256]
        la_at = lambda p, n, f: 10 * p + 2 * n - 1 + f
        y_at = lambda p, n, f: 12 * p + (2 * n + 1 + f if n else 2)
        x_at = lambda p, n, f: 8 * p + 2 * n - 1 + f
        la_bank = lambda f: bank(3 * f)

        def gdn_plan():
            for p in range(NT + 1):
                q = p - 1
                here, before = p < NT, p > 0
                if here:
                    yield "prep", p, 0
                if before:
                    yield "R1", q, 0
                if here:
                    yield "X", p, 0
                    yield "La", p, 1
                if before:
                    yield "R2", q, 0
                if here:
                    yield "Lb", p, 1
                    yield "La", p, 2
                if before:
                    yield "R1", q, 1
                if here:
                    yield "Lb", p, 2
                    yield "La", p, 3
                if before:
                    yield "R2", q, 1
                if here:
                    yield "Lb", p, 3
                    yield "La", p, 4
                if before:
                    yield "R3", q, 0
                if here:
                    yield "Lb", p, 4
                    yield "La", p, 5
                    yield "Lb", p, 5
                    yield "fin", p, 0

        def gdn_sp(sp):
            sp.wait_ge(s_ln2, 8)
            sp.dma_start(lvl[:, :], A["const"][:, 400:1168]).then_inc(s_lvl, 16)

        def gdn_pe(pe):
            for what, p, n in gdn_plan():
                ps = slice(p * P, (p + 1) * P)
                if what == "prep":
                    if p == 0:
                        pe.wait_ge(s_gate, 1)
                    else:
                        pe.wait_ge(s_w1, 10 * p)
                        pe.wait_ge(s_xx, 8 * p)
                    pe.wait_ge(s_dg, 2 * p + 2)
                    pe.matmul(bank(0), ones[:, :], dgG[:, :], start=True, stop=True).then_inc(s_pp, 1)
                    pe.matmul(bank(1), ones[:, :], dgB[:, :], start=True, stop=True).then_inc(s_pp, 1)
                    if p:
                        pe.wait_ge(s_y, 12 * p)
                        pe.wait_ge(s_wts, p)
                    for h in range(4):
                        mm = pe.matmul(hd(bank(2), h), gkF[:, h, ps], gkF[:, h, ps], start=True, stop=True)
                    mm.then_inc(s_pp, 1)
                    for h in range(4):
                        mm = pe.matmul(hd(bank(3), h), gkF[:, h, ps], gqF[:, h, ps], start=True, stop=True)
                    mm.then_inc(s_pp, 1)
                elif what == "X":
                    pe.wait_ge(s_y, 12 * p + 2)
                    pe.wait_ge(s_de, 3 * p + 3)
                    for h in range(4):
                        mm = pe.transpose(hd(bank(0), h), hd(Y, h), ident)
                    mm.then_inc(s_xt, 1)
                elif what == "La":
                    for f in range(2):
                        if n == 1:
                            pe.wait_ge(s_x1, p + 1)
                            pe.wait_ge(s_I, p + 1)
                        else:
                            pe.wait_ge(s_xx, x_at(p, n - 1, f))
                        pe.wait_ge(s_us, 6 * p + n + 1)
                        for h in range(2):
                            mm = pe.matmul(hd(la_bank(f), h), hd(Us[:, n % 2, :], 2 * f + h), hd(X, 2 * f + h), start=True, stop=True)
                        mm.then_inc(s_la, 1)
                elif what == "Lb":
                    for f in range(2):
                        pe.wait_ge(s_w1, la_at(p, n, f))
                        pe.wait_ge(s_y, y_at(p, n - 1, f))
                        if n < 5:
                            for h in range(2):
                                pe.matmul(hd(bank(1 + f), h), hd(Y, 2 * f + h), hd(W1, 2 * f + h), start=True, stop=True)
                        for h in range(2):
                            mm = pe.matmul(hd(bank(1 + f), 2 + h), hd(W1, 2 * f + h), hd(Y, 2 * f + h), start=True, stop=True)
                        mm.then_inc(s_lb, 1)
                elif what == "fin":
                    pe.wait_ge(s_y, 12 * p + 12)
                    pe.wait_ge(s_vkk, 3 * p + 3)
                    pe.wait_ge(s_I, p + 1)
                    for h in range(4):
                        mm = pe.matmul(hd(bank(3), h), hd(kb, h), hd(Y, h), start=True, stop=True)
                    mm.then_inc(s_wt, 1)
                    if p >= 2:
                        pe.wait_ge(s_vn, 2 * p - 2)
                    for h in range(4):
                        mm = pe.matmul(hd(att[:, p % 2, :], h), hd(Y, h), hd(vb, h), start=h == 0, stop=True, skip_group_check=True)
                    mm.then_inc(s_v, 1)
                elif what == "R1":
                    if 2 * p + n:
                        pe.wait_ge(s_S, 2 * p + n)
                        if n == 0:
                            pe.wait_ge(s_of, p)
                    pe.wait_ge(s_wts, p + 1)
                    pe.wait_ge(s_qe, p + 1)
                    r = slice(64 * n, 64 * n + 64)
                    if 2 * p + n == 0:
                        pe.matmul(att[0:64, 0, 0:2], zero[:, :], ones[:, 0:2], start=False, stop=True, skip_group_check=True).then_inc(s_r1, 1)
                        continue
                    for h in range(4):
                        mm = pe.matmul(hd(att[r, p % 2, :], h), wT[:, p % 2, h * P + 64 * n:h * P + 64 * n + 64], Sg[:, h, :],
                                       start=False, stop=True, skip_group_check=True)
                    mm.then_inc(s_r1, 1)
                    for h in range(4):
                        c = h * P + 64 * n
                        pe.matmul(att[:, 2, c:c + 64], Sg[:, h, :], qe[:, p % 2, c:c + 64],
                                  start=h == 0 and (n == 0 or p == 0), stop=True, skip_group_check=True)
                elif what == "R2":
                    pe.wait_ge(s_vn, 2 * p + n + 1)
                    r = slice(64 * n, 64 * n + 64)
                    for h in range(4):
                        mm = pe.matmul(hd(att[:, 3, :], h), kd[r, p % 2, h * P:(h + 1) * P], vn[r, h * P:(h + 1) * P], start=True, stop=True)
                    mm.then_inc(s_r2, 1)
                elif what == "R3":
                    for h in range(4):
                        mm = pe.matmul(hd(att[:, 2, :], h), hd(vn, h), hd(In[:, p % 2, :], h), start=False, stop=True, skip_group_check=True)
                    mm.then_inc(s_r3, 1)

        def gdn_act(act):
            for what, p, n in gdn_plan():
                if what == "prep":
                    act.wait_ge(s_dt, p + 1)
                    act.activation(Dm[:, :], Dm[:, :], ACT.Exp).then_inc(s_de, 1)
                    if p >= 2:
                        act.wait_ge(s_r3, p - 1)
                    act.activation(qe[:, p % 2, :], bank(0), ACT.Exp).then_inc(s_de, 1)
                    if p >= 2:
                        act.wait_ge(s_S, 2 * p - 2)
                    act.activation(decg[:, p % 2, :, :], h4(bank(0))[:, :, 63::64], ACT.Exp).then_inc(s_de, 1)
                elif what == "X":
                    act.wait_ge(s_xt, p + 1)
                    act.activation(X[:, :], bank(0), ACT.Copy).then_inc(s_x1, 1)
                elif what == "La":
                    for f in range(2):
                        act.wait_ge(s_la, la_at(p, n, f))
                        if n == 1 and p:
                            act.wait_ge(s_lb, 10 * p)
                        act.activation(hf2(W1, f), hf2(la_bank(f), 0), ACT.Copy).then_inc(s_w1, 1)
                elif what == "fin":
                    act.wait_ge(s_wt, p + 1)
                    act.activation(wT[:, p % 2, :], bank(3), ACT.Copy, scale=-1.0).then_inc(s_wts, 1)
                elif what == "R1":
                    act.wait_ge(s_r1, 2 * p + n + 1)
                    act.wait_ge(s_v, p + 1)
                    if n == 0 and p:
                        act.wait_ge(s_r3, p)
                    r = slice(64 * n, 64 * n + 64)
                    act.activation(vn[r, :], att[r, p % 2, :], ACT.Copy).then_inc(s_vn, 1)
                elif what == "R3":
                    act.wait_ge(s_r3, p + 1)
                    act.activation(gqF[:, :, p * P:(p + 1) * P], h4(att[:, 2, :]), ACT.Copy).then_inc(s_of, 1)

        def gdn_pool(pool):
            pool.wait_ge(s_ln2, 8)
            pool.wait_ge(s_hmv, 32)
            pool.wait_ge(s_gate, 2)
            pool.wait_ge(s_lvl, 16)
            for what, p, n in gdn_plan():
                if what == "prep":
                    if p:
                        pool.wait_ge(s_pp, 4 * p)
                    pool.tensor_tensor(h4(dgG[:, :]), bc4(ident), col4(1, p), ALU.mult).then_inc(s_dg, 1)
                    pool.tensor_tensor(h4(dgB[:, :]), bc4(ident), col4(3, p), ALU.mult).then_inc(s_dg, 1)
                    pool.wait_ge(s_de, 3 * p + 1)
                    pool.tensor_tensor(h4(Dm[:, :]), h4(Dm[:, :]), bc4(causal), ALU.mult).then_inc(s_dm, 1)
                    pool.wait_ge(s_U, p + 1)
                    if p:
                        pool.wait_ge(s_la, 10 * p)
                    for k in range(2):
                        pool.tensor_tensor(h4(Us[:, k, :]), h4(U[:, :]), bc4(lvl[:, k * P:(k + 1) * P]), ALU.mult).then_inc(s_us, 1)
                elif what == "La":
                    k = n + 1
                    if k <= 5:
                        if k == 2:
                            pool.wait_ge(s_y, 12 * p + 2)
                        else:
                            pool.wait_ge(s_la, la_at(p, k - 2, 1))
                        pool.tensor_tensor(h4(Us[:, k % 2, :]), h4(U[:, :]), bc4(lvl[:, k * P:(k + 1) * P]), ALU.mult).then_inc(s_us, 1)
                    if n == 1:
                        if p:
                            pool.wait_ge(s_v, p)
                        pool.tensor_tensor(h4(vb[:, :]), h4(gvT[:, p, :]), col4(3, p), ALU.mult).then_inc(s_vkk, 1)
                    if n == 2:
                        pool.tensor_tensor(h4(kb[:, :]), h4(gkT[:, p, :]), col4(7, p), ALU.mult).then_inc(s_vkk, 1)
                    if n == 3:
                        if p >= 2:
                            pool.wait_ge(s_r2, 2 * p - 2)
                        pool.tensor_tensor(h4(kd[:, p % 2, :]), h4(gkT[:, p, :]), col4(6, p), ALU.mult).then_inc(s_vkk, 1)

        def gdn_dve(dve):
            dve.memset(zero[:, :], 0.0).then_inc(s_set, 1)
            for what, p, n in gdn_plan():
                ps = slice(p * P, (p + 1) * P)
                if what == "prep":
                    if p == 0:
                        dve.wait_ge(s_hmv, 32)
                        dve.wait_ge(s_gate, 2)
                    else:
                        dve.wait_ge(s_U, p)
                        dve.wait_ge(s_us, 6 * p)
                    dve.wait_ge(s_pp, 4 * p + 1)
                    for h in range(4):
                        ins = dve.tensor_scalar(hd(Dm, h), hd(bank(0), h), gsm[:, 1, 4 * p + h:4 * p + h + 1], 0.0, ALU.subtract, ALU.min)
                    ins.then_inc(s_dt, 1)
                    dve.wait_ge(s_dm, p + 1)
                    dve.wait_ge(s_pp, 4 * p + 4)
                    if p >= 2:
                        dve.wait_ge(s_r3, p - 1)
                    dlink(dve.tensor_tensor(U[:, :], bank(2), Dm[:, :], ALU.mult))
                    dve.tensor_tensor(U[:, :], U[:, :], bank(1), ALU.mult).then_inc(s_U, 1)
                    dve.tensor_tensor(In[:, p % 2, :], bank(3), Dm[:, :], ALU.mult).then_inc(s_I, 1)
                    dve.wait_ge(s_de, 3 * p + 2)
                    dve.tensor_tensor(h4(qe[:, p % 2, :]), gqF[:, :, ps], h4(qe[:, p % 2, :]), ALU.mult).then_inc(s_qe, 1)
                    dve.wait_ge(s_us, 6 * p + 1)
                    if p:
                        dve.wait_ge(s_v, p)
                    dve.tensor_tensor(h4(Y[:, :]), bc4(ident), h4(Us[:, 0, :]), ALU.subtract).then_inc(s_y, 2)
                elif what == "Lb":
                    for f in range(2):
                        dve.wait_ge(s_lb, la_at(p, n, f))
                        if n < 5:
                            dve.tensor_tensor(hf2(X, f), hf2(X, f), hf2(bank(1 + f), 0), ALU.subtract).then_inc(s_xx, 1)
                        dve.tensor_tensor(hf2(Y, f), hf2(Y, f), hf2(bank(1 + f), 1), ALU.subtract).then_inc(s_y, 1)
                elif what == "R2":
                    dve.wait_ge(s_r2, 2 * p + n + 1)
                    if p + n == 0:
                        dve.tensor_copy(Sg[:, :, :], h4(att[:, 3, :])).then_inc(s_S, 1)
                    else:
                        dve.wait_ge(s_S, 2 * p + n)
                        dve.wait_ge(s_de, 3 * p + 3)
                        for h in range(4):
                            ins = dve.scalar_tensor_tensor(out=Sg[:, h, :], in0=Sg[:, h, :], scalar=decg[:, p % 2, h, n:n + 1],
                                                           in1=hd(att[:, 3, :], h), op0=ALU.mult, op1=ALU.add)
                        ins.then_inc(s_S, 1)

        rb, sg2 = T["rb"], T["sg2"]
        og2h, og2l, os2h, os2l, mrg, mt6 = (T[x] for x in ("og2h", "og2l", "os2h", "os2l", "mrg", "mt6"))
        s_osq, s_ost, s_ors, s_ond = (sem("onorm_" + x) for x in ("sq", "stat", "rstd", "out"))
        s_gf2, s_gh2, s_gl2, s_sh2, s_sl2 = (sem("merge_" + x) for x in ("gated", "og_hi", "og_lo", "os_hi", "os_lo"))
        s_m2, s_mh, s_ml = (sem("merge_" + x) for x in ("sum", "hi", "lo"))

        def mg_sp(sp):
            sp.wait_ge(s_of, NT)
            sp.wait_ge(s_S, 2 * NT)
            sp.dma_start(hh[:, :, :].bitcast(F32).rearrange("p a b -> p (a b)"), hres.ap()[0]).then_inc(s_hmv, 16)
            sp.dma_start(hl[:, :, :].bitcast(F32).rearrange("p a b -> p (a b)"), hres.ap()[1]).then_inc(s_hmv, 16)
            for c in range(C_GG, C_O2):
                load_chunk(sp, c + AHEAD + 2)

        def mg_pe(pe):
            for x in range(4):
                pe.wait_ge(s_osq, x + 1)
                if x:
                    pe.wait_ge(s_ors, 2 * x - 1)
                for half in range(2):
                    mm = pe.matmul(att[:, half, :], ones[:, :], rb[:, x % 2, half * 512:half * 512 + 512], start=True, stop=True)
                mm.then_inc(s_ost, 1)
            pe.wait_ge(s_hmv, 64)
            xs = lambda k: (hh[:, k, :], hl[:, k, :])
            for n in range(4):
                product_f(pe, G_GG + n, C_GG + n, 0, range(KT), xs)
            osx = lambda k: (os2h[:, k, :], os2l[:, k, :])
            ogx = lambda k: (og2h[:, k, :], og2l[:, k, :])
            g, c = G_MG, C_MG
            for m in range(0, 8, 2):
                for br, src, ready in ((0, osx, s_sl2), (1, ogx, s_gl2)):
                    product_f(pe, g, c, 0, range(KT), xs)
                    if m == 0:
                        pe.wait_ge(ready, 4)
                    product_f(pe, g + 1, c + 1, 0, range(4), src)
                    product_f(pe, g + 2, c + 2, 0, range(KT), xs)
                    product_f(pe, g + 3, c + 1, P, range(4), src)
                    g += 4; c += 3

        def mg_act(act):
            act.wait_ge(s_of, NT)
            act.wait_ge(s_S, 2 * NT)
            for x in range(5):
                if x < 4:
                    if x >= 2:
                        act.wait_ge(s_ond, x - 1)
                    act.activation(rb[:, x % 2, :], gqF[:, x, :], ACT.Square).then_inc(s_osq, 1)
                if x:
                    act.wait_ge(s_ost, x)
                    act.activation(rb[:, (x - 1) % 2, :], att[:, 0:2, :].rearrange("p a b -> p (a b)"), ACT.Ln, scale=1.0 / P, bias=epsc[:, 0:1]).then_inc(s_ors, 1)
                    act.wait_ge(s_ors, 2 * x - 1)
                    act.activation(rb[:, (x - 1) % 2, :], rb[:, (x - 1) % 2, :], ACT.Exp, scale=-0.5).then_inc(s_ors, 1)
            for n in range(4):
                split_hi(act, C_GG + n + AHEAD)
                g = G_GG + n
                wait_done(act, g)
                if n >= 2:
                    act.wait_ge(s_gf2, n - 1)
                act.activation(sg2[:, n % 2, :], acc[:, g % 2, :], ACT.Silu).then_inc(acc_free[g % 2], 1)
                act.wait_ge(s_gf2, n + 1)
                act.activation(og2h[:, n, :], gqF[:, n, :], ACT.Copy).then_inc(s_gh2, 1)
            act.wait_ge(s_gl2, 4)
            for n in range(4):
                act.activation(os2h[:, n, :], sbq[:, n, :], ACT.Copy).then_inc(s_sh2, 1)
            g, c = G_MG, C_MG
            for m in range(0, 8, 2):
                for br in range(2):
                    for k in range(3):
                        split_hi(act, c + k + AHEAD)
                        if k != 1:
                            gg_, mm = (g, m) if k == 0 else (g + 2, m + 1)
                            wait_done(act, gg_)
                            if m == 0 and k == 0 and br == 0:
                                act.wait_ge(s_sl2, 4)
                            dst = mrg[:, mm, :] if br == 0 else (mrg[:, mm + 2, :] if m < 6 else mt6[:, mm - 6, :])
                            if br == 0 and m:
                                act.wait_ge(s_m2, mm - 1)
                            act.activation(dst, acc[:, gg_ % 2, :], ACT.Sigmoid).then_inc(acc_free[gg_ % 2], 1)
                    g += 4; c += 3
            for m in range(8):
                act.wait_ge(s_m2, m + 1)
                x_complete(act, G_O2)
                act.activation(hh[:, m, :], mrg[:, m, :], ACT.Copy).then_inc(s_mh, 1)

        def mg_pool(pool):
            for c in range(C_GG, C_O2):
                split_lo(pool, c + AHEAD)

        def mg_dve(dve):
            for x in range(4):
                dve.wait_ge(s_ors, 2 * x + 2)
                dve.scalar_tensor_tensor(out=gqF[:, x, :], in0=gqF[:, x, :], scalar=vcol("gdnn"), in1=rb[:, x % 2, :],
                                         op0=ALU.mult, op1=ALU.mult).then_inc(s_ond, 1)
            for n in range(4):
                g = G_GG + n
                dve.wait_ge(acc_free[g % 2], g // 2 + 1)
                dve.wait_ge(s_ond, n + 1)
                dve.tensor_tensor(gqF[:, n, :], gqF[:, n, :], sg2[:, n % 2, :], ALU.mult).then_inc(s_gf2, 1)
                dve.wait_ge(s_gh2, n + 1)
                dve.tensor_tensor(og2l[:, n, :], gqF[:, n, :], og2h[:, n, :].bitcast(F32), ALU.subtract).then_inc(s_gl2, 1)
            for n in range(4):
                dve.wait_ge(s_sh2, n + 1)
                dve.tensor_tensor(os2l[:, n, :], sbq[:, n, :], os2h[:, n, :].bitcast(F32), ALU.subtract).then_inc(s_sl2, 1)
            g = G_MG
            for m in range(0, 8, 2):
                for br in range(2):
                    for k in range(2):
                        mm = m + k
                        gs, gb = g + 2 * k, g + 2 * k + 1
                        dst = mrg[:, mm, :] if br == 0 else (mrg[:, mm + 2, :] if m < 6 else mt6[:, mm - 6, :])
                        dve.wait_ge(acc_free[gs % 2], gs // 2 + 1)
                        wait_done(dve, gb)
                        dve.tensor_tensor(dst, dst, acc[:, gb % 2, :], ALU.mult).then_inc(acc_free[gb % 2], 1)
                        if br:
                            dve.wait_ge(acc_free[gb % 2], gb // 2 + 1)
                            dve.tensor_tensor(mrg[:, mm, :], mrg[:, mm, :], dst, ALU.add).then_inc(s_m2, 1)
                    g += 4
            for m in range(8):
                dve.wait_ge(s_mh, m + 1)
                dve.tensor_tensor(hl[:, m, :], mrg[:, m, :], hh[:, m, :].bitcast(F32), ALU.subtract).then_inc(s_ml, 1)

        yF, x5, outb = T["yF"], T["x5"], T["outb"]
        s_ya, s_ot, s_oc2, s_out = sem("y_added"), sem("out_turned"), sem("out_sb"), sem("out")

        def end_sp(sp):
            for c in range(C_O2, C_END):
                load_chunk(sp, c + AHEAD + 2)
            sp.wait_ge(s_ml, 8)
            sp.dma_start(x5[:, :, :].rearrange("p a b -> p (a b)"), xres.ap()).then_inc(s_xmv, 16)
            for t in range(NT):
                sp.wait_ge(s_oc2, t + 1)
                sp.dma_start(out[0, t * P:(t + 1) * P, :], outb[:, t, :]).then_inc(s_out, 16)
            sp.wait_ge(s_out, 16 * NT)

        def end_pe(pe):
            for n in range(8):
                product_f(pe, G_O2 + n, C_O2 + n, 0, range(KT), lambda k: (hh[:, k, :], hl[:, k, :]),
                          on_kt=(lambda k: pe.wait_ge(s_ml, k + 1)) if n == 0 else None)
            norm_sum(pe, NY)
            for t in range(NT):
                if t >= 2:
                    pe.wait_ge(s_oc2, t - 1)
                for ft in range(KT):
                    if t % 4 == 0:
                        pe.wait_ge(s_ya, 2 * t + ft + 1)
                    mm = pe.transpose(acc[:, t % 2, ft * P:(ft + 1) * P], yF[:, ft, t * P:(t + 1) * P], ident)
                mm.then_inc(s_ot, 1)

        def end_act(act):
            act.preload_act_table_set("natural_log_exp_and_others")
            for n in range(8):
                split_hi(act, C_O2 + n + AHEAD)
                wait_done(act, G_O2 + n)
                act.activation(yF[:, n, :], acc[:, (G_O2 + n) % 2, :], ACT.Copy).then_inc(acc_free[(G_O2 + n) % 2], 1)
                added(act, G_O2 + n)
                norm_square(act, NY, yF, n)
            norm_rstd(act, NY)
            for t in range(NT):
                act.wait_ge(s_ot, t + 1)
                act.activation(outb[:, t, :], acc[:, t % 2, :], ACT.Copy).then_inc(s_oc2, 1)

        def end_pool(pool):
            for n in range(8):
                split_lo(pool, C_O2 + n + AHEAD)

        def end_dve(dve):
            for kt in range(KT):
                norm_add(dve, NY, kt)
            dve.wait_ge(s_xmv, X_BACK2)
            dve.wait_ge(NY.rs, NY.rs0 + 1)
            for half in range(2):
                ts = slice(512 * half, 512 * half + 512)
                for kt in range(KT):
                    dve.scalar_tensor_tensor(out=yF[:, kt, ts], in0=yF[:, kt, ts], scalar=vcol("post", kt), in1=rstd[:, ts],
                                             op0=ALU.mult, op1=ALU.mult).then_inc(NY.out, 1)
                for kt in range(KT):
                    NY.wait_out(dve, 8 * half + kt + 1)
                    dve.tensor_tensor(yF[:, kt, ts], yF[:, kt, ts], x5[:, kt, ts], ALU.add).then_inc(s_ya, 1)

        stages = {"start": (start_sp, start_act, start_pe, start_dve, None),
                  "in": (in_sp, in_act, in_pe, in_dve, in_pool),
                  "swa": (None, swa_act, swa_pe, swa_dve, None),
                  "gla": (None, gla_act, gla_pe, gla_dve, None),
                  "out": (out_sp, out_act, out_pe, out_dve, out_pool),
                  "mlp0": mlp_stage(0, C_M0, G_M0, 1),
                  "pool": (pool_sp, pool_act, pool_pe, pool_dve, pool_pool),
                  "mlp1": mlp_stage(1, C_M1, G_M1, 3),
                  "sbin": (sbin_sp, sbin_act, sbin_pe, sbin_dve, sbin_pool),
                  "sb": (None, sb_act, sb_pe, sb_dve, sb_pool),
                  "gin": (gin_sp, gin_act, gin_pe, gin_dve, gin_pool),
                  "gdn": (gdn_sp, gdn_act, gdn_pe, gdn_dve, gdn_pool),
                  "mg": (mg_sp, mg_act, mg_pe, mg_dve, mg_pool),
                  "end": (end_sp, end_act, end_pe, end_dve, end_pool)}
        block = ctx.enter_context(nc.Block())

        @block.sync
        def _(sp):
            for s in stages:
                if stages[s][0]:
                    stages[s][0](sp)

        @block.scalar
        def _(act):
            alink.eng = act
            for s in stages:
                if stages[s][1]:
                    stages[s][1](act)

        @block.tensor
        def _(pe):
            for s in stages:
                if stages[s][2]:
                    stages[s][2](pe)

        @block.vector
        def _(dve):
            dlink.eng = dve
            for s in stages:
                if stages[s][3]:
                    stages[s][3](dve)

        @block.gpsimd
        def _(pool):
            for s in stages:
                if stages[s][4]:
                    stages[s][4](pool)



def kernel(**inputs):
    import concourse.bacc as bacc
    from concourse.bass_utils import run_bass_kernel_spmd

    nc = bacc.Bacc("TRN2", target_bir_lowering=False, num_devices=1)
    tables = dict(zip(("const", "onehot", "same"), constants()))
    arrays, args = {}, {}
    for name, a in list(inputs.items()) + list(tables.items()):
        a = np.ascontiguousarray(a)
        arrays[f"in_{name}_dram"] = a
        args[name] = nc.dram_tensor(f"in_{name}_dram", a.shape, mybir.dt.from_np(a.dtype), kind="ExternalInput").ap()
    out = nc.dram_tensor("out_0_dram", (1, S, D), F32, kind="ExternalOutput").ap()
    build_program(nc, args, out)
    result = run_bass_kernel_spmd(nc, [arrays], core_ids=[0])
    return result.results[0]["out_0_dram"]
```
